# Optimizing a Trainium2 kernel written in Bass

```python
import jax, jax.numpy as jnp
from jax import lax
import numpy as np
import math

D_MODEL = 2048
BATCH = 1
SEQ = 256
DEPTH = 1

ATTN_WIDTH = D_MODEL // 2
HEAD_DIM_ATTN = 128
N_HEADS_ATTN = ATTN_WIDTH // HEAD_DIM_ATTN
DILATION_PATTERNS = ((128, 1), (512, 4), (2048, 16))
RET_WIDTH = D_MODEL // 2
N_HEADS_RET = 4
RET_V_DIM = RET_WIDTH // N_HEADS_RET
RET_QK_DIM = RET_V_DIM // 2
RET_CHUNK = 128
MIX_WIDTH = ATTN_WIDTH + RET_WIDTH
IN_SPLIT_SIZES = (ATTN_WIDTH, ATTN_WIDTH, ATTN_WIDTH, ATTN_WIDTH,
                  N_HEADS_RET * RET_QK_DIM, N_HEADS_RET * RET_QK_DIM, RET_WIDTH, RET_WIDTH)
IN_PROJ_WIDTH = sum(IN_SPLIT_SIZES)
IN_SPLIT_IDX = tuple(int(i) for i in np.cumsum(IN_SPLIT_SIZES)[:-1])
NORM_EPS = 1e-6
MASK_VALUE = -1e30


def rms_norm(x, g):
    xf = x.astype(jnp.float32)
    y = xf * lax.rsqrt(jnp.mean(xf * xf, axis=-1, keepdims=True) + NORM_EPS)
    return (y * g.astype(jnp.float32)).astype(x.dtype)

def alibi_slopes(n_heads):
    return jnp.exp2(-8.0 * (jnp.arange(n_heads, dtype=jnp.float32) + 1.0) / n_heads)

def dilated_window_attention(q, k, v, window, dilation, slopes):
    b, s, h, e = q.shape
    radius = window // (2 * dilation)
    blk = radius
    sub_len = s // dilation
    n_blk = -(-sub_len // blk)
    pad_len = n_blk * blk
    def to_sub(t):
        return t.reshape(b, sub_len, dilation, h, e)
    qs = jnp.pad(to_sub(q), ((0, 0), (0, pad_len - sub_len), (0, 0), (0, 0), (0, 0)))
    qb = qs.reshape(b, n_blk, blk, dilation, h, e)
    def key_windows(t):
        tp = jnp.pad(to_sub(t), ((0, 0), (blk, blk + pad_len - sub_len), (0, 0), (0, 0), (0, 0)))
        tb = tp.reshape(b, n_blk + 2, blk, dilation, h, e)
        return jnp.concatenate([tb[:, :-2], tb[:, 1:-1], tb[:, 2:]], axis=2)
    kw = key_windows(k)
    vw = key_windows(v)
    scores = jnp.einsum('bnirhe,bnjrhe->bnrhij', qb, kw).astype(jnp.float32)
    i_idx = jnp.arange(blk)[:, None]
    j_idx = jnp.arange(3 * blk)[None, :]
    rel = j_idx - blk - i_idx
    key_pos = jnp.arange(n_blk)[:, None] * blk + jnp.arange(3 * blk)[None, :] - blk
    valid = (key_pos >= 0) & (key_pos < sub_len)
    mask = (jnp.abs(rel) <= radius)[None] & valid[:, None, :]
    dist = (jnp.abs(rel) * dilation).astype(jnp.float32)
    bias = -slopes[:, None, None] * dist[None]
    scores = jnp.where(mask[None, :, None, None], scores + bias[None, None, None], MASK_VALUE)
    m = jnp.max(scores, axis=-1, keepdims=True)
    p = jnp.exp(scores - m)
    den = jnp.sum(p, axis=-1)
    o = jnp.einsum('bnrhij,bnjrhe->bnirhe', p, vw.astype(jnp.float32))
    o = o / den.transpose(0, 1, 4, 2, 3)[..., None]
    lse = (m[..., 0] + jnp.log(den)).transpose(0, 1, 4, 2, 3)
    o = o.reshape(b, pad_len, dilation, h, e)[:, :sub_len].reshape(b, s, h, e)
    lse = lse.reshape(b, pad_len, dilation, h)[:, :sub_len].reshape(b, s, h)
    return o, lse

def dilated_attention_mixture(q, k, v):
    slopes = alibi_slopes(q.shape[2])
    outs, lses = [], []
    for window, dilation in DILATION_PATTERNS:
        o, lse = dilated_window_attention(q, k, v, window, dilation, slopes)
        outs.append(o)
        lses.append(lse)
    w = jax.nn.softmax(jnp.stack(lses, axis=0), axis=0)
    o = jnp.sum(w[..., None] * jnp.stack(outs, axis=0), axis=0)
    return o.astype(v.dtype)

def retention_one_direction(q, k, v, log_gamma):
    b, s, h, dk = q.shape
    dv = v.shape[-1]
    c = RET_CHUNK
    n = s // c
    def chunk(t):
        return t.reshape(b, n, c, h, t.shape[-1]).transpose(1, 0, 3, 2, 4)
    qc, kc, vc = chunk(q), chunk(k), chunk(v)
    idx = jnp.arange(c, dtype=jnp.float32)
    rel = idx[:, None] - idx[None, :]
    lg = log_gamma[:, None, None]
    decay = jnp.where(rel[None] >= 0, jnp.exp(jnp.maximum(rel, 0.0)[None] * lg), 0.0).astype(q.dtype)
    xi = jnp.exp((idx[None] + 1.0) * log_gamma[:, None]).astype(q.dtype)[..., None]
    zeta = jnp.exp((c - 1.0 - idx[None]) * log_gamma[:, None]).astype(q.dtype)[..., None]
    g_chunk = jnp.exp(c * log_gamma).astype(q.dtype)[:, None, None]

    def step(state, inp):
        qi, ki, vi = inp
        inner = jnp.einsum('bhid,bhjd->bhij', qi, ki) * decay
        o = jnp.einsum('bhij,bhje->bhie', inner, vi) + jnp.einsum('bhid,bhde->bhie', qi, state) * xi
        state = state * g_chunk + jnp.einsum('bhjd,bhje->bhde', ki * zeta, vi)
        return state, o

    state0 = jnp.zeros((b, h, dk, dv), dtype=q.dtype)
    _, oc = lax.scan(step, state0, (qc, kc, vc))
    return oc.transpose(1, 0, 3, 2, 4).reshape(b, s, h, dv)

def bidirectional_retention(q, k, v, decay_logit_f, decay_logit_b):
    lg_f = jax.nn.log_sigmoid(decay_logit_f.astype(jnp.float32))
    lg_b = jax.nn.log_sigmoid(decay_logit_b.astype(jnp.float32))
    o_f = retention_one_direction(q, k, v, lg_f)
    o_b = jnp.flip(retention_one_direction(jnp.flip(q, 1), jnp.flip(k, 1), jnp.flip(v, 1), lg_b), 1)
    o = (o_f + o_b).astype(jnp.float32)
    o = o * lax.rsqrt(jnp.mean(o * o, axis=-1, keepdims=True) + NORM_EPS)
    return o.astype(v.dtype)

def hybrid_layer(x, c_act, g, w_ada, b_ada, w_in, w_out, dec_f, dec_b):
    b, s, _ = x.shape
    mod = c_act @ w_ada + b_ada
    shift, scale, gate = jnp.split(mod, 3, axis=-1)
    h = rms_norm(x, g) * (1.0 + scale[:, None]) + shift[:, None]
    proj = jnp.einsum('bsd,df->bsf', h, w_in)
    q_a, k_a, v_a, z_a, q_r, k_r, v_r, z_r = jnp.split(proj, IN_SPLIT_IDX, axis=-1)
    q_a = q_a.reshape(b, s, N_HEADS_ATTN, HEAD_DIM_ATTN) * (HEAD_DIM_ATTN ** -0.5)
    k_a = k_a.reshape(b, s, N_HEADS_ATTN, HEAD_DIM_ATTN)
    v_a = v_a.reshape(b, s, N_HEADS_ATTN, HEAD_DIM_ATTN)
    y_a = dilated_attention_mixture(q_a, k_a, v_a).reshape(b, s, ATTN_WIDTH)
    q_r = q_r.reshape(b, s, N_HEADS_RET, RET_QK_DIM)
    k_r = k_r.reshape(b, s, N_HEADS_RET, RET_QK_DIM) * (RET_QK_DIM ** -0.5)
    v_r = v_r.reshape(b, s, N_HEADS_RET, RET_V_DIM)
    y_r = bidirectional_retention(q_r, k_r, v_r, dec_f, dec_b).reshape(b, s, RET_WIDTH)
    y = jnp.concatenate([y_a * jax.nn.silu(z_a), y_r * jax.nn.silu(z_r)], axis=-1)
    out = jnp.einsum('bsf,fd->bsd', y, w_out)
    return x + gate[:, None] * out

def first_inputs(seed: int = 0) -> dict:
    key = jax.random.key(seed)
    ks = jax.random.split(key, 10)
    f32 = jnp.float32
    x = jax.random.normal(ks[0], (BATCH, SEQ, D_MODEL), f32)
    c = jax.random.normal(ks[1], (BATCH, D_MODEL), f32)
    norm_gain = 1.0 + 0.02 * jax.random.normal(ks[2], (DEPTH, D_MODEL), f32)
    w_ada = 0.5 * D_MODEL ** -0.5 * jax.random.normal(ks[3], (DEPTH, D_MODEL, 3 * D_MODEL), f32)
    b_ada = 0.02 * jax.random.normal(ks[4], (DEPTH, 3 * D_MODEL), f32)
    w_in = D_MODEL ** -0.5 * jax.random.normal(ks[5], (DEPTH, D_MODEL, IN_PROJ_WIDTH), f32)
    w_out = MIX_WIDTH ** -0.5 * jax.random.normal(ks[6], (DEPTH, MIX_WIDTH, D_MODEL), f32)
    gamma = 1.0 - jnp.exp2(-5.0 - jnp.arange(N_HEADS_RET, dtype=f32))
    base_logit = jnp.log(gamma) - jnp.log1p(-gamma)
    ret_decay_logit_f = base_logit[None] + 0.1 * jax.random.normal(ks[7], (DEPTH, N_HEADS_RET), f32)
    ret_decay_logit_b = base_logit[None] + 0.1 * jax.random.normal(ks[8], (DEPTH, N_HEADS_RET), f32)
    final_gain = 1.0 + 0.02 * jax.random.normal(ks[9], (D_MODEL,), f32)
    return {"x": x, "c": c, "norm_gain": norm_gain, "w_ada": w_ada, "b_ada": b_ada,
            "w_in": w_in, "w_out": w_out, "ret_decay_logit_f": ret_decay_logit_f,
            "ret_decay_logit_b": ret_decay_logit_b, "final_gain": final_gain}

def first_block(x, c, norm_gain, w_ada, b_ada, w_in, w_out, ret_decay_logit_f, ret_decay_logit_b, final_gain):
    c_act = jax.nn.silu(c)
    h = x
    for layer in range(DEPTH):
        h = hybrid_layer(h, c_act, norm_gain[layer], w_ada[layer], b_ada[layer], w_in[layer],
                         w_out[layer], ret_decay_logit_f[layer], ret_decay_logit_b[layer])
    return rms_norm(h, final_gain)


DEPTH_2 = 2

N_A = DEPTH_2 // 2
N_B = DEPTH_2 - N_A
A_QK_DIM = 128
A_V_DIM = 2 * A_QK_DIM
A_HEADS = D_MODEL // A_V_DIM
A_WIDTH = A_HEADS * A_V_DIM
B_HEAD_DIM = 128
B_HEADS = D_MODEL // B_HEAD_DIM
B_WIDTH = B_HEADS * B_HEAD_DIM
BLOCK = 128
NEG = -1e30
EPS = 1e-5
DN_ALPHA = (2.0 * DEPTH_2) ** 0.25
DN_BETA = (8.0 * DEPTH_2) ** -0.25


def layer_norm(x, g, b):
    xf = x.astype(jnp.float32)
    mu = jnp.mean(xf, axis=-1, keepdims=True)
    var = jnp.mean(jnp.square(xf - mu), axis=-1, keepdims=True)
    y = (xf - mu) * lax.rsqrt(var + EPS)
    return (y * g.astype(jnp.float32) + b.astype(jnp.float32)).astype(x.dtype)

def rms_norm_2(x, g):
    xf = x.astype(jnp.float32)
    y = xf * lax.rsqrt(jnp.mean(jnp.square(xf), axis=-1, keepdims=True) + EPS)
    return (y * g.astype(jnp.float32)).astype(x.dtype)

def to_blocks(a):
    b, s = a.shape[:2]
    a = a.reshape((b, s // BLOCK, BLOCK) + a.shape[2:])
    return jnp.moveaxis(a, 1, 0)

def from_blocks(a):
    a = jnp.moveaxis(a, 0, 1)
    return a.reshape((a.shape[0], a.shape[1] * a.shape[2]) + a.shape[3:])

def alibi_slopes_2(n_heads):
    return jnp.asarray([2.0 ** (-8.0 * (h + 1) / n_heads) for h in range(n_heads)], dtype=jnp.float32)

def diff_attention(h, w_in, w_out, lq1, lk1, lq2, lk2, subln_g, layer_idx):
    B, S, _ = h.shape
    proj = h @ w_in
    q, k, v, g = jnp.split(proj, 4, axis=-1)
    q = q.reshape(B, S, A_HEADS, 2, A_QK_DIM) * (A_QK_DIM ** -0.5)
    k = k.reshape(B, S, A_HEADS, 2, A_QK_DIM)
    v = v.reshape(B, S, A_HEADS, A_V_DIM)
    lam_init = 0.8 - 0.6 * math.exp(-0.3 * layer_idx)
    f32 = jnp.float32
    lam = (jnp.exp(jnp.sum(lq1.astype(f32) * lk1.astype(f32)))
           - jnp.exp(jnp.sum(lq2.astype(f32) * lk2.astype(f32))) + lam_init)
    slopes = alibi_slopes_2(A_HEADS)
    s_pos = jnp.arange(S)

    def block(args):
        qb, i = args
        t_pos = i * BLOCK + jnp.arange(BLOCK)
        dist = (t_pos[:, None] - s_pos[None, :]).astype(f32)
        bias = -slopes[:, None, None] * dist
        sc = jnp.einsum('bqhcd,bkhcd->bhcqk', qb, k).astype(f32) + bias[None, :, None]
        sc = jnp.where(dist >= 0, sc, NEG)
        p = jax.nn.softmax(sc, axis=-1)
        a = p[:, :, 0] - lam * p[:, :, 1]
        return jnp.einsum('bhqk,bkhe->bqhe', a.astype(v.dtype), v)

    o = from_blocks(lax.map(block, (to_blocks(q), jnp.arange(S // BLOCK))))
    o = rms_norm_2(o, subln_g) * (1.0 - lam_init)
    o = o.reshape(B, S, A_WIDTH) * jax.nn.silu(g)
    return o @ w_out

def shared_kv(x, c_act, w_mod_kv, b_mod_kv, w_kv, b_f):
    B, S, _ = x.shape
    mod = c_act @ w_mod_kv + b_mod_kv
    shift, scale = jnp.split(mod, 2, axis=-1)
    hk = x * (1.0 + scale[:, None]) + shift[:, None]
    kvf = hk @ w_kv
    k, v, zf = jnp.split(kvf, [B_WIDTH, 2 * B_WIDTH], axis=-1)
    k = k.reshape(B, S, B_HEADS, B_HEAD_DIM)
    v = v.reshape(B, S, B_HEADS, B_HEAD_DIM)
    log_f = jax.nn.log_sigmoid(zf.astype(jnp.float32) + b_f.astype(jnp.float32))
    F = jnp.cumsum(log_f, axis=1)
    return k, v, F

def forgetting_attention(h, w_q, w_out, k, v, F):
    B, S, _ = h.shape
    f32 = jnp.float32
    proj = h @ w_q
    q, g = jnp.split(proj, 2, axis=-1)
    q = q.reshape(B, S, B_HEADS, B_HEAD_DIM) * (B_HEAD_DIM ** -0.5)
    Fk = jnp.moveaxis(F, 1, 2)
    s_pos = jnp.arange(S)

    def block(args):
        qb, Fq, i = args
        t_pos = i * BLOCK + jnp.arange(BLOCK)
        causal = t_pos[:, None] >= s_pos[None, :]
        decay = jnp.moveaxis(Fq, 1, 2)[..., None] - Fk[:, :, None, :]
        sc = jnp.einsum('bqhd,bkhd->bhqk', qb, k).astype(f32) + decay
        sc = jnp.where(causal, sc, NEG)
        p = jax.nn.softmax(sc, axis=-1)
        return jnp.einsum('bhqk,bkhd->bqhd', p.astype(v.dtype), v)

    o = from_blocks(lax.map(block, (to_blocks(q), to_blocks(F), jnp.arange(S // BLOCK))))
    o = o.reshape(B, S, B_WIDTH) * jax.nn.silu(g)
    return o @ w_out

def second_inputs(seed: int = 0) -> dict:
    key = jax.random.key(seed)
    ks = jax.random.split(key, 20)
    nrm = jax.random.normal
    D = D_MODEL
    x = nrm(ks[0], (BATCH, SEQ, D), jnp.float32)
    c = nrm(ks[1], (BATCH, D), jnp.float32)
    w_mod = nrm(ks[2], (DEPTH_2, D, 3 * D), jnp.float32) * D ** -0.5
    b_mod = nrm(ks[3], (DEPTH_2, 3 * D), jnp.float32) * 0.02
    ln_g = 1.0 + 0.02 * nrm(ks[4], (DEPTH_2, D), jnp.float32)
    ln_b = 0.02 * nrm(ks[5], (DEPTH_2, D), jnp.float32)
    a_w_in = nrm(ks[6], (N_A, D, 4 * A_WIDTH), jnp.float32) * D ** -0.5
    a_w_out = nrm(ks[7], (N_A, A_WIDTH, D), jnp.float32) * (A_WIDTH ** -0.5 * DN_BETA)
    a_lam_q1 = 0.1 * nrm(ks[8], (N_A, A_QK_DIM), jnp.float32)
    a_lam_k1 = 0.1 * nrm(ks[9], (N_A, A_QK_DIM), jnp.float32)
    a_lam_q2 = 0.1 * nrm(ks[10], (N_A, A_QK_DIM), jnp.float32)
    a_lam_k2 = 0.1 * nrm(ks[11], (N_A, A_QK_DIM), jnp.float32)
    a_subln_g = 1.0 + 0.02 * nrm(ks[12], (N_A, A_V_DIM), jnp.float32)
    kv_w_mod = nrm(ks[13], (D, 2 * D), jnp.float32) * D ** -0.5
    kv_b_mod = nrm(ks[14], (2 * D,), jnp.float32) * 0.02
    kv_w = nrm(ks[15], (D, 2 * B_WIDTH + B_HEADS), jnp.float32) * D ** -0.5
    kv_b_f = jax.random.uniform(ks[16], (B_HEADS,), jnp.float32, minval=1.0, maxval=6.0)
    b_w_in = nrm(ks[17], (N_B, D, 2 * B_WIDTH), jnp.float32) * D ** -0.5
    b_w_out = nrm(ks[18], (N_B, B_WIDTH, D), jnp.float32) * (B_WIDTH ** -0.5 * DN_BETA)
    return {"x": x, "c": c, "w_mod": w_mod, "b_mod": b_mod, "ln_g": ln_g, "ln_b": ln_b,
            "a_w_in": a_w_in, "a_w_out": a_w_out, "a_lam_q1": a_lam_q1, "a_lam_k1": a_lam_k1,
            "a_lam_q2": a_lam_q2, "a_lam_k2": a_lam_k2, "a_subln_g": a_subln_g,
            "kv_w_mod": kv_w_mod, "kv_b_mod": kv_b_mod, "kv_w": kv_w, "kv_b_f": kv_b_f,
            "b_w_in": b_w_in, "b_w_out": b_w_out}

def second_block(x, c, w_mod, b_mod, ln_g, ln_b, a_w_in, a_w_out, a_lam_q1, a_lam_k1,
              a_lam_q2, a_lam_k2, a_subln_g, kv_w_mod, kv_b_mod, kv_w, kv_b_f,
              b_w_in, b_w_out):
    c_act = jax.nn.silu(c)
    kv = None
    for l in range(DEPTH_2):
        mod = c_act @ w_mod[l] + b_mod[l]
        shift, scale, gate = jnp.split(mod, 3, axis=-1)
        h = x * (1.0 + scale[:, None]) + shift[:, None]
        if l < N_A:
            y = diff_attention(h, a_w_in[l], a_w_out[l], a_lam_q1[l], a_lam_k1[l],
                               a_lam_q2[l], a_lam_k2[l], a_subln_g[l], l)
        else:
            if kv is None:
                kv = shared_kv(x, c_act, kv_w_mod, kv_b_mod, kv_w, kv_b_f)
            k_sh, v_sh, F_sh = kv
            y = forgetting_attention(h, b_w_in[l - N_A], b_w_out[l - N_A], k_sh, v_sh, F_sh)
        x = layer_norm(DN_ALPHA * x + gate[:, None] * y, ln_g[l], ln_b[l])
    return x


def setup_inputs(seed=0):
    out = dict(first_inputs(seed))
    for name, value in second_inputs(seed + 1).items():
        if name != "x":
            out[name + "_2"] = value
    return out


def reference(
    x, c, norm_gain, w_ada, b_ada, w_in, w_out, ret_decay_logit_f, ret_decay_logit_b,
    final_gain, c_2, w_mod_2, b_mod_2, ln_g_2, ln_b_2, a_w_in_2, a_w_out_2, a_lam_q1_2,
    a_lam_k1_2, a_lam_q2_2, a_lam_k2_2, a_subln_g_2, kv_w_mod_2, kv_b_mod_2, kv_w_2, kv_b_f_2,
    b_w_in_2, b_w_out_2,
):
    x = first_block(
        x, c, norm_gain, w_ada, b_ada, w_in, w_out, ret_decay_logit_f, ret_decay_logit_b,
        final_gain,
    )
    return second_block(
        x, c_2, w_mod_2, b_mod_2, ln_g_2, ln_b_2, a_w_in_2, a_w_out_2, a_lam_q1_2, a_lam_k1_2,
        a_lam_q2_2, a_lam_k2_2, a_subln_g_2, kv_w_mod_2, kv_b_mod_2, kv_w_2, kv_b_f_2, b_w_in_2,
        b_w_out_2,
    )


_drawn_inputs = setup_inputs


def setup_inputs(seed=0):
    import zlib

    import numpy as np

    out = dict(_drawn_inputs(seed))
    spreads = {}
    factors = {'norm_gain': 8.0,
     'b_ada': 3.62,
     'final_gain': 2.694,
     'b_mod_2': 5.839,
     'a_lam_k2_2': 8.0,
     'a_subln_g_2': 8.0,
     'kv_b_mod_2': 8.0}
    for name, (base, spread) in spreads.items():
        noise = np.random.default_rng([zlib.crc32(name.encode()), seed]).standard_normal(out[name].shape)
        drawn = base * np.exp(spread * noise) if base else spread * noise
        out[name] = __import__('jax').numpy.asarray(drawn.astype(out[name].dtype))
    for name, factor in factors.items():
        out[name] = (out[name] * factor).astype(out[name].dtype)
    return out
```

```python
import math
from contextlib import ExitStack

import numpy as np

import concourse.bass as bass
from concourse import mybir

F32 = mybir.dt.float32
F32R = mybir.dt.float32r
ALU = mybir.AluOpType
ACT = mybir.ActivationFunctionType

P = 128
D = 2048
SEQ = 256
TT = SEQ // P
KT = D // P
CHUNK = 512
SLOT_KT = 4
SLOTS = KT // SLOT_KT
HALF_KT = 2
HALVES = KT // HALF_KT
GEMV_RING = 2
TURN_BANKS = 4
TURNS = KT // 2

DIL_HEADS = 8
RET_HEADS = 4
DIFF_HEADS = 8
FOX_HEADS = 16
HEAD = 128
WIDE = 256
QK_SCALE = HEAD ** -0.5
DILATIONS = ((128, 1), (512, 4), (2048, 16))
NEG = -1e30
FLT_MAX = 3e38
NORM_EPS = 1e-6
EPS = 1e-5
LAM_INIT = 0.8 - 0.6 * math.exp(-0.3 * 0)
DN_ALPHA = (2.0 * 2) ** 0.25

(ADA_SHIFT, ADA_SCALE, ADA_GATE, A_SHIFT, A_SCALE, A_GATE, KV_SHIFT, KV_SCALE, B_SHIFT, B_SCALE,
 B_GATE) = range(11)
MODS = 11
MOD_AT_PAIR = {0: ADA_GATE, 2: A_SHIFT, 5: A_SCALE, 7: A_GATE, 9: KV_SHIFT, 11: KV_SCALE, 13: B_SHIFT,
               17: B_SCALE, 19: B_GATE}
PAIRS = 29

VEC_C, VEC_GAIN, VEC_BIAS = 0, 2 * KT, 3 * KT
VECS = VEC_BIAS + MODS * KT


def alibi(n):
    return [2.0 ** (-8.0 * (h + 1) / n) for h in range(n)]


def shape_tables():
    t = np.arange(SEQ)
    rel = t[:, None] - t[None, :]
    dist = np.abs(rel).astype(np.float64)
    seen = np.zeros((SEQ, SEQ))
    for window, dilation in DILATIONS:
        seen += (rel % dilation == 0) & (dist <= (window // (2 * dilation)) * dilation)
    log_seen = np.where(seen > 0, np.log(np.maximum(seen, 1)), NEG)

    def by_tile(a):
        return a.reshape(TT, P, SEQ).transpose(1, 0, 2)

    def causal_blocks(a):
        b = by_tile(a)
        return np.concatenate([b[:, 0, :P], b[:, 1, :]], axis=1)

    dil = np.stack([by_tile(np.where(seen > 0, -s * dist + log_seen, NEG)).reshape(P, -1)
                    for s in alibi(DIL_HEADS)])
    diff = np.stack([causal_blocks(np.where(rel >= 0, -s * dist, NEG)) for s in alibi(DIFF_HEADS)])
    causal = causal_blocks(np.where(rel >= 0, 0.0, NEG))
    q_minus_k = t[None, :] - t[:, None]
    fwd = by_tile(np.where(q_minus_k >= 0, q_minus_k, 1e30)).reshape(P, -1)
    bwd = by_tile(np.where(q_minus_k <= 0, -q_minus_k, 1e30)).reshape(P, -1)
    p = np.arange(P)
    neg_upto = -(p[:, None] <= t[None, :]).astype(np.float64)
    out = {"t_ident": np.eye(P), "t_dil": dil, "t_diff": diff, "t_causal": causal, "t_fwd": fwd,
           "t_bwd": bwd, "t_neg_upto": neg_upto}
    return {k: np.ascontiguousarray(v, dtype=np.float32) for k, v in out.items()}


def t_uses():
    uses = [("vec",), ("mod", ADA_SHIFT), ("mod", ADA_SCALE)]

    def attention(layer, units, softmax_heads_of):
        for s in range(units + 3):
            if s < units:
                uses.append(("qk", layer, s))
            if 0 <= s - 2 < units and softmax_heads_of(s - 2):
                uses.append(("probs", layer, s - 2))

    def gate(layer):
        uses.extend(("gate", layer, n) for n in range(D // CHUNK))

    for pair in range(PAIRS):
        if pair == 5:
            attention(0, DIL_HEADS + RET_HEADS, lambda u: u < DIL_HEADS)
        if pair == 7:
            gate(0)
        if pair == 15:
            attention(1, 2 * DIFF_HEADS, lambda u: u % 2 == 1)
        if pair == 17:
            gate(1)
        if pair == 23:
            uses.append(("forget",))
        if pair == 25:
            attention(2, FOX_HEADS, lambda u: True)
        if pair == 27:
            gate(2)
        if pair - 1 in MOD_AT_PAIR:
            uses.append(("mod", MOD_AT_PAIR[pair - 1]))
    return {u: n for n, u in enumerate(uses)}


def two_blocks(nc, a, out):
    T = t_uses()
    UNITS = [DIL_HEADS + RET_HEADS, 2 * DIFF_HEADS, FOX_HEADS]
    UNIT0 = [0, UNITS[0], UNITS[0] + UNITS[1]]
    SOFT = [DIL_HEADS, UNITS[1], UNITS[2]]
    SOFT0 = [0, SOFT[0], SOFT[0] + SOFT[1]]
    OUTS = [UNITS[0], DIFF_HEADS, FOX_HEADS]
    OUT0 = [0, OUTS[0], OUTS[0] + OUTS[1]]

    def out_of(layer, u):
        if layer == 1:
            return u // 2 if u % 2 else None
        return u

    def is_ret(layer, u):
        return layer == 0 and u >= DIL_HEADS

    def is_normed(layer, u):
        return is_ret(layer, u) or (layer == 1 and u % 2 == 1)

    ROOTS = [("x",)]
    for layer in range(3):
        ROOTS += [("head", layer, u) for u in range(UNITS[layer]) if is_normed(layer, u)]
        ROOTS.append(("norm", layer))
    ROOTS = {key: n for n, key in enumerate(ROOTS)}

    with ExitStack() as ctx:
        def sb(name, shape, dt=F32):
            return ctx.enter_context(nc.sbuf_tensor(name, shape, dt))

        def psum(name, shape):
            return ctx.enter_context(nc.psum_tensor(name, shape, F32))

        def sem(name):
            return ctx.enter_context(nc.semaphore(name))

        resid = sb("resid", [P, TT, D])
        act_hi = sb("act_hi", [P, KT, SEQ], F32R)
        act_lo = sb("act_lo", [P, KT, SEQ], F32R)
        area = sb("area", [P, 3, TT, D])
        Q, K, V = 0, 1, 2
        raw = sb("raw", [P, SLOTS, SLOT_KT, CHUNK])
        w_hi = sb("w_hi", [P, 2, HALF_KT, CHUNK], F32R)
        w_lo = sb("w_lo", [P, 2, HALF_KT, CHUNK], F32R)
        gw = sb("gw", [P, GEMV_RING, D])
        acc = sb("acc", [P, D])
        vec_rows = sb("vec_rows", [P, 2, P])
        vecs = sb("vecs", [P, VECS])
        c_act = sb("c_act", [P, 2 * KT])
        mod = sb("mod", [P, MODS, KT])
        scales = sb("scales", [P, 4, KT])
        qk_t = sb("qk_t", [P, 2, 4 * P])
        probs = sb("probs", [P, 4 * 384])
        probs_t = sb("probs_t", [P, 2, 4 * P])
        bias = sb("bias", [P, 2, TT * SEQ])
        neg_max = sb("neg_max", [P, 4, TT])
        den = sb("den", [P, 4, TT])
        rden = sb("rden", [P, 4, TT])
        stats = sb("stats", [P, TT, 4, 6])
        moments = sb("moments", [P, TT, 2])
        mean_sq = sb("mean_sq", [P, TT])
        rstd = sb("rstd", [P, TT])
        root = sb("root", [P, TT])
        log_sq = sb("log_sq", [P, TT])
        forget = sb("forget", [P, TT * FOX_HEADS])
        w_forget = sb("w_forget", [P, KT, FOX_HEADS])
        ident = sb("ident", [P, P])
        ones = sb("ones", [P, 1])
        neg_upto = sb("neg_upto", [P, SEQ])
        subln = sb("subln", [P, WIDE])
        b_forget = sb("b_forget", [P, FOX_HEADS])
        decay = sb("decay", [P, 2 * RET_HEADS])
        ls = sb("ls", [P, 7, TT * FOX_HEADS])
        lam = sb("lam", [P, 8])
        side = sb("side", [P, 2, CHUNK])

        banks = [psum(f"bank{i}", [P, CHUNK]) for i in range(8)]
        acc_banks, t_bank, s_banks, o_bank = banks[0:4], banks[4], banks[5:7], banks[7]

        vecs_landed = sem("vecs_landed")
        smalls_landed = sem("smalls_landed")
        x_landed = sem("x_landed")
        raw_landed = [sem(f"raw_landed{i}") for i in range(SLOTS)]
        gw_landed = [sem(f"gw_landed{i}") for i in range(GEMV_RING)]
        rows_landed = sem("rows_landed")
        bias_landed = [sem(f"bias_landed{i}") for i in range(2)]
        stored = sem("stored")
        hi_ready = sem("hi_ready")
        lo_ready = sem("lo_ready")
        half_used = sem("half_used")
        evacuated = sem("evacuated")
        gated = sem("gated")
        summed = sem("summed")
        measured = sem("measured")
        gemv_used = sem("gemv_used")
        t_ready = sem("t_ready")
        t_free = sem("t_free")
        turned = sem("turned")
        turned_hi = sem("turned_hi")
        turned_lo = sem("turned_lo")
        shifted = sem("shifted")
        scored = sem("scored")
        maxed = sem("maxed")
        exped = sem("exped")
        mixed = sem("mixed")
        weighed = sem("weighed")
        finished = sem("finished")
        dve_chain = sem("dve_chain")
        consts_ready = sem("consts_ready")
        silu_ready = sem("silu_ready")
        xhat_scale = sem("xhat_scale")
        xhat_ready = sem("xhat_ready")
        scales_ready = sem("scales_ready")
        sigmoid_to_act = sem("sigmoid_to_act")
        sigmoid_to_dve = sem("sigmoid_to_dve")
        lam_products = sem("lam_products")
        lam_exped = sem("lam_exped")
        decay_ready = sem("decay_ready")
        decay_exped = sem("decay_exped")
        decay_used = sem("decay_used")
        forget_ready = sem("forget_ready")
        normed = sem("normed")
        var_ready = sem("var_ready")
        root_ready = sem("root_ready")

        def wait(eng, s, value):
            if isinstance(value, int) and value <= 0:
                return
            eng.wait_ge(s, value)

        def decay_table(h):
            return area[:, K, h // 2, 1024 + (h % 2) * 512:1024 + (h % 2) * 512 + 512]

        def q_cols(layer, u):
            if is_ret(layer, u):
                return 1024 + (u - DIL_HEADS) * WIDE
            return u * HEAD

        def k_src(layer, u, tt):
            if is_ret(layer, u):
                c = q_cols(layer, u) + HEAD
                return area[:, Q, tt, c:c + HEAD]
            return area[:, K, tt, u * HEAD:(u + 1) * HEAD]

        def head_cols(layer, u):
            if is_ret(layer, u):
                return 1024 + (u - DIL_HEADS) * WIDE, WIDE
            if layer == 1:
                return (u // 2) * WIDE, WIDE
            return u * HEAD, HEAD

        def prob_slot(layer, u):
            w = 384 if layer else 512
            s = u % 4 if layer else u % 2
            return probs[:, s * w:(s + 1) * w]

        def blocks(layer):
            return ((0, 256), (256, 512)) if layer == 0 else ((0, 128), (128, 384))

        def row_of(v):
            return v.rearrange("(a n) -> a n", a=1).broadcast_to([P, v.shape[0]])

        def by_depth(w):
            return w.rearrange("(k p) n -> p k n", p=P)

        w_in, w_out = by_depth(a["w_in"][0]), by_depth(a["w_out"][0])
        wa_in, wa_out = by_depth(a["a_w_in_2"][0]), by_depth(a["a_w_out_2"][0])
        w_kv, wb_in = by_depth(a["kv_w_2"]), by_depth(a["b_w_in_2"][0])
        wb_out = by_depth(a["b_w_out_2"][0])
        RUNS = [(w_in, 0, 6), (w_in, 4096, 4), (w_in, 3072, 2), (w_in, 6144, 2), (w_out, 0, 4),
                (wa_in, 0, 16), (wa_out, 0, 4), (w_kv, 0, 8), (wb_in, 0, 8), (wb_out, 0, 4)]
        MOD_SRC = ([(a["w_ada"][0], D * i) for i in range(3)] + [(a["w_mod_2"][0], D * i) for i in range(3)]
                   + [(a["kv_w_mod_2"], D * i) for i in range(2)]
                   + [(a["w_mod_2"][1], D * i) for i in range(3)])

        block = ctx.enter_context(nc.Block())

        @block.sync
        def _(sp):
            sp.dma_start(resid[:], a["x"][0].rearrange("(t p) d -> p t d", p=P)).then_inc(x_landed, 16)

            def load_chunk(src, col, after):
                for s in range(SLOTS):
                    wait(sp, lo_ready, after + 2 * s)
                    sp.dma_start(raw[:, s], src[:, s * SLOT_KT:(s + 1) * SLOT_KT, bass.ds(col, CHUNK)]
                                 ).then_inc(raw_landed[s], 16)

            first = 0
            for n, (src, col, chunks) in enumerate(RUNS):
                start = 0
                if n == 0:
                    load_chunk(src, col, -HALVES)
                    start = 1
                with sp.Fori(0, chunks - start) as i:
                    load_chunk(src, i * CHUNK + (col + start * CHUNK),
                               i * HALVES + (HALVES * (first + start - 1) + 2))
                first += chunks
            for tt in range(TT):
                sp.wait_ge(normed, 3 * TT - TT + tt + 1)
                sp.dma_start(out[0, tt * P:(tt + 1) * P, :], resid[:, tt]).then_inc(stored, 16)
            sp.wait_ge(stored, 16 * TT)

        @block.gpsimd
        def _(pool):
            def load(src, row, col, slot, after):
                wait(pool, gemv_used, after)
                pool.dma_start(gw[:, slot], src[bass.ds(row, P), col:col + D]).then_inc(gw_landed[slot], 16)

            for b, (src, col) in enumerate(MOD_SRC):
                start = 0
                if b == 0:
                    for slot in range(GEMV_RING):
                        load(src, slot * P, col, slot, 0)
                    start = 1
                with pool.Fori(0, KT // GEMV_RING - start) as i:
                    for slot in range(GEMV_RING):
                        load(src, i * (GEMV_RING * P) + (start * GEMV_RING + slot) * P, col, slot,
                             i * GEMV_RING + (b * KT + start * GEMV_RING + slot - GEMV_RING + 1))

        @block.tensor
        def _(pe):
            def turn_vectors():
                pe.wait_ge(vecs_landed, 16 * 8)
                nc.tensor.transpose(t_bank[:, 0:96], vec_rows[0:96, 0, :], ident[0:96, 0:96])
                nc.tensor.transpose(t_bank[:, 96:VECS], vec_rows[:, 1, :], ident[:]).then_inc(t_ready, 1)

            def sum_mod(b):
                pe.wait_ge(gemv_used, KT * (b + 1))
                pe.wait_ge(t_free, T[("mod", b)])
                pe.wait_ge(consts_ready, 1)
                for k in range(KT):
                    last = nc.tensor.matmul(t_bank[:, k:k + 1], acc[:, k * P:(k + 1) * P], ones[:],
                                            start=True, stop=True)
                last.then_inc(t_ready, 1)

            def spread_gate(layer, b):
                for n in range(D // CHUNK):
                    pe.wait_ge(t_free, T[("gate", layer, n)])
                    for k in range(4):
                        g = mod[:, b, 4 * n + k:4 * n + k + 1].broadcast_to([P, P])
                        last = nc.tensor.matmul(t_bank[:, k * P:(k + 1) * P], g, ident[:], start=True, stop=True)
                    last.then_inc(t_ready, 1)

            def turn(m, src, t_used):
                pe.wait_ge(t_free, t_used)
                for r in range(TURNS):
                    wait(pe, turned_lo, TURNS * m + r - TURN_BANKS + 1 if r >= TURN_BANKS else TURNS * m)
                    bank = banks[4 + r % TURN_BANKS]
                    for k in range(2):
                        for tt in range(TT):
                            kt = 2 * r + k
                            last = nc.tensor.transpose(bank[:, k * SEQ + tt * P:k * SEQ + (tt + 1) * P],
                                                       src[:, tt, kt * P:(kt + 1) * P], ident[:])
                    last.then_inc(turned, 1)

            def pair(i, p0):
                for c in range(2):
                    wait(pe, evacuated, i * 4 + (4 * p0 + 2 * c - 2))
                    for j in range(HALVES):
                        b = j % 2
                        pe.wait_ge(lo_ready, i * 16 + (16 * p0 + HALVES * c + j + 1))
                        for k in range(HALF_KT):
                            kt = HALF_KT * j + k
                            for tt in range(TT):
                                dst = acc_banks[2 * c + tt][:]
                                hi = act_hi[:, kt, tt * P:(tt + 1) * P]
                                lo = act_lo[:, kt, tt * P:(tt + 1) * P]
                                nc.tensor.matmul(dst, hi, w_hi[:, b, k], start=(kt == 0), stop=False)
                                nc.tensor.matmul(dst, hi, w_lo[:, b, k], start=False, stop=False)
                                last = nc.tensor.matmul(dst, lo, w_hi[:, b, k], start=False, stop=(kt == KT - 1))
                        last.then_inc(half_used, 1)

            def pairs(p0, n):
                with pe.Fori(0, n) as i:
                    pair(i, p0)

            def await_turned(m):
                pe.wait_ge(turned_hi, TURNS * (m + 1))
                pe.wait_ge(turned_lo, TURNS * (m + 1))

            def attention(layer, pairs_done):
                units, u0, o0 = UNITS[layer], UNIT0[layer], OUT0[layer]
                pe.wait_ge(evacuated, 4 * pairs_done)
                for s in range(units + 3):
                    if s < units:
                        u = s
                        n = T[("qk", layer, u)]
                        pe.wait_ge(t_free, n)
                        c = q_cols(layer, u)
                        for tt in range(TT):
                            nc.tensor.transpose(t_bank[:, tt * P:(tt + 1) * P], area[:, Q, tt, c:c + HEAD], ident[:])
                        for tt in range(TT):
                            last = nc.tensor.transpose(t_bank[:, SEQ + tt * P:SEQ + (tt + 1) * P],
                                                       k_src(layer, u, tt), ident[:])
                        last.then_inc(t_ready, 1)
                    if 0 <= s - 1 < units:
                        u = s - 1
                        pe.wait_ge(t_free, T[("qk", layer, u)] + 1)
                        wait(pe, maxed, 2 * (u0 + u - 1) if u >= 2 else 2 * u0)
                        q, k = qk_t[:, u % 2, 0:SEQ], qk_t[:, u % 2, SEQ:2 * SEQ]
                        s_bank = s_banks[u % 2]
                        if is_ret(layer, u):
                            for j in range(TT):
                                last = nc.tensor.matmul(s_bank[:, j * SEQ:(j + 1) * SEQ], k[:, j * P:(j + 1) * P], q,
                                                        start=True, stop=True)
                        else:
                            for tt, (c0, c1) in enumerate(blocks(layer)):
                                last = nc.tensor.matmul(s_bank[:, c0:c1], q[:, tt * P:(tt + 1) * P], k[:, 0:c1 - c0],
                                                        start=True, stop=(layer != 2))
                                if layer == 2:
                                    if u == 0 and tt == 0:
                                        pe.wait_ge(forget_ready, 1)
                                    for j in range(tt + 1):
                                        f = forget[:, j * FOX_HEADS + u:j * FOX_HEADS + u + 1].broadcast_to([P, P])
                                        last = nc.tensor.matmul(s_bank[:, c0 + j * P:c1], f,
                                                                neg_upto[:, 0:c1 - c0 - j * P],
                                                                start=False, stop=(j == tt))
                        last.then_inc(scored, 1)
                    if 0 <= s - 2 < units and ("probs", layer, s - 2) in T:
                        u = s - 2
                        pe.wait_ge(t_free, T[("probs", layer, u)])
                        if layer == 1:
                            pe.wait_ge(mixed, u // 2 + 1)
                        else:
                            pe.wait_ge(exped, 2 * (SOFT0[layer] + u + 1))
                        src = prob_slot(layer, u - 1 if layer == 1 else u)
                        for tt, (c0, c1) in enumerate(blocks(layer)):
                            for j in range((c1 - c0) // P):
                                at = j * SEQ + tt * P if layer == 0 else (tt if j == 0 else 2) * P
                                last = nc.tensor.transpose(t_bank[:, at:at + P], src[:, c0 + j * P:c0 + (j + 1) * P],
                                                           ident[:])
                        last.then_inc(t_ready, 1)
                    if 0 <= s - 3 < units and out_of(layer, s - 3) is not None:
                        u = s - 3
                        h = out_of(layer, u)
                        c, w = head_cols(layer, u)
                        if is_ret(layer, u):
                            pe.wait_ge(maxed, 2 * (u0 + u + 1))
                            pt = prob_slot(layer, u)
                        else:
                            pe.wait_ge(t_free, T[("probs", layer, u)] + 1)
                            pt = probs_t[:, h % 2]
                        wait(pe, finished, o0 + h)
                        for tt in range(TT):
                            keys = TT if layer == 0 else tt + 1
                            for j in range(keys):
                                at = j * SEQ + tt * P if layer == 0 else (tt if j == 0 else 2) * P
                                last = nc.tensor.matmul(o_bank[:, tt * w:(tt + 1) * w], pt[:, at:at + P],
                                                        area[:, V, j, c:c + w], start=(j == 0), stop=(j == keys - 1))
                        last.then_inc(weighed, 1)

            def forget_scores():
                pe.wait_ge(smalls_landed, 16 * 14)
                pe.wait_ge(t_free, T[("forget",)])
                for tt in range(TT):
                    for kt in range(KT):
                        for n, part in enumerate((act_hi, act_lo)):
                            last = nc.tensor.matmul(t_bank[:, tt * FOX_HEADS:(tt + 1) * FOX_HEADS],
                                                    part[:, kt, tt * P:(tt + 1) * P].bitcast(F32), w_forget[:, kt],
                                                    start=(kt == 0 and n == 0), stop=(kt == KT - 1 and n == 1))
                last.then_inc(t_ready, 1)

            turn_vectors()
            sum_mod(ADA_SHIFT)
            sum_mod(ADA_SCALE)
            pe.wait_ge(xhat_ready, TT)
            turn(0, area[:, Q], T[("mod", ADA_SCALE)] + 1)
            await_turned(0)
            pair(0, 0)
            pair(0, 1)
            sum_mod(ADA_GATE)
            pairs(2, 2)
            sum_mod(A_SHIFT)
            pair(0, 4)
            attention(0, 5)
            pairs(5, 2)
            sum_mod(A_SCALE)
            spread_gate(0, ADA_GATE)
            pe.wait_ge(gated, 8)
            turn(1, area[:, Q], T[("gate", 0, 3)] + 1)
            await_turned(1)
            pairs(7, 2)
            sum_mod(A_GATE)
            pe.wait_ge(normed, TT)
            turn(2, resid, T[("mod", A_GATE)] + 1)
            await_turned(2)
            pairs(9, 2)
            sum_mod(KV_SHIFT)
            pairs(11, 2)
            sum_mod(KV_SCALE)
            pairs(13, 2)
            sum_mod(B_SHIFT)
            attention(1, 15)
            pairs(15, 2)
            spread_gate(1, A_GATE)
            pe.wait_ge(gated, 16)
            turn(3, area[:, Q], T[("gate", 1, 3)] + 1)
            await_turned(3)
            pairs(17, 2)
            sum_mod(B_SCALE)
            pe.wait_ge(normed, 2 * TT)
            turn(4, resid, T[("mod", B_SCALE)] + 1)
            await_turned(4)
            pairs(19, 2)
            sum_mod(B_GATE)
            pairs(21, 2)
            forget_scores()
            turn(5, resid, T[("forget",)] + 1)
            await_turned(5)
            pairs(23, 2)
            attention(2, 25)
            pairs(25, 2)
            spread_gate(2, B_GATE)
            pe.wait_ge(gated, 24)
            turn(6, area[:, Q], T[("gate", 2, 3)] + 1)
            await_turned(6)
            pairs(27, 2)

        @block.scalar
        def _(act):
            act.dma_start(ident[:], a["t_ident"]).then_inc(vecs_landed, 16)
            for dst, src in ((vec_rows[0:16, 0], a["c"][0]), (vec_rows[16:32, 0], a["c_2"][0]),
                             (vec_rows[32:48, 0], a["norm_gain"][0]), (vec_rows[48:96, 0], a["b_ada"][0]),
                             (vec_rows[0:48, 1], a["b_mod_2"][0]), (vec_rows[48:80, 1], a["kv_b_mod_2"]),
                             (vec_rows[80:128, 1], a["b_mod_2"][1])):
                act.dma_start(dst, src.rearrange("(k p) -> k p", p=P)).then_inc(vecs_landed, 16)
            for dst, src in ((probs_t[:, 0], a["t_fwd"]), (probs_t[:, 1], a["t_bwd"]),
                             (neg_upto[:], a["t_neg_upto"]), (subln[:], row_of(a["a_subln_g_2"][0])),
                             (b_forget[:], row_of(a["kv_b_f_2"])),
                             (decay[:, 0:4], row_of(a["ret_decay_logit_f"][0])),
                             (decay[:, 4:8], row_of(a["ret_decay_logit_b"][0])),
                             (probs[:, 0:128], row_of(a["a_lam_q1_2"][0])),
                             (probs[:, 128:256], row_of(a["a_lam_q2_2"][0])),
                             (probs[:, 256:384], row_of(a["a_lam_k1_2"][0])),
                             (probs[:, 384:512], row_of(a["a_lam_k2_2"][0])),
                             (w_forget[:], w_kv[:, :, 2 * D:2 * D + FOX_HEADS]),
                             (bias[:, 0], a["t_dil"][0]), (bias[:, 1], a["t_dil"][1])):
                act.dma_start(dst, src).then_inc(smalls_landed, 16)

            def split_high(half, slot, b, k, chunk_landed):
                if k == 0:
                    act.wait_ge(raw_landed[slot], chunk_landed)
                wait(act, half_used, half - 1)
                nc.scalar.copy(w_hi[:, b], raw[:, slot, HALF_KT * k:HALF_KT * (k + 1)]).then_inc(hi_ready, 1)

            def chunk_halves(i, scale, chunk, js):
                for j in js:
                    split_high(i * (HALVES * scale) + (HALVES * chunk + j), j // 2, j % 2, j % 2,
                               i * (16 * scale) + 16 * (chunk + 1))

            def keep(dst_of, scale):
                def copy_out(i, p0, c):
                    for tt in range(TT):
                        nc.scalar.activation(dst_of(i, c, tt), acc_banks[2 * c + tt][:], ACT.Copy,
                                             scale=scale(c)).then_inc(evacuated, 1)
                return copy_out

            def silu_gate(layer):
                def copy_out(i, p0, c):
                    for tt in range(TT):
                        wait(act, gated, i * 4 + (8 * layer + 4 * (p0 - (5, 15, 25)[layer]) + 2 * c + tt - 1))
                        nc.scalar.activation(side[:, tt], acc_banks[2 * c + tt][:], ACT.Silu).then_inc(evacuated, 1)
                return copy_out

            def pair(i, p0, copy_out, last=False):
                for c in range(2):
                    chunk_halves(i, 2, 2 * p0 + c, range(2, HALVES))
                    if not (last and c == 1):
                        chunk_halves(i, 2, 2 * p0 + c + 1, range(0, 2))
                    if copy_out:
                        act.wait_ge(half_used, i * 16 + (16 * p0 + HALVES * (c + 1)))
                        copy_out(i, p0, c)

            def turn_plain(m):
                for r in range(TURNS):
                    act.wait_ge(turned, TURNS * m + r + 1)
                    nc.scalar.copy(act_hi[:, 2 * r:2 * r + 2], banks[4 + r % TURN_BANKS][:].rearrange(
                        "p (k t) -> p k t", k=2)).then_inc(turned_hi, 1)

            def turn_scaled(m, n, shift):
                act.wait_ge(scales_ready, n + 1)
                for r in range(TURNS):
                    act.wait_ge(turned, TURNS * m + r + 1)
                    for k in range(2):
                        kt = 2 * r + k
                        last = nc.scalar.activation(act_hi[:, kt], banks[4 + r % TURN_BANKS][:, k * SEQ:(k + 1) * SEQ],
                                                    ACT.Identity, scale=scales[:, n, kt:kt + 1],
                                                    bias=mod[:, shift, kt:kt + 1])
                    last.then_inc(turned_hi, 1)

            def gate_row(layer):
                for n in range(D // CHUNK):
                    act.wait_ge(t_ready, T[("gate", layer, n)] + 1)
                    nc.scalar.copy(area[:, K, 0, n * CHUNK:(n + 1) * CHUNK], t_bank[:]).then_inc(t_free, 1)

            def norm_rows(layer):
                act.wait_ge(weighed, OUT0[layer] + OUTS[layer])
                act.dma_start(area[:, K, 1], row_of(a["final_gain"] if layer == 0 else a["ln_g_2"][layer - 1])
                              ).then_inc(rows_landed, 16)
                if layer:
                    act.dma_start(area[:, V, 0], row_of(a["ln_b_2"][layer - 1])).then_inc(rows_landed, 16)

            def attention(layer):
                units, u0, o0 = UNITS[layer], UNIT0[layer], OUT0[layer]
                for s in range(units + 3):
                    if s < units:
                        u = s
                        act.wait_ge(t_ready, T[("qk", layer, u)] + 1)
                        wait(act, scored, u0 + u - 1 if u >= 2 else u0)
                        nc.scalar.copy(qk_t[:, u % 2], t_bank[:]).then_inc(t_free, 1)
                    if 0 <= s - 2 < units and ("probs", layer, s - 2) in T:
                        u = s - 2
                        h = out_of(layer, u)
                        w = 512 if layer == 0 else 384
                        act.wait_ge(t_ready, T[("probs", layer, u)] + 1)
                        wait(act, weighed, o0 + h - 1 if h >= 2 else o0)
                        nc.scalar.copy(probs_t[:, h % 2, 0:w], t_bank[:, 0:w]).then_inc(t_free, 1)
                    if 0 <= s - 1 < units and not is_ret(layer, s - 1):
                        u = s - 1
                        p = prob_slot(layer, u)
                        act.wait_ge(maxed, 2 * (u0 + u + 1))
                        if layer == 1:
                            wait(act, mixed, (u - 2) // 2 if u >= 4 else 0)
                        elif u >= 4:
                            act.wait_ge(finished, o0 + u - 3)
                        for tt, (c0, c1) in enumerate(blocks(layer)):
                            nc.scalar.activation(p[:, c0:c1], p[:, c0:c1], ACT.Exp, scale=-1.0,
                                                 bias=neg_max[:, u % 4, tt:tt + 1],
                                                 accum_out=den[:, u % 4, tt:tt + 1]).then_inc(exped, 1)
                        if layer == 0 and u + 2 < DIL_HEADS:
                            act.dma_start(bias[:, u % 2], a["t_dil"][u + 2]).then_inc(bias_landed[u % 2], 16)
                        if layer == 1 and u % 2 and u // 2 + 2 < DIFF_HEADS:
                            act.dma_start(bias[:, u // 2 % 2, 0:384], a["t_diff"][u // 2 + 2]
                                          ).then_inc(bias_landed[u // 2 % 2], 16)
                    if 0 <= s - 3 < units and is_normed(layer, s - 3):
                        inverse_root(("head", layer, s - 3))

            def first_bias(layer):
                act.wait_ge(maxed, 2 * (UNIT0[layer - 1] + UNITS[layer - 1]))
                if layer == 1:
                    for i in range(2):
                        act.dma_start(bias[:, i, 0:384], a["t_diff"][i]).then_inc(bias_landed[i], 16)
                else:
                    act.dma_start(bias[:, 0, 0:384], a["t_causal"]).then_inc(bias_landed[0], 16)

            def inverse_root(key):
                n = ROOTS[key]
                act.wait_ge(var_ready, n + 1)
                nc.scalar.activation(log_sq[:], mean_sq[:], ACT.Ln).then_inc(root_ready, 1)
                act.wait_ge(root_ready, 2 * n + 1)
                nc.scalar.activation(root[:], log_sq[:], ACT.Exp, scale=-0.5).then_inc(root_ready, 1)

            def log_sigmoid(n, cols):
                act.wait_ge(sigmoid_to_act, 2 * n + 1)
                nc.scalar.activation(ls[:, 2, 0:cols], ls[:, 1, 0:cols], ACT.Exp).then_inc(sigmoid_to_dve, 1)
                act.wait_ge(sigmoid_to_act, 2 * n + 2)
                nc.scalar.activation(ls[:, 4, 0:cols], ls[:, 3, 0:cols], ACT.Ln).then_inc(sigmoid_to_dve, 1)

            act.wait_ge(t_free, T[("vec",)] + 1)
            nc.scalar.activation(c_act[:], vecs[:, 0:2 * KT], ACT.Silu).then_inc(silu_ready, 1)
            log_sigmoid(0, 2 * RET_HEADS)
            act.wait_ge(lam_products, 2)
            nc.scalar.activation(lam[:, 2:4], lam[:, 0:2], ACT.Exp).then_inc(lam_exped, 1)
            act.wait_ge(decay_ready, 1)
            for h in range(RET_HEADS):
                wait(act, decay_used, h)
                nc.scalar.activation(side[:, 0], probs_t[:, 0], ACT.Exp, scale=decay[:, h:h + 1])
                nc.scalar.activation(side[:, 1], probs_t[:, 1], ACT.Exp,
                                     scale=decay[:, 4 + h:5 + h]).then_inc(decay_exped, 1)
            inverse_root(("x",))
            act.wait_ge(xhat_scale, 1)
            for tt in range(TT):
                nc.scalar.activation(area[:, Q, tt], resid[:, tt], ACT.Copy, scale=rstd[:, tt:tt + 1]
                                     ).then_inc(xhat_ready, 1)
            turn_scaled(0, 0, ADA_SHIFT)
            chunk_halves(0, 1, 0, range(0, 2))
            one = lambda c: 1.0
            pair(0, 0, keep(lambda i, c, tt: area[:, Q, tt, c * CHUNK:(c + 1) * CHUNK], lambda c: QK_SCALE))
            pair(0, 1, keep(lambda i, c, tt: area[:, K, tt, c * CHUNK:(c + 1) * CHUNK], one))
            pair(0, 2, keep(lambda i, c, tt: area[:, V, tt, c * CHUNK:(c + 1) * CHUNK], one))
            ret_qk = area[:, Q, :, 1024:2048].rearrange("p t (h c e) -> p t c h e", c=2, e=HEAD)

            def keep_ret(i, p0, c):
                for tt in range(TT):
                    nc.scalar.activation(ret_qk[:, tt, c], acc_banks[2 * c + tt][:].rearrange(
                        "p (h e) -> p h e", e=HEAD), ACT.Copy, scale=QK_SCALE if c else 1.0).then_inc(evacuated, 1)
            pair(0, 3, keep_ret)
            pair(0, 4, keep(lambda i, c, tt: area[:, V, tt, 1024 + c * CHUNK:1024 + (c + 1) * CHUNK], one))
            attention(0)
            pair(0, 5, silu_gate(0))
            pair(0, 6, silu_gate(0))
            norm_rows(0)
            first_bias(1)
            gate_row(0)
            turn_plain(1)
            with act.Fori(0, 2) as i:
                pair(i, 7, None)
            inverse_root(("norm", 0))
            turn_scaled(2, 1, A_SHIFT)
            for which, scale in ((Q, QK_SCALE), (K, 1.0), (V, 1.0)):
                with act.Fori(0, 2) as i:
                    pair(i, 9 + 2 * which, keep(
                        lambda i, c, tt: area[:, which, tt, bass.ds(i * (2 * CHUNK) + c * CHUNK, CHUNK)],
                        lambda c: scale))
            attention(1)
            with act.Fori(0, 2) as i:
                pair(i, 15, silu_gate(1))
            norm_rows(1)
            first_bias(2)
            gate_row(1)
            turn_plain(3)
            with act.Fori(0, 2) as i:
                pair(i, 17, None)
            inverse_root(("norm", 1))
            turn_scaled(4, 2, KV_SHIFT)
            for n, which in enumerate((K, V)):
                with act.Fori(0, 2) as i:
                    pair(i, 19 + 2 * n, keep(
                        lambda i, c, tt: area[:, which, tt, bass.ds(i * (2 * CHUNK) + c * CHUNK, CHUNK)], one))
            log_sigmoid(1, TT * FOX_HEADS)
            turn_scaled(5, 3, B_SHIFT)
            with act.Fori(0, 2) as i:
                pair(i, 23, keep(lambda i, c, tt: area[:, Q, tt, bass.ds(i * (2 * CHUNK) + c * CHUNK, CHUNK)],
                                 lambda c: QK_SCALE))
            attention(2)
            with act.Fori(0, 2) as i:
                pair(i, 25, silu_gate(2))
            norm_rows(2)
            gate_row(2)
            turn_plain(6)
            pair(0, 27, None)
            pair(0, 28, None, last=True)
            inverse_root(("norm", 2))

        @block.vector
        def _(dve):
            chain = [0]

            def link(ins):
                chain[0] += 1
                ins.then_inc(dve_chain, 1)
                dve.wait_ge(dve_chain, chain[0])

            def chunk_halves(i, scale, chunk, js):
                for j in js:
                    dve.wait_ge(hi_ready, i * (HALVES * scale) + (HALVES * chunk + j + 1))
                    nc.vector.tensor_tensor(w_lo[:, j % 2], raw[:, j // 2, HALF_KT * (j % 2):HALF_KT * (j % 2 + 1)],
                                            w_hi[:, j % 2].bitcast(F32), ALU.subtract).then_inc(lo_ready, 1)

            def gemv_step(b, k):
                g = KT * b + k
                cc = c_act[:, (0 if b <= ADA_GATE else KT) + k:(0 if b <= ADA_GATE else KT) + k + 1]
                dve.wait_ge(gw_landed[g % GEMV_RING], 16 * (g // GEMV_RING + 1))
                if k == 0:
                    nc.vector.tensor_scalar(acc[:], gw[:, g % GEMV_RING], cc, None, ALU.mult).then_inc(gemv_used, 1)
                else:
                    dve.wait_ge(gemv_used, g)
                    nc.vector.scalar_tensor_tensor(out=acc[:], in0=gw[:, g % GEMV_RING], scalar=cc, in1=acc[:],
                                                   op0=ALU.mult, op1=ALU.add).then_inc(gemv_used, 1)

            def finish_mod(b):
                dve.wait_ge(t_ready, T[("mod", b)] + 1)
                nc.vector.tensor_tensor(mod[:, b], t_bank[:, 0:KT], vecs[:, VEC_BIAS + KT * b:VEC_BIAS + KT * (b + 1)],
                                        ALU.add).then_inc(t_free, 1)

            def gate_y(layer):
                def take(i, p0, c):
                    for tt in range(TT):
                        p1 = p0 - (5, 15, 25)[layer]
                        y = area[:, Q, tt, bass.ds(i * (2 * CHUNK) + (2 * p1 + c) * CHUNK, CHUNK)]
                        dve.wait_ge(evacuated, i * 4 + (4 * p0 + 2 * c + tt + 1))
                        nc.vector.tensor_tensor(y, y, side[:, tt], ALU.mult).then_inc(gated, 1)
                return take

            def add_out(layer):
                first = (7, 17, 27)[layer]
                alpha = 1.0 if layer == 0 else DN_ALPHA

                def take(i, p0, c):
                    col = i * (2 * CHUNK) + (2 * (p0 - first) + c) * CHUNK
                    dve.wait_ge(half_used, i * 16 + (16 * p0 + HALVES * (c + 1)))
                    for tt in range(TT):
                        nc.vector.tensor_tensor(side[:, tt], acc_banks[2 * c + tt][:], area[:, K, 0, bass.ds(col, CHUNK)],
                                                ALU.mult).then_inc(evacuated, 1)
                    for tt in range(TT):
                        x = resid[:, tt, bass.ds(col, CHUNK)]
                        dve.wait_ge(evacuated, i * 4 + (4 * p0 + 2 * c + tt + 1))
                        nc.vector.scalar_tensor_tensor(out=x, in0=x, scalar=alpha, in1=side[:, tt], op0=ALU.mult,
                                                       op1=ALU.add).then_inc(summed, 1)
                    for tt in range(TT):
                        dve.wait_ge(summed, i * 4 + (8 * layer + 4 * (p0 - first) + 2 * c + tt + 1))
                        nc.vector.bn_stats(stats[:, tt, 2 * (p0 - first) + c],
                                           resid[:, tt, bass.ds(col, CHUNK)]).then_inc(measured, 1)
                return take

            def pair(p0, take, i=0, last=False):
                b, k0 = MOD_AT_PAIR.get(p0), 0
                if b is None and p0 - 1 in MOD_AT_PAIR and isinstance(i, int):
                    b, k0 = MOD_AT_PAIR[p0 - 1], 8
                k = 0
                for c in range(2):
                    order = [(2 * p0 + c, j) for j in range(2, HALVES)]
                    if not (last and c == 1):
                        order += [(2 * p0 + c + 1, j) for j in range(2)]
                    for n, (chunk, j) in enumerate(order):
                        chunk_halves(i, 2, chunk, [j])
                        if n == 1 and c == 0 and p0 in (2, 4, 11, 13):
                            finish_mod(MOD_AT_PAIR[p0 - 2])
                        if b is not None and n % 2 == 1:
                            gemv_step(b, k0 + k)
                            k += 1
                    if take:
                        take(i, p0, c)

            def turn_scaled(m, n, shift, scale):
                if n == 0:
                    nc.vector.scalar_tensor_tensor(
                        out=scales[:, 0], in0=mod[:, scale], scalar=1.0, in1=vecs[:, VEC_GAIN:VEC_GAIN + KT],
                        op0=ALU.add, op1=ALU.mult).then_inc(scales_ready, 1)
                else:
                    nc.vector.tensor_scalar(scales[:, n], mod[:, scale], 1.0, None, ALU.add).then_inc(scales_ready, 1)
                dve.wait_ge(scales_ready, n + 1)
                for r in range(TURNS):
                    dve.wait_ge(turned_hi, TURNS * m + r + 1)
                    for k in range(2):
                        kt = 2 * r + k
                        nc.vector.tensor_scalar(side[:, r % 2, k * SEQ:(k + 1) * SEQ],
                                                banks[4 + r % TURN_BANKS][:, k * SEQ:(k + 1) * SEQ],
                                                scales[:, n, kt:kt + 1], mod[:, shift, kt:kt + 1], ALU.mult, ALU.add
                                                ).then_inc(shifted, 1)
                    dve.wait_ge(shifted, 2 * (TURNS * n + r + 1))
                    nc.vector.tensor_tensor(act_lo[:, 2 * r:2 * r + 2], side[:, r % 2].rearrange("p (k t) -> p k t", k=2),
                                            act_hi[:, 2 * r:2 * r + 2].bitcast(F32), ALU.subtract).then_inc(turned_lo, 1)

            def turn_plain(m):
                for r in range(TURNS):
                    dve.wait_ge(turned_hi, TURNS * m + r + 1)
                    nc.vector.tensor_tensor(act_lo[:, 2 * r:2 * r + 2],
                                            banks[4 + r % TURN_BANKS][:].rearrange("p (k t) -> p k t", k=2),
                                            act_hi[:, 2 * r:2 * r + 2].bitcast(F32), ALU.subtract).then_inc(turned_lo, 1)

            def inverse_root(key, to_mean_sq):
                to_mean_sq.then_inc(var_ready, 1)
                dve.wait_ge(root_ready, 2 * (ROOTS[key] + 1))
                link(nc.vector.tensor_tensor(rstd[:], root[:], root[:], ALU.mult))
                link(nc.vector.scalar_tensor_tensor(out=rstd[:], in0=rstd[:], scalar=-0.5, in1=mean_sq[:],
                                                    op0=ALU.mult, op1=ALU.mult))
                return nc.vector.scalar_tensor_tensor(out=rstd[:], in0=rstd[:], scalar=1.5, in1=root[:],
                                                      op0=ALU.add, op1=ALU.mult)

            def root_mean_square(key, eps):
                link(nc.vector.tensor_tensor(mean_sq[:], moments[:, :, 0], moments[:, :, 0], ALU.mult))
                return inverse_root(key, nc.vector.scalar_tensor_tensor(
                    out=mean_sq[:], in0=mean_sq[:], scalar=eps, in1=moments[:, :, 1], op0=ALU.add, op1=ALU.add))

            def norm(layer):
                dve.wait_ge(measured, 4 * TT * (layer + 1))
                link(nc.vector.bn_aggr(moments[:, 0], stats[:, 0]))
                link(nc.vector.bn_aggr(moments[:, 1], stats[:, 1]))
                if layer == 0:
                    link(root_mean_square(("norm", layer), NORM_EPS))
                else:
                    link(inverse_root(("norm", layer), nc.vector.tensor_scalar(
                        mean_sq[:], moments[:, :, 1], EPS, None, ALU.add)))
                dve.wait_ge(rows_landed, 16 * (1, 3, 5)[layer])
                gain, shift = area[:, K, 1], area[:, V, 0]
                for tt in range(TT):
                    x = resid[:, tt]
                    if layer == 0:
                        nc.vector.scalar_tensor_tensor(out=x, in0=x, scalar=rstd[:, tt:tt + 1], in1=gain,
                                                       op0=ALU.mult, op1=ALU.mult).then_inc(normed, 1)
                    else:
                        link(nc.vector.tensor_scalar(x, x, moments[:, tt, 0:1], rstd[:, tt:tt + 1],
                                                     ALU.subtract, ALU.mult))
                        link(nc.vector.tensor_tensor(x, x, gain, ALU.mult))
                        nc.vector.tensor_tensor(x, x, shift, ALU.add).then_inc(normed, 1)

            def finish_head(layer, u):
                h, (c, w) = out_of(layer, u), head_cols(layer, u)
                dve.wait_ge(weighed, OUT0[layer] + h + 1)
                o = [o_bank[:, tt * w:(tt + 1) * w] for tt in range(TT)]
                y = [area[:, Q, tt, c:c + w] for tt in range(TT)]
                if layer == 1 or is_ret(layer, u):
                    for tt in range(TT):
                        link(nc.vector.bn_stats(stats[:, tt, 0], o[tt]))
                    for tt in range(TT):
                        link(nc.vector.bn_aggr(moments[:, tt], stats[:, tt, 0]))
                    link(root_mean_square(("head", layer, u), EPS if layer == 1 else NORM_EPS))
                    for tt in range(TT):
                        if layer == 1:
                            last = nc.vector.scalar_tensor_tensor(out=y[tt], in0=o[tt], scalar=rstd[:, tt:tt + 1],
                                                                  in1=subln[:], op0=ALU.mult, op1=ALU.mult)
                        else:
                            last = nc.vector.tensor_scalar(y[tt], o[tt], rstd[:, tt:tt + 1], None, ALU.mult)
                else:
                    for tt in range(TT):
                        last = nc.vector.tensor_scalar(y[tt], o[tt], rden[:, u % 4, tt:tt + 1], None, ALU.mult)
                last.then_inc(finished, 1)

            def attention(layer):
                units, u0, o0 = UNITS[layer], UNIT0[layer], OUT0[layer]
                for s in range(units + 3):
                    if 0 <= s - 2 < units and not is_ret(layer, s - 2):
                        u = s - 2
                        dve.wait_ge(exped, 2 * (SOFT0[layer] + u + 1))
                        if layer != 1:
                            link(nc.vector.reciprocal(rden[:, u % 4], den[:, u % 4]))
                        elif u % 2:
                            p0, p1 = prob_slot(layer, u - 1), prob_slot(layer, u)
                            link(nc.vector.reciprocal(rden[:, u % 4 - 1:u % 4 + 1], den[:, u % 4 - 1:u % 4 + 1]))
                            link(nc.vector.tensor_scalar(rden[:, u % 4], rden[:, u % 4], lam[:, 4:5], None, ALU.mult))
                            for tt, (c0, c1) in enumerate(blocks(layer)):
                                link(nc.vector.tensor_scalar(p0[:, c0:c1], p0[:, c0:c1],
                                                             rden[:, u % 4 - 1, tt:tt + 1], None, ALU.mult))
                            for tt, (c0, c1) in enumerate(blocks(layer)):
                                last = nc.vector.scalar_tensor_tensor(
                                    out=p0[:, c0:c1], in0=p1[:, c0:c1], scalar=rden[:, u % 4, tt:tt + 1],
                                    in1=p0[:, c0:c1], op0=ALU.mult, op1=ALU.add)
                            last.then_inc(mixed, 1)
                    if 0 <= s - 1 < units:
                        u = s - 1
                        dve.wait_ge(scored, u0 + u + 1)
                        s_bank, p = s_banks[u % 2], prob_slot(layer, u)
                        if layer == 0 and u >= 2:
                            if is_ret(layer, u - 2):
                                dve.wait_ge(weighed, o0 + u - 1)
                            else:
                                dve.wait_ge(t_ready, T[("probs", layer, u - 2)] + 1)
                        if layer == 1 and u >= 4:
                            dve.wait_ge(t_ready, T[("probs", layer, (u - 4) | 1)] + 1)
                        if layer == 2 and u >= 4:
                            dve.wait_ge(t_ready, T[("probs", layer, u - 4)] + 1)
                        if is_ret(layer, u):
                            nc.vector.tensor_tensor(p, s_bank[:], decay_table(u - DIL_HEADS), ALU.mult).then_inc(maxed, 2)
                        else:
                            if layer == 0:
                                if u >= 2:
                                    dve.wait_ge(bias_landed[u % 2], 16 * (u // 2))
                                b = bias[:, u % 2]
                            elif layer == 1:
                                h = u // 2
                                dve.wait_ge(bias_landed[h % 2], 16 * (DIL_HEADS // 2 - 1 + h // 2 + 1))
                                b = bias[:, h % 2]
                            else:
                                dve.wait_ge(bias_landed[0], 16 * (DIL_HEADS // 2 - 1 + DIFF_HEADS // 2 + 1))
                                b = bias[:, 0]
                            for tt, (c0, c1) in enumerate(blocks(layer)):
                                nc.vector.tensor_tensor_reduce(
                                    out=p[:, c0:c1], in0=s_bank[:, c0:c1], in1=b[:, c0:c1], scale=-1.0, scalar=FLT_MAX,
                                    op0=ALU.add, op1=ALU.min, accum_out=neg_max[:, u % 4, tt:tt + 1]).then_inc(maxed, 1)
                    if 0 <= s - 3 < units and out_of(layer, s - 3) is not None:
                        finish_head(layer, s - 3)

            def log_sigmoid(n, cols, dst):
                z, nz, e, w, l, d, one = (ls[:, k, 0:cols] for k in range(7))
                nc.vector.scalar_tensor_tensor(out=nz, in0=z, scalar=-1.0, in1=z, op0=ALU.mult,
                                               op1=ALU.min).then_inc(sigmoid_to_act, 1)
                dve.wait_ge(sigmoid_to_dve, 2 * n + 1)
                nc.vector.tensor_scalar(w, e, 1.0, None, ALU.add).then_inc(sigmoid_to_act, 1)
                dve.wait_ge(sigmoid_to_act, 2 * n + 2)
                link(nc.vector.tensor_scalar(d, w, -1.0, None, ALU.add))
                link(nc.vector.tensor_scalar(one, d, 0.0, None, ALU.is_equal))
                link(nc.vector.tensor_tensor(d, d, one, ALU.add))
                link(nc.vector.reciprocal(d, d))
                link(nc.vector.tensor_tensor(d, d, e, ALU.mult))
                dve.wait_ge(sigmoid_to_dve, 2 * n + 2)
                link(nc.vector.tensor_tensor(l, l, one, ALU.add))
                link(nc.vector.tensor_tensor(d, d, l, ALU.mult))
                return nc.vector.scalar_tensor_tensor(out=dst, in0=z, scalar=0.0, in1=d, op0=ALU.min, op1=ALU.subtract)

            nc.vector.memset(ones[:], 1.0).then_inc(consts_ready, 1)
            dve.wait_ge(t_ready, T[("vec",)] + 1)
            nc.vector.tensor_copy(vecs[:], t_bank[:, 0:VECS]).then_inc(t_free, 1)
            dve.wait_ge(smalls_landed, 16 * 14)
            link(nc.vector.tensor_copy(ls[:, 0, 0:2 * RET_HEADS], decay[:]))
            link(log_sigmoid(0, 2 * RET_HEADS, decay[:]))
            nc.vector.tensor_scalar(decay[:], decay[:], -1e-20, None, ALU.min).then_inc(decay_ready, 1)
            for n in range(2):
                nc.vector.tensor_tensor_reduce(
                    out=ls[:].rearrange("p a b -> p (a b)")[:, 0:HEAD], in0=probs[:, n * HEAD:(n + 1) * HEAD],
                    in1=probs[:, (2 + n) * HEAD:(3 + n) * HEAD], scale=1.0, scalar=0.0, op0=ALU.mult, op1=ALU.add,
                    accum_out=lam[:, n:n + 1]).then_inc(lam_products, 1)
                dve.wait_ge(lam_products, n + 1)
            dve.wait_ge(lam_exped, 1)
            link(nc.vector.scalar_tensor_tensor(out=lam[:, 4:5], in0=lam[:, 3:4], scalar=LAM_INIT, in1=lam[:, 2:3],
                                                op0=ALU.subtract, op1=ALU.subtract))
            link(nc.vector.tensor_scalar(subln[:], subln[:], 1.0 - LAM_INIT, None, ALU.mult))
            for h in range(RET_HEADS):
                dve.wait_ge(decay_exped, h + 1)
                nc.vector.tensor_tensor(decay_table(h), side[:, 0], side[:, 1], ALU.add).then_inc(decay_used, 1)
            dve.wait_ge(x_landed, 16)
            for tt in range(TT):
                for n in range(D // CHUNK):
                    link(nc.vector.bn_stats(stats[:, tt, n], resid[:, tt, n * CHUNK:(n + 1) * CHUNK]))
                link(nc.vector.bn_aggr(moments[:, tt], stats[:, tt]))
            root_mean_square(("x",), NORM_EPS).then_inc(xhat_scale, 1)
            dve.wait_ge(silu_ready, 1)
            for b in (ADA_SHIFT, ADA_SCALE):
                for k in range(KT):
                    gemv_step(b, k)
                finish_mod(b)
            dve.wait_ge(t_free, T[("mod", ADA_SCALE)] + 1)
            turn_scaled(0, 0, ADA_SHIFT, ADA_SCALE)
            chunk_halves(0, 1, 0, range(0, 2))
            for p in range(5):
                pair(p, None)
            attention(0)
            pair(5, gate_y(0))
            pair(6, gate_y(0))
            finish_mod(A_SCALE)
            turn_plain(1)
            pair(7, add_out(0))
            pair(8, add_out(0))
            norm(0)
            finish_mod(A_GATE)
            turn_scaled(2, 1, A_SHIFT, A_SCALE)
            for p in range(9, 15):
                pair(p, None)
            finish_mod(B_SHIFT)
            attention(1)
            with dve.Fori(0, 2) as i:
                pair(15, gate_y(1), i=i)
            turn_plain(3)
            pair(17, add_out(1))
            pair(18, add_out(1))
            norm(1)
            finish_mod(B_SCALE)
            turn_scaled(4, 2, KV_SHIFT, KV_SCALE)
            pair(19, None)
            pair(20, None)
            finish_mod(B_GATE)
            with dve.Fori(0, 2) as i:
                pair(21, None, i=i)
            dve.wait_ge(t_ready, T[("forget",)] + 1)
            for tt in range(TT):
                last = nc.vector.tensor_tensor(ls[:, 0, tt * FOX_HEADS:(tt + 1) * FOX_HEADS],
                                               t_bank[:, tt * FOX_HEADS:(tt + 1) * FOX_HEADS], b_forget[:], ALU.add)
            last.then_inc(t_free, 1)
            dve.wait_ge(t_free, T[("forget",)] + 1)
            log_sigmoid(1, TT * FOX_HEADS, forget[:]).then_inc(forget_ready, 1)
            turn_scaled(5, 3, B_SHIFT, B_SCALE)
            with dve.Fori(0, 2) as i:
                pair(23, None, i=i)
            attention(2)
            with dve.Fori(0, 2) as i:
                pair(25, gate_y(2), i=i)
            turn_plain(6)
            pair(27, add_out(2))
            pair(28, add_out(2), last=True)
            norm(2)


INPUTS = ["x", "c", "norm_gain", "w_ada", "b_ada", "w_in", "w_out", "ret_decay_logit_f", "ret_decay_logit_b",
          "final_gain", "c_2", "w_mod_2", "b_mod_2", "ln_g_2", "ln_b_2", "a_w_in_2", "a_w_out_2", "a_lam_q1_2",
          "a_lam_k1_2", "a_lam_q2_2", "a_lam_k2_2", "a_subln_g_2", "kv_w_mod_2", "kv_b_mod_2", "kv_w_2", "kv_b_f_2",
          "b_w_in_2", "b_w_out_2"]


def kernel(**inputs):
    import concourse.bacc as bacc
    from concourse.bass_utils import run_bass_kernel_spmd as run

    nc = bacc.Bacc("TRN2", target_bir_lowering=False, num_devices=1)
    arrays = {name: np.ascontiguousarray(inputs[name]) for name in INPUTS}
    arrays.update(shape_tables())
    aps = {name: nc.dram_tensor(f"in_{name}", v.shape, mybir.dt.from_np(v.dtype), kind="ExternalInput").ap()
           for name, v in arrays.items()}
    out = nc.dram_tensor("out_0", (1, SEQ, D), F32, kind="ExternalOutput").ap()
    two_blocks(nc, aps, out)
    r = run(nc, [{f"in_{k}": v for k, v in arrays.items()}], core_ids=[0])
    return r.results[0]["out_0"]
```

```python
import math
from contextlib import ExitStack

import numpy as np

import concourse.bass as bass
from concourse import mybir

F32 = mybir.dt.float32
F32R = mybir.dt.float32r
ALU = mybir.AluOpType
ACT = mybir.ActivationFunctionType

P = 128
D = 2048
SEQ = 256
TT = SEQ // P
KT = D // P
CHUNK = 512
STEP_KT = 2
STEPS = KT // STEP_KT
SLOTS = 4
LEAD = 4
GEMV_RING = 2
TURN_BANKS = 4
TURNS = KT // 2

DIL_HEADS = 8
RET_HEADS = 4
DIFF_HEADS = 8
FOX_HEADS = 16
HEAD = 128
WIDE = 256
QK_SCALE = HEAD ** -0.5
DILATIONS = ((128, 1), (512, 4), (2048, 16))
NEG = -1e30
FLT_MAX = 3e38
NORM_EPS = 1e-6
EPS = 1e-5
LAM_INIT = 0.8 - 0.6 * math.exp(-0.3 * 0)
DN_ALPHA = (2.0 * 2) ** 0.25

(ADA_SHIFT, ADA_SCALE, ADA_GATE, A_SHIFT, A_SCALE, A_GATE, KV_SHIFT, KV_SCALE, B_SHIFT, B_SCALE,
 B_GATE) = range(11)
MODS = 11
PAIRS = 29
MOD_STEPS = {ADA_GATE: ((0, 6), (1, 5), (2, 5)), A_SHIFT: ((3, 6), (4, 5), (5, 5)),
             A_SCALE: ((6, 6), (7, 5), (8, 5)), A_GATE: ((9, 6), (10, 5), (11, 5)),
             KV_SHIFT: ((12, 6), (13, 5), (14, 5)), KV_SCALE: ((15, 6), (16, 5), (17, 5)),
             B_SHIFT: ((18, 8), (19, 8)), B_SCALE: ((20, 6), (21, 5), (22, 5)),
             B_GATE: ((23, 4), (24, 4), (25, 4), (26, 4))}
SUM_AFTER = {steps[-1][0]: b for b, steps in MOD_STEPS.items()}
PAIR_STEPS = 2 * STEPS
STEP_HALVES = (2, 5, 8, 11, 14, 17, 20, 23, 24, 26, 28, 30, 32, 34, 36, 38, 40, 42, 44, 46)
STEP_AT = {h: s for s, h in enumerate(STEP_HALVES)}
ATTENTION_PAIR = (4, 14, 24)
GATE_PAIR = (5, 15, 25)
OUT_PAIR = (7, 17, 27)
TURN_PAIR = (0, 7, 9, 17, 19, 23, 27)
START_RING = 4

VEC_C, VEC_GAIN, VEC_BIAS = 0, 2 * KT, 3 * KT
VEC_FINAL = VEC_BIAS + MODS * KT
VEC_LN_G, VEC_LN_B = VEC_FINAL + KT, VEC_FINAL + 2 * KT
VECS = VEC_FINAL + 3 * KT


def finish_half(pair):
    if pair - 1 not in SUM_AFTER or pair in TURN_PAIR:
        return None
    return 0 if any(0 <= pair - p < 3 for p in ATTENTION_PAIR) else LEAD


def gemv_steps(pair):
    for b, steps in MOD_STEPS.items():
        k = 0
        for p, n in steps:
            if p == pair:
                first = (finish_half(pair) or 0) + 1
                return [(first + i * ((14 - first) / n), b, k + i) for i in range(n)]
            k += n
    return []


def alibi(n):
    return [2.0 ** (-8.0 * (h + 1) / n) for h in range(n)]


def shape_tables():
    t = np.arange(SEQ)
    rel = t[:, None] - t[None, :]
    dist = np.abs(rel).astype(np.float64)
    seen = np.zeros((SEQ, SEQ))
    for window, dilation in DILATIONS:
        seen += (rel % dilation == 0) & (dist <= (window // (2 * dilation)) * dilation)
    log_seen = np.where(seen > 0, np.log(np.maximum(seen, 1)), NEG)

    def by_tile(a):
        return a.reshape(TT, P, SEQ).transpose(1, 0, 2)

    def causal_blocks(a):
        b = by_tile(a)
        return np.concatenate([b[:, 0, :P], b[:, 1, :]], axis=1)

    dil = np.stack([by_tile(np.where(seen > 0, -s * dist + log_seen, NEG)).reshape(P, -1)
                    for s in alibi(DIL_HEADS)])
    diff = np.stack([causal_blocks(np.where(rel >= 0, -s * dist, NEG)) for s in alibi(DIFF_HEADS)])
    causal = causal_blocks(np.where(rel >= 0, 0.0, NEG))
    q_minus_k = t[None, :] - t[:, None]
    fwd = by_tile(np.where(q_minus_k >= 0, q_minus_k, 1e30)).reshape(P, -1)
    bwd = by_tile(np.where(q_minus_k <= 0, -q_minus_k, 1e30)).reshape(P, -1)
    p = np.arange(P)
    neg_upto = -(p[:, None] <= t[None, :]).astype(np.float64)
    out = {"t_ident": np.eye(P), "t_dil": dil, "t_diff": diff, "t_causal": causal, "t_fwd": fwd,
           "t_bwd": bwd, "t_neg_upto": neg_upto}
    return {k: np.ascontiguousarray(v, dtype=np.float32) for k, v in out.items()}


def t_uses(units, has_probs):
    uses = [("vec",), ("mod", ADA_SHIFT), ("mod", ADA_SCALE)]
    for pair in range(PAIRS):
        for h in range(PAIR_STEPS):
            for layer in range(3):
                at = h + PAIR_STEPS * (pair - ATTENTION_PAIR[layer])
                if at in STEP_AT:
                    s = STEP_AT[at]
                    if s < units[layer]:
                        uses.append(("qk", layer, s))
                    if has_probs(layer, s - 2):
                        uses.append(("probs", layer, s - 2))
                if pair == OUT_PAIR[layer] and h < 4:
                    uses.append(("gate", layer, h))
        if pair in SUM_AFTER:
            uses.append(("mod", SUM_AFTER[pair]))
        if pair == 22:
            uses.append(("forget",))
    return {u: n for n, u in enumerate(uses)}


def two_blocks(nc, a, out):
    UNITS = [DIL_HEADS + RET_HEADS, 2 * DIFF_HEADS, FOX_HEADS]
    UNIT0 = [0, UNITS[0], UNITS[0] + UNITS[1]]
    SOFT = [DIL_HEADS, UNITS[1], UNITS[2]]
    SOFT0 = [0, SOFT[0], SOFT[0] + SOFT[1]]
    OUTS = [UNITS[0], DIFF_HEADS, FOX_HEADS]
    OUT0 = [0, OUTS[0], OUTS[0] + OUTS[1]]

    def out_of(layer, u):
        if layer == 1:
            return u // 2 if u % 2 else None
        return u

    def is_ret(layer, u):
        return layer == 0 and u >= DIL_HEADS

    def is_normed(layer, u):
        return is_ret(layer, u) or (layer == 1 and u % 2 == 1)

    def has_probs(layer, u):
        return 0 <= u < UNITS[layer] and not is_ret(layer, u) and (layer != 1 or u % 2 == 1)

    T = t_uses(UNITS, has_probs)

    ROOTS = [("x",)]
    for layer in range(3):
        ROOTS += [("head", layer, u) for u in range(UNITS[layer]) if is_normed(layer, u)]
        ROOTS.append(("norm", layer))
    ROOTS = {key: n for n, key in enumerate(ROOTS)}

    with ExitStack() as ctx:
        def sb(name, shape, dt=F32):
            return ctx.enter_context(nc.sbuf_tensor(name, shape, dt))

        def psum(name, shape):
            return ctx.enter_context(nc.psum_tensor(name, shape, F32))

        def sem(name):
            return ctx.enter_context(nc.semaphore(name))

        resid = sb("resid", [P, TT, D])
        act_hi = sb("act_hi", [P, KT, SEQ], F32R)
        act_lo = sb("act_lo", [P, KT, SEQ], F32R)
        area = sb("area", [P, 3, TT, D])
        Q, K, V = 0, 1, 2
        raw = sb("raw", [P, SLOTS, STEP_KT, CHUNK])
        w_hi = sb("w_hi", [P, LEAD, STEP_KT, CHUNK], F32R)
        w_lo = sb("w_lo", [P, LEAD, STEP_KT, CHUNK], F32R)
        gw = sb("gw", [P, GEMV_RING, D])
        acc = sb("acc", [P, D])
        vec_rows = sb("vec_rows", [P, 3, P])
        vecs = sb("vecs", [P, VECS])
        c_act = sb("c_act", [P, 2 * KT])
        mod = sb("mod", [P, MODS, KT])
        scales = sb("scales", [P, 4, KT])
        kv_shift = sb("kv_shift", [P, KT])
        qk_t = sb("qk_t", [P, 2, 4 * P])
        probs = sb("probs", [P, 4 * 384])
        probs_t = sb("probs_t", [P, 2, 4 * P])
        bias = sb("bias", [P, 2, TT * SEQ])
        neg_max = sb("neg_max", [P, 4, TT])
        den = sb("den", [P, 4, TT])
        rden = sb("rden", [P, 4, TT])
        stats = sb("stats", [P, TT, 4, 6])
        moments = sb("moments", [P, TT, 2])
        mean_sq = sb("mean_sq", [P, TT])
        rstd = sb("rstd", [P, TT])
        minus_half = sb("minus_half", [P, TT])
        forget = sb("forget", [P, TT * FOX_HEADS])
        w_forget = sb("w_forget", [P, KT, FOX_HEADS])
        wf_hi = sb("wf_hi", [P, KT, FOX_HEADS], F32R)
        wf_lo = sb("wf_lo", [P, KT, FOX_HEADS], F32R)
        ident = sb("ident", [P, P])
        ones = sb("ones", [P, 1])
        neg_upto = sb("neg_upto", [P, SEQ])
        subln = sb("subln", [P, WIDE])
        b_forget = sb("b_forget", [P, FOX_HEADS])
        decay = sb("decay", [P, 2 * RET_HEADS])
        ls = sb("ls", [P, 7, TT * FOX_HEADS])
        lam = sb("lam", [P, 8])
        side = sb("side", [P, 2, CHUNK])

        banks = [psum(f"bank{i}", [P, CHUNK]) for i in range(8)]
        acc_banks, t_bank, s_banks, o_bank = banks[0:4], banks[4], banks[5:7], banks[7]

        vecs_landed = sem("vecs_landed")
        smalls_landed = sem("smalls_landed")
        x_landed = sem("x_landed")
        raw_landed = [sem(f"raw_landed{i}") for i in range(SLOTS)]
        gw_landed = [sem(f"gw_landed{i}") for i in range(START_RING)]
        rows_landed = sem("rows_landed")
        bias_landed = [sem(f"bias_landed{i}") for i in range(2)]
        stored = sem("stored")
        hi_ready = sem("hi_ready")
        lo_ready = sem("lo_ready")
        half_used = sem("half_used")
        evacuated = sem("evacuated")
        gated = sem("gated")
        summed = sem("summed")
        measured = sem("measured")
        gemv_used = sem("gemv_used")
        t_ready = sem("t_ready")
        t_free = sem("t_free")
        turned = sem("turned")
        turned_hi = sem("turned_hi")
        turned_lo = sem("turned_lo")
        shifted = sem("shifted")
        scored = sem("scored")
        maxed = sem("maxed")
        exped = sem("exped")
        mixed = sem("mixed")
        weighed = sem("weighed")
        finished = sem("finished")
        dve_chain = sem("dve_chain")
        consts_ready = sem("consts_ready")
        forget_split = sem("forget_split")
        silu_ready = sem("silu_ready")
        xhat_ready = sem("xhat_ready")
        scales_ready = sem("scales_ready")
        sigmoid_to_act = sem("sigmoid_to_act")
        sigmoid_to_dve = sem("sigmoid_to_dve")
        lam_products = sem("lam_products")
        lam_exped = sem("lam_exped")
        decay_ready = sem("decay_ready")
        decay_exped = sem("decay_exped")
        decay_used = sem("decay_used")
        forget_ready = sem("forget_ready")
        normed = sem("normed")
        resid_ready = sem("resid_ready")
        var_ready = sem("var_ready")
        root_ready = sem("root_ready")

        def wait(eng, s, value):
            if isinstance(value, int) and value <= 0:
                return
            eng.wait_ge(s, value)

        def decay_table(h):
            return area[:, K, h // 2, 1024 + (h % 2) * 512:1024 + (h % 2) * 512 + 512]

        def q_cols(layer, u):
            if is_ret(layer, u):
                return 1024 + (u - DIL_HEADS) * WIDE
            return u * HEAD

        def k_src(layer, u, tt):
            if is_ret(layer, u):
                c = q_cols(layer, u) + HEAD
                return area[:, Q, tt, c:c + HEAD]
            return area[:, K, tt, u * HEAD:(u + 1) * HEAD]

        def head_cols(layer, u):
            if is_ret(layer, u):
                return 1024 + (u - DIL_HEADS) * WIDE, WIDE
            if layer == 1:
                return (u // 2) * WIDE, WIDE
            return u * HEAD, HEAD

        def prob_slot(layer, u):
            w = 384 if layer else 512
            s = u % 4 if layer else u % 3
            return probs[:, s * w:(s + 1) * w]

        def blocks(layer):
            return ((0, 256), (256, 512)) if layer == 0 else ((0, 128), (128, 384))

        def row_of(v):
            return v.rearrange("(a n) -> a n", a=1).broadcast_to([P, v.shape[0]])

        def gemv_slot(g):
            start = 2 * KT
            if g < start:
                slots = [gw[:, 0], gw[:, 1], area[:, V, 0], area[:, V, 1]]
                return slots[g % START_RING], gw_landed[g % START_RING], 16 * (g // START_RING + 1)
            n = start // START_RING + (g - start) // GEMV_RING + 1
            return gw[:, g % GEMV_RING], gw_landed[g % GEMV_RING], 16 * n

        def row_places(layer):
            return (area[:, Q, 0], area[:, Q, 1]) if layer == 1 else (area[:, K, 1], area[:, V, 0])

        def root_at(layer, s):
            u = s - 3
            return u if 0 <= u < UNITS[layer] and is_normed(layer, u) else None

        def steps_of(pair, half):
            for layer in range(3):
                at = half + PAIR_STEPS * (pair - ATTENTION_PAIR[layer])
                if at in STEP_AT:
                    return layer, STEP_AT[at]
            return None

        def by_depth(w):
            return w.rearrange("(k p) n -> p k n", p=P)

        w_in, w_out = by_depth(a["w_in"][0]), by_depth(a["w_out"][0])
        wa_in, wa_out = by_depth(a["a_w_in_2"][0]), by_depth(a["a_w_out_2"][0])
        w_kv, wb_in = by_depth(a["kv_w_2"]), by_depth(a["b_w_in_2"][0])
        wb_out = by_depth(a["b_w_out_2"][0])
        RUNS = [(w_in, 0, 6), (w_in, 4096, 4), (w_in, 3072, 2), (w_in, 6144, 2), (w_out, 0, 4),
                (wa_in, 0, 16), (wa_out, 0, 4), (w_kv, 0, 8), (wb_in, 0, 8), (wb_out, 0, 4)]
        MOD_SRC = ([(a["w_ada"][0], D * i) for i in range(3)] + [(a["w_mod_2"][0], D * i) for i in range(3)]
                   + [(a["kv_w_mod_2"], D * i) for i in range(2)]
                   + [(a["w_mod_2"][1], D * i) for i in range(3)])

        VEC_LOADS = 11

        block = ctx.enter_context(nc.Block())

        @block.sync
        def _(sp):
            sp.wait_ge(vecs_landed, 16 * VEC_LOADS)
            sp.dma_start(resid[:], a["x"][0].rearrange("(t p) d -> p t d", p=P)).then_inc(x_landed, 16)

            def load_chunk(src, col, before):
                for j in range(STEPS):
                    wait(sp, lo_ready, before + (j - SLOTS + 1))
                    sp.dma_start(raw[:, j % SLOTS], src[:, j * STEP_KT:(j + 1) * STEP_KT, bass.ds(col, CHUNK)]
                                 ).then_inc(raw_landed[j % SLOTS], 16)

            first = 0
            for n, (src, col, chunks) in enumerate(RUNS):
                start = 0
                if n == 0:
                    sp.wait_ge(gemv_used, 2 * KT - 7)
                    load_chunk(src, col, 0)
                    start = 1
                with sp.Fori(0, chunks - start) as i:
                    load_chunk(src, i * CHUNK + (col + start * CHUNK),
                               i * STEPS + STEPS * (first + start))
                first += chunks
            for tt in range(TT):
                sp.wait_ge(resid_ready, 2 * TT + tt + 1)
                sp.dma_start(out[0, tt * P:(tt + 1) * P, :], resid[:, tt]).then_inc(stored, 16)
            sp.wait_ge(stored, 16 * TT)

        @block.gpsimd
        def _(pool):
            pool.memset(minus_half[:], -0.5).then_inc(consts_ready, 1)

            def load(g):
                b, k = g // KT, g % KT
                src, col = MOD_SRC[b]
                dst, landed, _ = gemv_slot(g)
                wait(pool, gemv_used, g - (START_RING if g < 2 * KT else GEMV_RING) + 1)
                pool.dma_start(dst, src[k * P:(k + 1) * P, col:col + D]).then_inc(landed, 16)

            def inverse_root(key):
                n = ROOTS[key]
                pool.wait_ge(var_ready, n + 1)
                if n == 0:
                    pool.wait_ge(consts_ready, 2)
                nc.gpsimd.tensor_tensor(rstd[:], mean_sq[:], minus_half[:], ALU.pow).then_inc(root_ready, 1)

            def loads_after(pair):
                steps = gemv_steps(pair)
                for h in range(PAIR_STEPS):
                    for at, b, k in steps:
                        if h <= at < h + 1 and KT * b + k + GEMV_RING < MODS * KT:
                            load(KT * b + k + GEMV_RING)
                    if steps_of(pair, h):
                        layer, s = steps_of(pair, h)
                        if root_at(layer, s) is not None:
                            inverse_root(("head", layer, root_at(layer, s)))

            for g in range(KT + START_RING):
                load(g)
            inverse_root(("x",))
            for g in range(KT + START_RING, 2 * KT + GEMV_RING):
                load(g)
            for p in range(PAIRS):
                loads_after(p)
                if p - 1 in OUT_PAIR:
                    inverse_root(("norm", OUT_PAIR.index(p - 1)))

        @block.tensor
        def _(pe):
            def turn_vectors():
                pe.wait_ge(vecs_landed, 16 * VEC_LOADS)
                nc.tensor.transpose(t_bank[:, 0:96], vec_rows[0:96, 0, :], ident[0:96, 0:96])
                nc.tensor.transpose(t_bank[:, 96:VEC_FINAL], vec_rows[:, 1, :], ident[:])
                nc.tensor.transpose(t_bank[:, VEC_FINAL:VECS], vec_rows[0:48, 2, :], ident[0:48, 0:48]
                                    ).then_inc(t_ready, 1)

            def sum_mod(b):
                pe.wait_ge(gemv_used, KT * (b + 1))
                pe.wait_ge(t_free, T[("mod", b)])
                if b == 0:
                    pe.wait_ge(consts_ready, 2)
                for k in range(KT):
                    last = nc.tensor.matmul(t_bank[:, k:k + 1], acc[:, k * P:(k + 1) * P], ones[:],
                                            start=True, stop=True)
                last.then_inc(t_ready, 1)

            def spread_gate(layer, n):
                b = (ADA_GATE, A_GATE, B_GATE)[layer]
                pe.wait_ge(t_free, T[("gate", layer, n)])
                for k in range(4):
                    g = mod[:, b, 4 * n + k:4 * n + k + 1].broadcast_to([P, P])
                    last = nc.tensor.matmul(t_bank[:, k * P:(k + 1) * P], g, ident[:], start=True, stop=True)
                last.then_inc(t_ready, 1)

            def turn_round(m, src, r):
                wait(pe, turned_lo, TURNS * m + r - TURN_BANKS + 1 if r >= TURN_BANKS else TURNS * m)
                bank = banks[4 + r % TURN_BANKS]
                for k in range(2):
                    for tt in range(TT):
                        kt = 2 * r + k
                        last = nc.tensor.transpose(bank[:, k * SEQ + tt * P:k * SEQ + (tt + 1) * P],
                                                   src[:, tt, kt * P:(kt + 1) * P], ident[:])
                last.then_inc(turned, 1)

            def half(i, p0, c, j):
                if j == 0:
                    wait(pe, evacuated, i * 4 + (4 * p0 + 2 * c - 2))
                b = j % LEAD
                pe.wait_ge(lo_ready, i * 16 + (16 * p0 + STEPS * c + j + 1))
                for k in range(STEP_KT):
                    kt = STEP_KT * j + k
                    for tt in range(TT):
                        dst = acc_banks[2 * c + tt][:]
                        hi = act_hi[:, kt, tt * P:(tt + 1) * P]
                        lo = act_lo[:, kt, tt * P:(tt + 1) * P]
                        nc.tensor.matmul(dst, hi, w_hi[:, b, k], start=(kt == 0), stop=False)
                        nc.tensor.matmul(dst, hi, w_lo[:, b, k], start=False, stop=False)
                        last = nc.tensor.matmul(dst, lo, w_hi[:, b, k], start=False, stop=(kt == KT - 1))
                last.then_inc(half_used, 1)

            def pairs(p0, n):
                with pe.Fori(0, n) as i:
                    for c in range(2):
                        for j in range(STEPS):
                            half(i, p0, c, j)

            def turn_and_pair(m, src, t_used):
                p = TURN_PAIR[m]
                pe.wait_ge(t_free, t_used)
                for r in range(TURN_BANKS):
                    turn_round(m, src, r)
                for c in range(2):
                    for j in range(STEPS):
                        if c == 0:
                            pe.wait_ge(turned_hi, TURNS * m + j + 1)
                            pe.wait_ge(turned_lo, TURNS * m + j + 1)
                        half(0, p, c, j)
                        if c == 0 and j < 2:
                            turn_round(m, src, TURN_BANKS + 2 * j)
                            turn_round(m, src, TURN_BANKS + 2 * j + 1)
                        if p in OUT_PAIR and c == 0 and j >= 4:
                            spread_gate(OUT_PAIR.index(p), j - 4)

            def attention_pair(p):
                for h in range(PAIR_STEPS):
                    step = steps_of(p, h)
                    if step:
                        scores_step(*step)
                    half(0, p, h // STEPS, h % STEPS)
                    if step:
                        values_step(*step)

            def scores_step(layer, s):
                units, u0 = UNITS[layer], UNIT0[layer]
                if s < units:
                    u = s
                    pe.wait_ge(evacuated, 4 * (ATTENTION_PAIR[layer] + (layer == 2 and u >= 8)))
                    pe.wait_ge(t_free, T[("qk", layer, u)])
                    c = q_cols(layer, u)
                    for tt in range(TT):
                        nc.tensor.transpose(t_bank[:, tt * P:(tt + 1) * P], area[:, Q, tt, c:c + HEAD], ident[:])
                    for tt in range(TT):
                        last = nc.tensor.transpose(t_bank[:, SEQ + tt * P:SEQ + (tt + 1) * P],
                                                   k_src(layer, u, tt), ident[:])
                    last.then_inc(t_ready, 1)
                if 0 <= s - 1 < units:
                    u = s - 1
                    pe.wait_ge(t_free, T[("qk", layer, u)] + 1)
                    wait(pe, maxed, 2 * (u0 + u - 1) if u >= 2 else 2 * u0)
                    q, k = qk_t[:, u % 2, 0:SEQ], qk_t[:, u % 2, SEQ:2 * SEQ]
                    s_bank = s_banks[u % 2]
                    if is_ret(layer, u):
                        for j in range(TT):
                            last = nc.tensor.matmul(s_bank[:, j * SEQ:(j + 1) * SEQ], k[:, j * P:(j + 1) * P], q,
                                                    start=True, stop=True)
                    else:
                        for tt, (c0, c1) in enumerate(blocks(layer)):
                            last = nc.tensor.matmul(s_bank[:, c0:c1], q[:, tt * P:(tt + 1) * P], k[:, 0:c1 - c0],
                                                    start=True, stop=(layer != 2))
                            if layer == 2:
                                if u == 0 and tt == 0:
                                    pe.wait_ge(forget_ready, 1)
                                for j in range(tt + 1):
                                    f = forget[:, j * FOX_HEADS + u:j * FOX_HEADS + u + 1].broadcast_to([P, P])
                                    last = nc.tensor.matmul(s_bank[:, c0 + j * P:c1], f,
                                                            neg_upto[:, 0:c1 - c0 - j * P],
                                                            start=False, stop=(j == tt))
                    last.then_inc(scored, 1)

            def values_step(layer, s):
                units, u0, o0 = UNITS[layer], UNIT0[layer], OUT0[layer]
                if has_probs(layer, s - 2):
                    u = s - 2
                    pe.wait_ge(t_free, T[("probs", layer, u)])
                    if layer == 1:
                        pe.wait_ge(mixed, u // 2 + 1)
                    else:
                        pe.wait_ge(exped, 2 * (SOFT0[layer] + u + 1))
                    src = prob_slot(layer, u - 1 if layer == 1 else u)
                    for tt, (c0, c1) in enumerate(blocks(layer)):
                        for j in range((c1 - c0) // P):
                            at = j * SEQ + tt * P if layer == 0 else (tt if j == 0 else 2) * P
                            last = nc.tensor.transpose(t_bank[:, at:at + P], src[:, c0 + j * P:c0 + (j + 1) * P],
                                                       ident[:])
                    last.then_inc(t_ready, 1)
                if 0 <= s - 3 < units and out_of(layer, s - 3) is not None:
                    u = s - 3
                    h = out_of(layer, u)
                    c, w = head_cols(layer, u)
                    if layer == 1:
                        pe.wait_ge(evacuated, min(4 * 13 + 2 * (c // CHUNK + 1), 4 * 15))
                    elif is_ret(layer, u):
                        pe.wait_ge(evacuated, 4 * 5)
                    if is_ret(layer, u):
                        pe.wait_ge(maxed, 2 * (u0 + u + 1))
                        pt = prob_slot(layer, u)
                    else:
                        pe.wait_ge(t_free, T[("probs", layer, u)] + 1)
                        pt = probs_t[:, h % 2]
                    wait(pe, finished, o0 + h)
                    for tt in range(TT):
                        keys = TT if layer == 0 else tt + 1
                        for j in range(keys):
                            at = j * SEQ + tt * P if layer == 0 else (tt if j == 0 else 2) * P
                            last = nc.tensor.matmul(o_bank[:, tt * w:(tt + 1) * w], pt[:, at:at + P],
                                                    area[:, V, j, c:c + w], start=(j == 0), stop=(j == keys - 1))
                    last.then_inc(weighed, 1)

            def forget_scores():
                pe.wait_ge(forget_split, 2)
                pe.wait_ge(t_free, T[("forget",)])
                for tt in range(TT):
                    dst = t_bank[:, tt * FOX_HEADS:(tt + 1) * FOX_HEADS]
                    for kt in range(KT):
                        hi = act_hi[:, kt, tt * P:(tt + 1) * P]
                        nc.tensor.matmul(dst, hi, wf_hi[:, kt], start=(kt == 0), stop=False)
                        nc.tensor.matmul(dst, hi, wf_lo[:, kt], start=False, stop=False)
                        last = nc.tensor.matmul(dst, act_lo[:, kt, tt * P:(tt + 1) * P], wf_hi[:, kt],
                                                start=False, stop=(kt == KT - 1))
                last.then_inc(t_ready, 1)

            turn_vectors()
            sum_mod(ADA_SHIFT)
            sum_mod(ADA_SCALE)
            pe.wait_ge(xhat_ready, TT)
            turn_and_pair(0, area[:, Q], T[("mod", ADA_SCALE)] + 1)
            pairs(1, 2)
            sum_mod(ADA_GATE)
            pairs(3, 1)
            attention_pair(4)
            attention_pair(5)
            sum_mod(A_SHIFT)
            attention_pair(6)
            pe.wait_ge(gated, 8)
            turn_and_pair(1, area[:, Q], T[("gate", 0, 0)])
            pairs(8, 1)
            sum_mod(A_SCALE)
            pe.wait_ge(normed, TT)
            turn_and_pair(2, resid, T[("mod", A_SCALE)] + 1)
            pairs(10, 2)
            sum_mod(A_GATE)
            pairs(12, 2)
            attention_pair(14)
            sum_mod(KV_SHIFT)
            attention_pair(15)
            attention_pair(16)
            pe.wait_ge(gated, 16)
            turn_and_pair(3, area[:, Q], T[("gate", 1, 0)])
            sum_mod(KV_SCALE)
            pairs(18, 1)
            pe.wait_ge(normed, 2 * TT)
            turn_and_pair(4, resid, T[("mod", KV_SCALE)] + 1)
            sum_mod(B_SHIFT)
            pairs(20, 3)
            sum_mod(B_SCALE)
            forget_scores()
            pe.wait_ge(resid_ready, 2 * TT)
            turn_and_pair(5, resid, T[("forget",)] + 1)
            attention_pair(24)
            attention_pair(25)
            attention_pair(26)
            sum_mod(B_GATE)
            pe.wait_ge(gated, 24)
            turn_and_pair(6, area[:, Q], T[("mod", B_GATE)] + 1)
            pairs(28, 1)

        @block.scalar
        def _(act):
            act.dma_start(ident[:], a["t_ident"]).then_inc(vecs_landed, 16)
            for dst, src in ((vec_rows[0:16, 0], a["c"][0]), (vec_rows[16:32, 0], a["c_2"][0]),
                             (vec_rows[32:48, 0], a["norm_gain"][0]), (vec_rows[48:96, 0], a["b_ada"][0]),
                             (vec_rows[0:48, 1], a["b_mod_2"][0]), (vec_rows[48:80, 1], a["kv_b_mod_2"]),
                             (vec_rows[80:128, 1], a["b_mod_2"][1]), (vec_rows[0:16, 2], a["final_gain"]),
                             (vec_rows[16:32, 2], a["ln_g_2"][0]), (vec_rows[32:48, 2], a["ln_b_2"][0])):
                act.dma_start(dst, src.rearrange("(k p) -> k p", p=P)).then_inc(vecs_landed, 16)
            for dst, src in ((probs_t[:, 0], a["t_fwd"]), (probs_t[:, 1], a["t_bwd"]),
                             (neg_upto[:], a["t_neg_upto"]), (subln[:], row_of(a["a_subln_g_2"][0])),
                             (b_forget[:], row_of(a["kv_b_f_2"])),
                             (decay[:, 0:4], row_of(a["ret_decay_logit_f"][0])),
                             (decay[:, 4:8], row_of(a["ret_decay_logit_b"][0])),
                             (probs[:, 0:128], row_of(a["a_lam_q1_2"][0])),
                             (probs[:, 128:256], row_of(a["a_lam_q2_2"][0])),
                             (probs[:, 256:384], row_of(a["a_lam_k1_2"][0])),
                             (probs[:, 384:512], row_of(a["a_lam_k2_2"][0])),
                             (w_forget[:], w_kv[:, :, 2 * D:2 * D + FOX_HEADS]),
                             (bias[:, 0], a["t_dil"][0]), (bias[:, 1], a["t_dil"][1])):
                act.dma_start(dst, src).then_inc(smalls_landed, 16)

            def split_high(half, j, landed):
                b = j % LEAD
                act.wait_ge(raw_landed[j % SLOTS], landed)
                wait(act, half_used, half + (1 - LEAD))
                nc.scalar.copy(w_hi[:, b], raw[:, j % SLOTS]).then_inc(hi_ready, 1)

            def chunk_halves(i, scale, chunk, js):
                for j in js:
                    split_high(i * (STEPS * scale) + (STEPS * chunk + j), j,
                               i * (32 * scale) + 16 * (2 * chunk + j // SLOTS + 1))

            def keep(dst_of, scale):
                def copy_out(i, p0, c):
                    for tt in range(TT):
                        nc.scalar.activation(dst_of(i, p0, c, tt), acc_banks[2 * c + tt][:], ACT.Copy,
                                             scale=scale).then_inc(evacuated, 1)
                return copy_out

            def silu_gate(layer):
                def copy_out(i, p0, c):
                    for tt in range(TT):
                        wait(act, gated, i * 4 + (8 * layer + 4 * (p0 - GATE_PAIR[layer]) + 2 * c + tt - 1))
                        nc.scalar.activation(side[:, tt], acc_banks[2 * c + tt][:], ACT.Silu).then_inc(evacuated, 1)
                return copy_out

            def pair(i, p0, copy_out, last=False):
                for h in range(PAIR_STEPS):
                    c, j = h // STEPS, h % STEPS
                    static = isinstance(i, int)
                    step = steps_of(p0, h) if static else None
                    if step:
                        scores_step(*step)
                    if not (last and h >= PAIR_STEPS - LEAD):
                        chunk_halves(i, 2, 2 * p0 + (h + LEAD) // STEPS, [(h + LEAD) % STEPS])
                    if step:
                        values_step(*step)
                    if static and p0 in OUT_PAIR and 4 <= h < 8:
                        gate_row(OUT_PAIR.index(p0), h - 4)
                    if copy_out and j == STEPS - 1:
                        act.wait_ge(half_used, i * 16 + (16 * p0 + h + 1))
                        copy_out(i, p0, c)

            def turn_plain(m):
                for r in range(TURNS):
                    act.wait_ge(turned, TURNS * m + r + 1)
                    nc.scalar.copy(act_hi[:, 2 * r:2 * r + 2], banks[4 + r % TURN_BANKS][:].rearrange(
                        "p (k t) -> p k t", k=2)).then_inc(turned_hi, 1)

            def turn_scaled(m, n, shift):
                act.wait_ge(scales_ready, n + 1)
                for r in range(TURNS):
                    act.wait_ge(turned, TURNS * m + r + 1)
                    for k in range(2):
                        kt = 2 * r + k
                        last = nc.scalar.activation(act_hi[:, kt], banks[4 + r % TURN_BANKS][:, k * SEQ:(k + 1) * SEQ],
                                                    ACT.Identity, scale=scales[:, n, kt:kt + 1],
                                                    bias=shift[:, kt:kt + 1])
                    last.then_inc(turned_hi, 1)

            def gate_row(layer, n):
                act.wait_ge(t_ready, T[("gate", layer, n)] + 1)
                nc.scalar.copy(area[:, K, 0, n * CHUNK:(n + 1) * CHUNK], t_bank[:]).then_inc(t_free, 1)

            def norm_rows(layer):
                gain, shift = row_places(layer)
                if layer == 1:
                    act.wait_ge(turned, TURNS * 4)
                else:
                    act.wait_ge(weighed, OUT0[layer] + OUTS[layer])
                act.dma_start(gain, row_of(a["final_gain"] if layer == 0 else a["ln_g_2"][layer - 1])
                              ).then_inc(rows_landed, 16)
                if layer:
                    act.dma_start(shift, row_of(a["ln_b_2"][layer - 1])).then_inc(rows_landed, 16)

            def scores_step(layer, s):
                units, u0, o0 = UNITS[layer], UNIT0[layer], OUT0[layer]
                if s < units:
                    u = s
                    act.wait_ge(t_ready, T[("qk", layer, u)] + 1)
                    wait(act, scored, u0 + u - 1 if u >= 2 else u0)
                    nc.scalar.copy(qk_t[:, u % 2], t_bank[:]).then_inc(t_free, 1)
                if 0 <= s - 1 < units and not is_ret(layer, s - 1):
                    u = s - 1
                    p = prob_slot(layer, u)
                    act.wait_ge(maxed, 2 * (u0 + u + 1))
                    if layer == 1:
                        wait(act, mixed, (u - 2) // 2 if u >= 4 else 0)
                    elif u >= 4:
                        act.wait_ge(finished, o0 + u - 3)
                    for tt, (c0, c1) in enumerate(blocks(layer)):
                        nc.scalar.activation(p[:, c0:c1], p[:, c0:c1], ACT.Exp, scale=-1.0,
                                             bias=neg_max[:, u % 4, tt:tt + 1],
                                             accum_out=den[:, u % 4, tt:tt + 1]).then_inc(exped, 1)
                    if layer == 0 and u + 2 < DIL_HEADS:
                        act.dma_start(bias[:, u % 2], a["t_dil"][u + 2]).then_inc(bias_landed[u % 2], 16)
                    if layer == 1 and u % 2 and u // 2 + 2 < DIFF_HEADS:
                        act.dma_start(bias[:, u // 2 % 2, 0:384], a["t_diff"][u // 2 + 2]
                                      ).then_inc(bias_landed[u // 2 % 2], 16)

            def values_step(layer, s):
                if has_probs(layer, s - 2):
                    u = s - 2
                    h, o0 = out_of(layer, u), OUT0[layer]
                    w = 512 if layer == 0 else 384
                    act.wait_ge(t_ready, T[("probs", layer, u)] + 1)
                    wait(act, weighed, o0 + h - 1 if h >= 2 else o0)
                    nc.scalar.copy(probs_t[:, h % 2, 0:w], t_bank[:, 0:w]).then_inc(t_free, 1)

            def first_bias(layer):
                act.wait_ge(maxed, 2 * (UNIT0[layer - 1] + UNITS[layer - 1]))
                if layer == 1:
                    for i in range(2):
                        act.dma_start(bias[:, i, 0:384], a["t_diff"][i]).then_inc(bias_landed[i], 16)
                else:
                    act.dma_start(bias[:, 0, 0:384], a["t_causal"]).then_inc(bias_landed[0], 16)

            def log_sigmoid(n, cols):
                act.wait_ge(sigmoid_to_act, 2 * n + 1)
                nc.scalar.activation(ls[:, 2, 0:cols], ls[:, 1, 0:cols], ACT.Exp).then_inc(sigmoid_to_dve, 1)
                act.wait_ge(sigmoid_to_act, 2 * n + 2)
                nc.scalar.activation(ls[:, 4, 0:cols], ls[:, 3, 0:cols], ACT.Ln).then_inc(sigmoid_to_dve, 1)

            act.wait_ge(t_free, T[("vec",)] + 1)
            nc.scalar.activation(c_act[:], vecs[:, 0:2 * KT], ACT.Silu).then_inc(silu_ready, 1)
            log_sigmoid(0, 2 * RET_HEADS)
            act.wait_ge(lam_products, 2)
            nc.scalar.activation(lam[:, 2:4], lam[:, 0:2], ACT.Exp).then_inc(lam_exped, 1)
            act.wait_ge(decay_ready, 1)
            for h in range(RET_HEADS):
                wait(act, decay_used, h)
                nc.scalar.activation(side[:, 0], probs_t[:, 0], ACT.Exp, scale=decay[:, h:h + 1])
                nc.scalar.activation(side[:, 1], probs_t[:, 1], ACT.Exp,
                                     scale=decay[:, 4 + h:5 + h]).then_inc(decay_exped, 1)
            act.wait_ge(root_ready, 1)
            act.wait_ge(x_landed, 16)
            for tt in range(TT):
                nc.scalar.activation(area[:, Q, tt], resid[:, tt], ACT.Copy, scale=rstd[:, tt:tt + 1]
                                     ).then_inc(xhat_ready, 1)
            chunk_halves(0, 1, 0, range(LEAD))
            turn_scaled(0, 0, mod[:, ADA_SHIFT])

            def keep_at(which, first, scale=1.0, col=0):
                return keep(lambda i, p0, c, tt: area[:, which, tt, bass.ds(
                    i * (2 * CHUNK) + (col + (2 * (p0 - first) + c) * CHUNK), CHUNK)], scale)

            ret_qk = area[:, Q, :, 1024:2048].rearrange("p t (h c e) -> p t c h e", c=2, e=HEAD)

            def keep_ret(i, p0, c):
                for tt in range(TT):
                    nc.scalar.activation(ret_qk[:, tt, c], acc_banks[2 * c + tt][:].rearrange(
                        "p (h e) -> p h e", e=HEAD), ACT.Copy, scale=QK_SCALE if c else 1.0).then_inc(evacuated, 1)

            def two_pairs(p0, copy_out):
                with act.Fori(0, 2) as i:
                    pair(i, p0, copy_out)

            pair(0, 0, keep_at(Q, 0, QK_SCALE))
            pair(0, 1, keep_at(K, 1))
            pair(0, 2, keep_at(V, 2))
            pair(0, 3, keep_ret)
            pair(0, 4, keep_at(V, 4, col=1024))
            pair(0, 5, silu_gate(0))
            pair(0, 6, silu_gate(0))
            norm_rows(0)
            first_bias(1)
            turn_plain(1)
            pair(0, 7, None)
            pair(0, 8, None)
            turn_scaled(2, 1, mod[:, A_SHIFT])
            two_pairs(9, keep_at(Q, 9, QK_SCALE))
            two_pairs(11, keep_at(K, 11))
            pair(0, 13, keep_at(V, 13))
            pair(0, 14, keep_at(V, 13))
            pair(0, 15, silu_gate(1))
            pair(0, 16, silu_gate(1))
            first_bias(2)
            turn_plain(3)
            norm_rows(1)
            pair(0, 17, None)
            pair(0, 18, None)
            turn_scaled(4, 2, kv_shift[:])
            two_pairs(19, keep_at(K, 19))
            two_pairs(21, keep_at(V, 21))
            log_sigmoid(1, TT * FOX_HEADS)
            turn_scaled(5, 3, mod[:, B_SHIFT])
            pair(0, 23, keep_at(Q, 23, QK_SCALE))
            pair(0, 24, keep_at(Q, 23, QK_SCALE))
            pair(0, 25, silu_gate(2))
            pair(0, 26, silu_gate(2))
            norm_rows(2)
            turn_plain(6)
            pair(0, 27, None)
            pair(0, 28, None, last=True)

        @block.vector
        def _(dve):
            chain = [0]

            def link(ins):
                chain[0] += 1
                ins.then_inc(dve_chain, 1)
                dve.wait_ge(dve_chain, chain[0])

            def chunk_halves(i, scale, chunk, js):
                for j in js:
                    dve.wait_ge(hi_ready, i * (STEPS * scale) + (STEPS * chunk + j + 1))
                    nc.vector.tensor_tensor(w_lo[:, j % LEAD], raw[:, j % SLOTS],
                                            w_hi[:, j % LEAD].bitcast(F32), ALU.subtract).then_inc(lo_ready, 1)

            def gemv_step(b, k):
                g = KT * b + k
                w, landed, count = gemv_slot(g)
                cc = c_act[:, (0 if b <= ADA_GATE else KT) + k:(0 if b <= ADA_GATE else KT) + k + 1]
                dve.wait_ge(landed, count)
                if k == 0:
                    nc.vector.tensor_scalar(acc[:], w, cc, None, ALU.mult).then_inc(gemv_used, 1)
                else:
                    dve.wait_ge(gemv_used, g)
                    nc.vector.scalar_tensor_tensor(out=acc[:], in0=w, scalar=cc, in1=acc[:],
                                                   op0=ALU.mult, op1=ALU.add).then_inc(gemv_used, 1)

            def finish_mod(b):
                dve.wait_ge(t_ready, T[("mod", b)] + 1)
                nc.vector.tensor_tensor(mod[:, b], t_bank[:, 0:KT], vecs[:, VEC_BIAS + KT * b:VEC_BIAS + KT * (b + 1)],
                                        ALU.add).then_inc(t_free, 1)

            def gate_y(layer):
                heads = ((4, 8, 10, 12), (2, 4, 6, 8), (4, 8, 12, 16))[layer]

                def take(i, p0, c):
                    p1 = p0 - GATE_PAIR[layer]
                    dve.wait_ge(finished, OUT0[layer] + heads[2 * p1 + c])
                    for tt in range(TT):
                        y = area[:, Q, tt, bass.ds(i * (2 * CHUNK) + (2 * p1 + c) * CHUNK, CHUNK)]
                        dve.wait_ge(evacuated, i * 4 + (4 * p0 + 2 * c + tt + 1))
                        nc.vector.tensor_tensor(y, y, side[:, tt], ALU.mult).then_inc(gated, 1)
                return take

            def add_out(layer):
                first = OUT_PAIR[layer]
                alpha = 1.0 if layer == 0 else DN_ALPHA

                def take(i, p0, c):
                    col = i * (2 * CHUNK) + (2 * (p0 - first) + c) * CHUNK
                    dve.wait_ge(half_used, i * 16 + (16 * p0 + STEPS * (c + 1)))
                    dve.wait_ge(t_free, T[("gate", layer, 2 * (p0 - first) + c)] + 1)
                    for tt in range(TT):
                        nc.vector.tensor_tensor(side[:, tt], acc_banks[2 * c + tt][:], area[:, K, 0, bass.ds(col, CHUNK)],
                                                ALU.mult).then_inc(evacuated, 1)
                    for tt in range(TT):
                        x = resid[:, tt, bass.ds(col, CHUNK)]
                        dve.wait_ge(evacuated, i * 4 + (4 * p0 + 2 * c + tt + 1))
                        nc.vector.scalar_tensor_tensor(out=x, in0=x, scalar=alpha, in1=side[:, tt], op0=ALU.mult,
                                                       op1=ALU.add).then_inc(summed, 1)
                    for tt in range(TT):
                        dve.wait_ge(summed, i * 4 + (8 * layer + 4 * (p0 - first) + 2 * c + tt + 1))
                        nc.vector.bn_stats(stats[:, tt, 2 * (p0 - first) + c],
                                           resid[:, tt, bass.ds(col, CHUNK)]).then_inc(measured, 1)
                return take

            def pair(p, take=None, last=False):
                gemv = gemv_steps(p)
                for h in range(PAIR_STEPS):
                    if h == finish_half(p):
                        finish_mod(SUM_AFTER[p - 1])
                    step = steps_of(p, h)
                    if step:
                        scores_step(*step)
                    if not (last and h >= PAIR_STEPS - LEAD):
                        chunk_halves(0, 2, 2 * p + (h + LEAD) // STEPS, [(h + LEAD) % STEPS])
                    for at, b, k in gemv:
                        if h <= at < h + 1:
                            gemv_step(b, k)
                    if step:
                        values_step(*step)
                    if take and h % STEPS == STEPS - 1:
                        take(0, p, h // STEPS)

            def turn_scaled(m, n, shift, scale):
                gain = {0: VEC_GAIN, 1: VEC_FINAL, 2: VEC_LN_G}.get(n)
                if n == 2:
                    b = vecs[:, VEC_LN_B:VEC_LN_B + KT]
                    link(nc.vector.scalar_tensor_tensor(out=kv_shift[:], in0=mod[:, scale], scalar=1.0, in1=b,
                                                        op0=ALU.add, op1=ALU.mult))
                    link(nc.vector.tensor_tensor(kv_shift[:], kv_shift[:], shift, ALU.add))
                    shift = kv_shift[:]
                if gain is None:
                    nc.vector.tensor_scalar(scales[:, n], mod[:, scale], 1.0, None, ALU.add).then_inc(scales_ready, 1)
                else:
                    nc.vector.scalar_tensor_tensor(out=scales[:, n], in0=mod[:, scale], scalar=1.0,
                                                   in1=vecs[:, gain:gain + KT], op0=ALU.add, op1=ALU.mult
                                                   ).then_inc(scales_ready, 1)
                dve.wait_ge(scales_ready, n + 1)
                for r in range(TURNS):
                    dve.wait_ge(turned_hi, TURNS * m + r + 1)
                    for k in range(2):
                        kt = 2 * r + k
                        nc.vector.tensor_scalar(side[:, r % 2, k * SEQ:(k + 1) * SEQ],
                                                banks[4 + r % TURN_BANKS][:, k * SEQ:(k + 1) * SEQ],
                                                scales[:, n, kt:kt + 1], shift[:, kt:kt + 1], ALU.mult, ALU.add
                                                ).then_inc(shifted, 1)
                    dve.wait_ge(shifted, 2 * (TURNS * n + r + 1))
                    nc.vector.tensor_tensor(act_lo[:, 2 * r:2 * r + 2], side[:, r % 2].rearrange("p (k t) -> p k t", k=2),
                                            act_hi[:, 2 * r:2 * r + 2].bitcast(F32), ALU.subtract).then_inc(turned_lo, 1)

            def turn_plain(m):
                for r in range(TURNS):
                    dve.wait_ge(turned_hi, TURNS * m + r + 1)
                    nc.vector.tensor_tensor(act_lo[:, 2 * r:2 * r + 2],
                                            banks[4 + r % TURN_BANKS][:].rearrange("p (k t) -> p k t", k=2),
                                            act_hi[:, 2 * r:2 * r + 2].bitcast(F32), ALU.subtract).then_inc(turned_lo, 1)

            def root_mean_square(key, eps):
                link(nc.vector.tensor_tensor(mean_sq[:], moments[:, :, 0], moments[:, :, 0], ALU.mult))
                nc.vector.scalar_tensor_tensor(out=mean_sq[:], in0=mean_sq[:], scalar=eps, in1=moments[:, :, 1],
                                               op0=ALU.add, op1=ALU.add).then_inc(var_ready, 1)

            def norm(layer):
                dve.wait_ge(measured, 4 * TT * (layer + 1))
                nc.vector.bn_aggr(moments[:, 0], stats[:, 0])
                link(nc.vector.bn_aggr(moments[:, 1], stats[:, 1]))
                if layer == 0:
                    root_mean_square(("norm", layer), NORM_EPS)
                else:
                    nc.vector.tensor_scalar(mean_sq[:], moments[:, :, 1], EPS, None, ALU.add).then_inc(var_ready, 1)
                dve.wait_ge(root_ready, ROOTS[("norm", layer)] + 1)
                for tt in range(TT):
                    x, r = resid[:, tt], rstd[:, tt:tt + 1]
                    if layer == 0:
                        nc.vector.tensor_scalar(x, x, r, None, ALU.mult).then_inc(normed, 1)
                    else:
                        nc.vector.tensor_scalar(x, x, moments[:, tt, 0:1], r, ALU.subtract, ALU.mult
                                                ).then_inc(normed, 1)

            def norm_row(layer, tt):
                gain, shift = row_places(layer)
                x = resid[:, tt]
                dve.wait_ge(rows_landed, 16 * (1, 3, 5)[layer])
                dve.wait_ge(normed, TT * layer + tt + 1)
                if layer == 0:
                    nc.vector.tensor_tensor(x, x, gain, ALU.mult).then_inc(resid_ready, 1)
                else:
                    link(nc.vector.tensor_tensor(x, x, gain, ALU.mult))
                    nc.vector.tensor_tensor(x, x, shift, ALU.add).then_inc(resid_ready, 1)

            def finish_normed(layer, u):
                c, w = head_cols(layer, u)
                dve.wait_ge(root_ready, ROOTS[("head", layer, u)] + 1)
                for tt in range(TT):
                    o, y, r = o_bank[:, tt * w:(tt + 1) * w], area[:, Q, tt, c:c + w], rstd[:, tt:tt + 1]
                    if layer == 1:
                        last = nc.vector.scalar_tensor_tensor(out=y, in0=o, scalar=r, in1=subln[:], op0=ALU.mult,
                                                              op1=ALU.mult)
                    else:
                        last = nc.vector.tensor_scalar(y, o, r, None, ALU.mult)
                last.then_inc(finished, 1)

            def values_step(layer, s):
                u = s - 3
                if not 0 <= u < UNITS[layer] or out_of(layer, u) is None:
                    return
                c, w = head_cols(layer, u)
                dve.wait_ge(weighed, OUT0[layer] + out_of(layer, u) + 1)
                o = [o_bank[:, tt * w:(tt + 1) * w] for tt in range(TT)]
                if is_normed(layer, u):
                    nc.vector.bn_stats(stats[:, 0, 0], o[0])
                    link(nc.vector.bn_stats(stats[:, 1, 0], o[1]))
                    nc.vector.bn_aggr(moments[:, 0], stats[:, 0, 0])
                    link(nc.vector.bn_aggr(moments[:, 1], stats[:, 1, 0]))
                    root_mean_square(("head", layer, u), EPS if layer == 1 else NORM_EPS)
                else:
                    for tt in range(TT):
                        last = nc.vector.tensor_scalar(area[:, Q, tt, c:c + w], o[tt], rden[:, u % 4, tt:tt + 1],
                                                       None, ALU.mult)
                    last.then_inc(finished, 1)

            def scores_step(layer, s):
                units, u0 = UNITS[layer], UNIT0[layer]
                if 0 <= s - 4 < units and is_normed(layer, s - 4):
                    finish_normed(layer, s - 4)
                if 0 <= s - 1 < units:
                    u = s - 1
                    dve.wait_ge(scored, u0 + u + 1)
                    s_bank, p = s_banks[u % 2], prob_slot(layer, u)
                    if layer == 0 and u >= 3:
                        if is_ret(layer, u - 3):
                            dve.wait_ge(weighed, OUT0[layer] + u - 2)
                        else:
                            dve.wait_ge(t_ready, T[("probs", layer, u - 3)] + 1)
                    if layer == 1 and u >= 4:
                        dve.wait_ge(t_ready, T[("probs", layer, (u - 4) | 1)] + 1)
                    if layer == 2 and u >= 4:
                        dve.wait_ge(t_ready, T[("probs", layer, u - 4)] + 1)
                    if is_ret(layer, u):
                        nc.vector.tensor_tensor(p, s_bank[:], decay_table(u - DIL_HEADS), ALU.mult).then_inc(maxed, 2)
                    else:
                        if layer == 0:
                            if u >= 2:
                                dve.wait_ge(bias_landed[u % 2], 16 * (u // 2))
                            b = bias[:, u % 2]
                        elif layer == 1:
                            h = u // 2
                            dve.wait_ge(bias_landed[h % 2], 16 * (DIL_HEADS // 2 - 1 + h // 2 + 1))
                            b = bias[:, h % 2]
                        else:
                            dve.wait_ge(bias_landed[0], 16 * (DIL_HEADS // 2 - 1 + DIFF_HEADS // 2 + 1))
                            b = bias[:, 0]
                        for tt, (c0, c1) in enumerate(blocks(layer)):
                            nc.vector.tensor_tensor_reduce(
                                out=p[:, c0:c1], in0=s_bank[:, c0:c1], in1=b[:, c0:c1], scale=-1.0, scalar=FLT_MAX,
                                op0=ALU.add, op1=ALU.min, accum_out=neg_max[:, u % 4, tt:tt + 1]).then_inc(maxed, 1)
                if 0 <= s - 2 < units and not is_ret(layer, s - 2):
                    u = s - 2
                    dve.wait_ge(exped, 2 * (SOFT0[layer] + u + 1))
                    if layer != 1:
                        link(nc.vector.reciprocal(rden[:, u % 4], den[:, u % 4]))
                    elif u % 2:
                        p0, p1 = prob_slot(layer, u - 1), prob_slot(layer, u)
                        link(nc.vector.reciprocal(rden[:, u % 4 - 1:u % 4 + 1], den[:, u % 4 - 1:u % 4 + 1]))
                        nc.vector.tensor_scalar(p0[:, 0:P], p0[:, 0:P], rden[:, u % 4 - 1, 0:1], None, ALU.mult)
                        nc.vector.tensor_scalar(p0[:, P:384], p0[:, P:384], rden[:, u % 4 - 1, 1:2], None, ALU.mult)
                        link(nc.vector.tensor_scalar(rden[:, u % 4], rden[:, u % 4], lam[:, 4:5], None, ALU.mult))
                        for tt, (c0, c1) in enumerate(blocks(layer)):
                            last = nc.vector.scalar_tensor_tensor(
                                out=p0[:, c0:c1], in0=p1[:, c0:c1], scalar=rden[:, u % 4, tt:tt + 1],
                                in1=p0[:, c0:c1], op0=ALU.mult, op1=ALU.add)
                        last.then_inc(mixed, 1)

            def log_sigmoid(n, cols, dst):
                z, nz, e, w, l, d, one = (ls[:, k, 0:cols] for k in range(7))
                nc.vector.scalar_tensor_tensor(out=nz, in0=z, scalar=-1.0, in1=z, op0=ALU.mult,
                                               op1=ALU.min).then_inc(sigmoid_to_act, 1)
                dve.wait_ge(sigmoid_to_dve, 2 * n + 1)
                nc.vector.tensor_scalar(w, e, 1.0, None, ALU.add).then_inc(sigmoid_to_act, 1)
                dve.wait_ge(sigmoid_to_act, 2 * n + 2)
                link(nc.vector.tensor_scalar(d, w, -1.0, None, ALU.add))
                link(nc.vector.tensor_scalar(one, d, 0.0, None, ALU.is_equal))
                link(nc.vector.tensor_tensor(d, d, one, ALU.add))
                link(nc.vector.reciprocal(d, d))
                link(nc.vector.tensor_tensor(d, d, e, ALU.mult))
                dve.wait_ge(sigmoid_to_dve, 2 * n + 2)
                link(nc.vector.tensor_tensor(l, l, one, ALU.add))
                link(nc.vector.tensor_tensor(d, d, l, ALU.mult))
                return nc.vector.scalar_tensor_tensor(out=dst, in0=z, scalar=0.0, in1=d, op0=ALU.min, op1=ALU.subtract)

            nc.vector.memset(ones[:], 1.0).then_inc(consts_ready, 1)
            dve.wait_ge(t_ready, T[("vec",)] + 1)
            nc.vector.tensor_copy(vecs[:], t_bank[:, 0:VECS]).then_inc(t_free, 1)
            dve.wait_ge(smalls_landed, 16 * 14)
            link(nc.vector.tensor_copy(ls[:, 0, 0:2 * RET_HEADS], decay[:]))
            link(log_sigmoid(0, 2 * RET_HEADS, decay[:]))
            nc.vector.tensor_scalar(decay[:], decay[:], -1e-20, None, ALU.min).then_inc(decay_ready, 1)
            for n in range(2):
                nc.vector.tensor_tensor_reduce(
                    out=ls[:].rearrange("p a b -> p (a b)")[:, 0:HEAD], in0=probs[:, n * HEAD:(n + 1) * HEAD],
                    in1=probs[:, (2 + n) * HEAD:(3 + n) * HEAD], scale=1.0, scalar=0.0, op0=ALU.mult, op1=ALU.add,
                    accum_out=lam[:, n:n + 1]).then_inc(lam_products, 1)
                dve.wait_ge(lam_products, n + 1)
            dve.wait_ge(lam_exped, 1)
            link(nc.vector.scalar_tensor_tensor(out=lam[:, 4:5], in0=lam[:, 3:4], scalar=LAM_INIT, in1=lam[:, 2:3],
                                                op0=ALU.subtract, op1=ALU.subtract))
            link(nc.vector.tensor_scalar(subln[:], subln[:], 1.0 - LAM_INIT, None, ALU.mult))
            for h in range(RET_HEADS):
                dve.wait_ge(decay_exped, h + 1)
                nc.vector.tensor_tensor(decay_table(h), side[:, 0], side[:, 1], ALU.add).then_inc(decay_used, 1)
            dve.wait_ge(silu_ready, 1)
            for k in range(KT):
                gemv_step(ADA_SHIFT, k)
            finish_mod(ADA_SHIFT)
            dve.wait_ge(x_landed, 16)
            for tt in range(TT):
                for n in range(D // CHUNK):
                    link(nc.vector.bn_stats(stats[:, tt, n], resid[:, tt, n * CHUNK:(n + 1) * CHUNK]))
                link(nc.vector.bn_aggr(moments[:, tt], stats[:, tt]))
            root_mean_square(("x",), NORM_EPS)
            for k in range(KT):
                gemv_step(ADA_SCALE, k)
            nc.vector.tensor_copy(wf_hi[:], w_forget[:]).then_inc(forget_split, 1)
            dve.wait_ge(forget_split, 1)
            nc.vector.tensor_tensor(wf_lo[:], w_forget[:], wf_hi[:].bitcast(F32), ALU.subtract
                                    ).then_inc(forget_split, 1)
            finish_mod(ADA_SCALE)
            dve.wait_ge(t_free, T[("mod", ADA_SCALE)] + 1)
            chunk_halves(0, 1, 0, range(LEAD))
            turn_scaled(0, 0, mod[:, ADA_SHIFT], ADA_SCALE)
            for p in range(5):
                pair(p)
            pair(5, gate_y(0))
            pair(6, gate_y(0))
            turn_plain(1)
            pair(7, add_out(0))
            pair(8, add_out(0))
            finish_mod(A_SCALE)
            norm(0)
            dve.wait_ge(t_free, T[("mod", A_SCALE)] + 1)
            turn_scaled(2, 1, mod[:, A_SHIFT], A_SCALE)
            for tt in range(TT):
                norm_row(0, tt)
            for p in range(9, 15):
                pair(p)
            pair(15, gate_y(1))
            pair(16, gate_y(1))
            turn_plain(3)
            pair(17, add_out(1))
            pair(18, add_out(1))
            norm(1)
            turn_scaled(4, 2, mod[:, KV_SHIFT], KV_SCALE)
            pair(19)
            for tt in range(TT):
                norm_row(1, tt)
            for p in range(20, 23):
                pair(p)
            finish_mod(B_SCALE)
            dve.wait_ge(t_ready, T[("forget",)] + 1)
            for tt in range(TT):
                last = nc.vector.tensor_tensor(ls[:, 0, tt * FOX_HEADS:(tt + 1) * FOX_HEADS],
                                               t_bank[:, tt * FOX_HEADS:(tt + 1) * FOX_HEADS], b_forget[:], ALU.add)
            last.then_inc(t_free, 1)
            dve.wait_ge(t_free, T[("forget",)] + 1)
            log_sigmoid(1, TT * FOX_HEADS, forget[:]).then_inc(forget_ready, 1)
            turn_scaled(5, 3, mod[:, B_SHIFT], B_SCALE)
            pair(23)
            pair(24)
            pair(25, gate_y(2))
            pair(26, gate_y(2))
            finish_mod(B_GATE)
            turn_plain(6)
            pair(27, add_out(2))
            pair(28, add_out(2), last=True)
            norm(2)
            for tt in range(TT):
                norm_row(2, tt)


INPUTS = ["x", "c", "norm_gain", "w_ada", "b_ada", "w_in", "w_out", "ret_decay_logit_f", "ret_decay_logit_b",
          "final_gain", "c_2", "w_mod_2", "b_mod_2", "ln_g_2", "ln_b_2", "a_w_in_2", "a_w_out_2", "a_lam_q1_2",
          "a_lam_k1_2", "a_lam_q2_2", "a_lam_k2_2", "a_subln_g_2", "kv_w_mod_2", "kv_b_mod_2", "kv_w_2", "kv_b_f_2",
          "b_w_in_2", "b_w_out_2"]


def kernel(**inputs):
    import concourse.bacc as bacc
    from concourse.bass_utils import run_bass_kernel_spmd as run

    nc = bacc.Bacc("TRN2", target_bir_lowering=False, num_devices=1)
    arrays = {name: np.ascontiguousarray(inputs[name]) for name in INPUTS}
    arrays.update(shape_tables())
    aps = {name: nc.dram_tensor(f"in_{name}", v.shape, mybir.dt.from_np(v.dtype), kind="ExternalInput").ap()
           for name, v in arrays.items()}
    out = nc.dram_tensor("out_0", (1, SEQ, D), F32, kind="ExternalOutput").ap()
    two_blocks(nc, aps, out)
    r = run(nc, [{f"in_{k}": v for k, v in arrays.items()}], core_ids=[0])
    return r.results[0]["out_0"]
```

```python
import math
from contextlib import ExitStack

import numpy as np

import concourse.bass as bass
from concourse import mybir

F32 = mybir.dt.float32
F32R = mybir.dt.float32r
ALU = mybir.AluOpType
ACT = mybir.ActivationFunctionType

P = 128
D = 2048
SEQ = 256
TT = SEQ // P
KT = D // P
CHUNK = 512
STEP_KT = 2
STEPS = KT // STEP_KT
SLOTS = 4
LEAD = 4
GEMV_RING = 2
TURN_BANKS = 4
TURNS = KT // 2

DIL_HEADS = 8
RET_HEADS = 4
DIFF_HEADS = 8
FOX_HEADS = 16
HEAD = 128
WIDE = 256
QK_SCALE = HEAD ** -0.5
DILATIONS = ((128, 1), (512, 4), (2048, 16))
NEG = -1e30
FLT_MAX = 3e38
NORM_EPS = 1e-6
EPS = 1e-5
LAM_INIT = 0.8 - 0.6 * math.exp(-0.3 * 0)
DN_ALPHA = (2.0 * 2) ** 0.25

(ADA_SHIFT, ADA_SCALE, ADA_GATE, A_SHIFT, A_SCALE, A_GATE, KV_SHIFT, KV_SCALE, B_SHIFT, B_SCALE,
 B_GATE) = range(11)
MODS = 11
PAIRS = 29
GROUPS = 4
GROUP_SLOTS = 8
GROUP_KT = KT // GROUPS
MOD_STEPS = {ADA_GATE: ((1, 5), (2, 5), (3, 6)), A_SHIFT: ((4, 8), (5, 8)),
             A_SCALE: ((6, 7), (7, 6), (8, 3)), A_GATE: ((9, 4), (10, 6), (11, 6)),
             KV_SHIFT: ((12, 5), (13, 6), (14, 5)), KV_SCALE: ((15, 8), (16, 8)),
             B_SHIFT: ((17, 6), (18, 4), (19, 6)), B_SCALE: ((20, 5), (21, 6), (22, 5)),
             B_GATE: ((23, 4), (24, 4), (25, 4), (26, 4))}
SUM_AFTER = {steps[-1][0]: b for b, steps in MOD_STEPS.items()}
PAIR_STEPS = 2 * STEPS
STEP_HALVES = (2, 5, 8, 11, 14, 17, 20, 23, 24, 26, 28, 30, 32, 34, 36, 38, 40, 42, 44, 46)
STEP_AT = {h: s for s, h in enumerate(STEP_HALVES)}
ATTENTION_PAIR = (4, 14, 24)
GATE_PAIR = (5, 15, 25)
OUT_PAIR = (7, 17, 27)
TURN_PAIR = (0, 7, 9, 17, 19, 23, 27)
FORGET_PAIR = 22
FORGET_COPY, FORGET_TURN, FORGET_SIGMOID = 4, 6, 11
NORM_ROW_AT = {(10, 3): (0, 0), (10, 10): (0, 1), (20, 3): (1, 0), (20, 10): (1, 1)}
DECAYS_AT, LAMBDA_AT = (1, 3), (1, 8)
DECAY_TABLE_AT = {(2, 2): 0, (2, 5): 1, (2, 8): 2, (2, 11): 3}
START_STEPS = [(c, 2 * q + j) for q in range(GROUPS) for c in range(2) for j in range(2)]
START_RING = 4

VEC_C, VEC_GAIN, VEC_BIAS = 0, 2 * KT, 3 * KT
VEC_FINAL = VEC_BIAS + MODS * KT
VEC_LN_G, VEC_LN_B = VEC_FINAL + KT, VEC_FINAL + 2 * KT
VECS = VEC_FINAL + 3 * KT


def finish_half(pair):
    if pair - 1 not in SUM_AFTER or pair in TURN_PAIR:
        return None
    return 0 if any(0 <= pair - p < 3 for p in ATTENTION_PAIR) else LEAD


def gemv_steps(pair):
    for b, steps in MOD_STEPS.items():
        k = 0
        for p, n in steps:
            if p == pair:
                first = (finish_half(pair) or 0) + 1
                return [(first + i * ((14 - first) / n), b, k + i) for i in range(n)]
            k += n
    return []


def alibi(n):
    return [2.0 ** (-8.0 * (h + 1) / n) for h in range(n)]


def shape_tables():
    t = np.arange(SEQ)
    rel = t[:, None] - t[None, :]
    dist = np.abs(rel).astype(np.float64)
    seen = np.zeros((SEQ, SEQ))
    for window, dilation in DILATIONS:
        seen += (rel % dilation == 0) & (dist <= (window // (2 * dilation)) * dilation)
    log_seen = np.where(seen > 0, np.log(np.maximum(seen, 1)), NEG)

    def by_tile(a):
        return a.reshape(TT, P, SEQ).transpose(1, 0, 2)

    def causal_blocks(a):
        b = by_tile(a)
        return np.concatenate([b[:, 0, :P], b[:, 1, :]], axis=1)

    dil = np.stack([by_tile(np.where(seen > 0, -s * dist + log_seen, NEG)).reshape(P, -1)
                    for s in alibi(DIL_HEADS)])
    diff = np.stack([causal_blocks(np.where(rel >= 0, -s * dist, NEG)) for s in alibi(DIFF_HEADS)])
    causal = causal_blocks(np.where(rel >= 0, 0.0, NEG))
    q_minus_k = t[None, :] - t[:, None]
    fwd = by_tile(np.where(q_minus_k >= 0, q_minus_k, 1e30)).reshape(P, -1)
    bwd = by_tile(np.where(q_minus_k <= 0, -q_minus_k, 1e30)).reshape(P, -1)
    p = np.arange(P)
    neg_upto = -(p[:, None] <= t[None, :]).astype(np.float64)
    out = {"t_ident": np.eye(P), "t_dil": dil, "t_diff": diff, "t_causal": causal, "t_fwd": fwd,
           "t_bwd": bwd, "t_neg_upto": neg_upto}
    return {k: np.ascontiguousarray(v, dtype=np.float32) for k, v in out.items()}


def t_uses(units, has_probs):
    uses = [("vec",)] + [("start", q) for q in range(GROUPS)]
    for pair in range(PAIRS):
        for h in range(PAIR_STEPS):
            for layer in range(3):
                at = h + PAIR_STEPS * (pair - ATTENTION_PAIR[layer])
                if at in STEP_AT:
                    s = STEP_AT[at]
                    if s < units[layer]:
                        uses.append(("qk", layer, s))
                    if has_probs(layer, s - 2):
                        uses.append(("probs", layer, s - 2))
                if pair == OUT_PAIR[layer] and h < 4:
                    uses.append(("gate", layer, h))
        if pair == FORGET_PAIR:
            uses += [("forget_rows",), ("forget",)]
        if pair in SUM_AFTER:
            uses.append(("mod", SUM_AFTER[pair]))
    return {u: n for n, u in enumerate(uses)}


def two_blocks(nc, a, out):
    UNITS = [DIL_HEADS + RET_HEADS, 2 * DIFF_HEADS, FOX_HEADS]
    UNIT0 = [0, UNITS[0], UNITS[0] + UNITS[1]]
    SOFT = [DIL_HEADS, UNITS[1], UNITS[2]]
    SOFT0 = [0, SOFT[0], SOFT[0] + SOFT[1]]
    OUTS = [UNITS[0], DIFF_HEADS, FOX_HEADS]
    OUT0 = [0, OUTS[0], OUTS[0] + OUTS[1]]

    def out_of(layer, u):
        if layer == 1:
            return u // 2 if u % 2 else None
        return u

    def is_ret(layer, u):
        return layer == 0 and u >= DIL_HEADS

    def is_normed(layer, u):
        return is_ret(layer, u) or (layer == 1 and u % 2 == 1)

    def has_probs(layer, u):
        return 0 <= u < UNITS[layer] and not is_ret(layer, u) and (layer != 1 or u % 2 == 1)

    T = t_uses(UNITS, has_probs)

    ROOTS = [("x",)]
    for layer in range(3):
        ROOTS += [("head", layer, u) for u in range(UNITS[layer]) if is_normed(layer, u)]
        ROOTS.append(("norm", layer))
    HEAD_ROOTS = {key: n for n, key in enumerate(k for k in ROOTS if k[0] == "head")}
    NORM_ROOTS = {key: n for n, key in enumerate(k for k in ROOTS if k[0] != "head")}
    ROOTS = {key: n for n, key in enumerate(ROOTS)}

    with ExitStack() as ctx:
        def sb(name, shape, dt=F32):
            return ctx.enter_context(nc.sbuf_tensor(name, shape, dt))

        def psum(name, shape):
            return ctx.enter_context(nc.psum_tensor(name, shape, F32))

        def sem(name):
            return ctx.enter_context(nc.semaphore(name))

        resid = sb("resid", [P, TT, D])
        act_hi = sb("act_hi", [P, KT, SEQ], F32R)
        act_lo = sb("act_lo", [P, KT, SEQ], F32R)
        area = sb("area", [P, 3, TT, D])
        Q, K, V = 0, 1, 2
        raw = sb("raw", [P, SLOTS, STEP_KT, CHUNK])
        w_hi = sb("w_hi", [P, LEAD, STEP_KT, CHUNK], F32R)
        w_lo = sb("w_lo", [P, LEAD, STEP_KT, CHUNK], F32R)
        gw = sb("gw", [P, GEMV_RING, D])
        acc = sb("acc", [P, D])
        vec_rows = sb("vec_rows", [P, 3, P])
        vecs = sb("vecs", [P, VECS])
        c_act = sb("c_act", [P, 2 * KT])
        mod = sb("mod", [P, MODS, KT])
        scales = sb("scales", [P, 4, KT])
        kv_shift = sb("kv_shift", [P, KT])
        qk_t = sb("qk_t", [P, 2, 4 * P])
        probs = sb("probs", [P, 4 * 384])
        probs_t = sb("probs_t", [P, 2, 4 * P])
        bias = sb("bias", [P, 2, TT * SEQ])
        neg_max = sb("neg_max", [P, 4, TT])
        den = sb("den", [P, 4, TT])
        rden = sb("rden", [P, 4, TT])
        stats = sb("stats", [P, TT, 4, 6])
        moments = sb("moments", [P, TT, 2])
        mean_sq = sb("mean_sq", [P, TT])
        square_sums = sb("square_sums", [P, TT])
        squares = sb("squares", [P, TT, WIDE])
        rstd = sb("rstd", [P, TT])
        minus_half = sb("minus_half", [P, TT])
        forget = sb("forget", [P, TT * FOX_HEADS])
        w_forget = sb("w_forget", [P, KT, FOX_HEADS])
        wf_hi = sb("wf_hi", [P, KT, FOX_HEADS], F32R)
        wf_lo = sb("wf_lo", [P, KT, FOX_HEADS], F32R)
        ident = sb("ident", [P, P])
        ones = sb("ones", [P, 1])
        neg_upto = sb("neg_upto", [P, SEQ])
        subln = sb("subln", [P, WIDE])
        b_forget = sb("b_forget", [P, FOX_HEADS])
        decay = sb("decay", [P, 2 * RET_HEADS])
        ls = sb("ls", [P, 7, TT * FOX_HEADS])
        lam = sb("lam", [P, 8])
        side = sb("side", [P, 2, CHUNK])

        banks = [psum(f"bank{i}", [P, CHUNK]) for i in range(8)]
        acc_banks, t_bank, s_banks, o_bank = banks[0:4], banks[4], banks[5:7], banks[7]

        vecs_landed = sem("vecs_landed")
        smalls_landed = sem("smalls_landed")
        x_landed = sem("x_landed")
        raw_landed = [sem(f"raw_landed{i}") for i in range(SLOTS)]
        gw_landed = [sem(f"gw_landed{i}") for i in range(START_RING)]
        rows_landed = sem("rows_landed")
        bias_landed = [sem(f"bias_landed{i}") for i in range(2)]
        stored = sem("stored")
        hi_ready = sem("hi_ready")
        lo_ready = sem("lo_ready")
        half_used = sem("half_used")
        evacuated = sem("evacuated")
        gated = sem("gated")
        summed = sem("summed")
        measured = sem("measured")
        gemv_used = sem("gemv_used")
        t_ready = sem("t_ready")
        t_free = sem("t_free")
        turned = sem("turned")
        turned_hi = sem("turned_hi")
        turned_lo = sem("turned_lo")
        shifted = sem("shifted")
        scored = sem("scored")
        maxed = sem("maxed")
        exped = sem("exped")
        mixed = sem("mixed")
        weighed = sem("weighed")
        finished = sem("finished")
        dve_chain = sem("dve_chain")
        consts_ready = sem("consts_ready")
        forget_split = sem("forget_split")
        forget_copied = sem("forget_copied")
        silu_ready = sem("silu_ready")
        xhat_ready = sem("xhat_ready")
        scales_ready = sem("scales_ready")
        sigmoid_to_act = sem("sigmoid_to_act")
        sigmoid_to_dve = sem("sigmoid_to_dve")
        lam_products = sem("lam_products")
        lam_exped = sem("lam_exped")
        decay_ready = sem("decay_ready")
        decay_exped = sem("decay_exped")
        decay_used = sem("decay_used")
        forget_ready = sem("forget_ready")
        normed = sem("normed")
        resid_ready = sem("resid_ready")
        var_ready = sem("var_ready")
        root_ready = sem("root_ready")
        squared = sem("squared")
        meaned = sem("meaned")

        def wait(eng, s, value):
            if isinstance(value, int) and value <= 0:
                return
            eng.wait_ge(s, value)

        def decay_table(h):
            return area[:, K, h // 2, 1024 + (h % 2) * 512:1024 + (h % 2) * 512 + 512]

        def q_cols(layer, u):
            if is_ret(layer, u):
                return 1024 + (u - DIL_HEADS) * WIDE
            return u * HEAD

        def k_src(layer, u, tt):
            if is_ret(layer, u):
                c = q_cols(layer, u) + HEAD
                return area[:, Q, tt, c:c + HEAD]
            return area[:, K, tt, u * HEAD:(u + 1) * HEAD]

        def head_cols(layer, u):
            if is_ret(layer, u):
                return 1024 + (u - DIL_HEADS) * WIDE, WIDE
            if layer == 1:
                return (u // 2) * WIDE, WIDE
            return u * HEAD, HEAD

        def prob_slot(layer, u):
            w = 384 if layer else 512
            s = u % 4 if layer else u % 3
            return probs[:, s * w:(s + 1) * w]

        def blocks(layer):
            return ((0, 256), (256, 512)) if layer == 0 else ((0, 128), (128, 384))

        def row_of(v):
            return v.rearrange("(a n) -> a n", a=1).broadcast_to([P, v.shape[0]])

        def gemv_slot(g):
            start = 2 * KT
            if g < start:
                slots = [gw[:, 0], gw[:, 1], area[:, V, 0], area[:, V, 1]]
                return slots[g % START_RING], gw_landed[g % START_RING], 32 * (g // START_RING + 1)
            n = 2 * start // START_RING + (g - start) // GEMV_RING + 1
            return gw[:, g % GEMV_RING], gw_landed[g % GEMV_RING], 16 * n

        def turn_bank(m, r):
            return banks[5 + r % 2] if m == 0 else banks[4 + r % TURN_BANKS]

        def group_acc(q):
            return acc[:, (q % 2) * 2 * CHUNK:(q % 2 + 1) * 2 * CHUNK]

        def row_places(layer):
            return (area[:, Q, 0], area[:, Q, 1]) if layer == 1 else (area[:, K, 1], area[:, V, 0])

        def root_at(layer, s):
            u = s - 3
            return u if 0 <= u < UNITS[layer] and is_normed(layer, u) else None

        def steps_of(pair, half):
            for layer in range(3):
                at = half + PAIR_STEPS * (pair - ATTENTION_PAIR[layer])
                if at in STEP_AT:
                    return layer, STEP_AT[at]
            return None

        def by_depth(w):
            return w.rearrange("(k p) n -> p k n", p=P)

        w_ada = a["w_ada"][0].rearrange("(k p) (b n) -> p k b n", p=P, n=D)
        w_in, w_out = by_depth(a["w_in"][0]), by_depth(a["w_out"][0])
        wa_in, wa_out = by_depth(a["a_w_in_2"][0]), by_depth(a["a_w_out_2"][0])
        w_kv, wb_in = by_depth(a["kv_w_2"]), by_depth(a["b_w_in_2"][0])
        wb_out = by_depth(a["b_w_out_2"][0])
        RUNS = [(w_in, 0, 6), (w_in, 4096, 4), (w_in, 3072, 2), (w_in, 6144, 2), (w_out, 0, 4),
                (wa_in, 0, 16), (wa_out, 0, 4), (w_kv, 0, 8), (wb_in, 0, 8), (wb_out, 0, 4)]
        MOD_SRC = ([(a["w_ada"][0], D * i) for i in range(3)] + [(a["w_mod_2"][0], D * i) for i in range(3)]
                   + [(a["kv_w_mod_2"], D * i) for i in range(2)]
                   + [(a["w_mod_2"][1], D * i) for i in range(3)])

        VEC_LOADS = 11

        block = ctx.enter_context(nc.Block())

        @block.sync
        def _(sp):
            sp.wait_ge(vecs_landed, 16 * VEC_LOADS)
            sp.dma_start(resid[:], a["x"][0].rearrange("(t p) d -> p t d", p=P)).then_inc(x_landed, 16)

            def load_chunk(src, col, before):
                for j in range(STEPS):
                    wait(sp, lo_ready, before + (j - SLOTS + 1))
                    sp.dma_start(raw[:, j % SLOTS], src[:, j * STEP_KT:(j + 1) * STEP_KT, bass.ds(col, CHUNK)]
                                 ).then_inc(raw_landed[j % SLOTS], 16)

            first = 0
            for n, (src, col, chunks) in enumerate(RUNS):
                start = 0
                if n == 0:
                    for k, (c, j) in enumerate(START_STEPS):
                        sp.wait_ge(gemv_used, GROUP_SLOTS * (k // 4) + 4)
                        wait(sp, lo_ready, k - SLOTS + 1)
                        sp.dma_start(raw[:, k % SLOTS], src[:, j * STEP_KT:(j + 1) * STEP_KT,
                                                            c * CHUNK:(c + 1) * CHUNK]
                                     ).then_inc(raw_landed[k % SLOTS], 16)
                    start = 2
                with sp.Fori(0, chunks - start) as i:
                    load_chunk(src, i * CHUNK + (col + start * CHUNK),
                               i * STEPS + STEPS * (first + start))
                first += chunks
            for n in range(2 * TT):
                tt, cols = n // 2, slice(n % 2 * D // 2, (n % 2 + 1) * D // 2)
                sp.wait_ge(resid_ready, 2 * TT + n + 1)
                sp.dma_start(out[0, tt * P:(tt + 1) * P, cols], resid[:, tt, cols]).then_inc(stored, 16)
            sp.wait_ge(stored, 16 * 2 * TT)

        @block.gpsimd
        def _(pool):
            pool.memset(minus_half[:], -0.5).then_inc(consts_ready, 1)

            def load(g):
                dst, landed, _ = gemv_slot(g)
                wait(pool, gemv_used, g - (START_RING if g < 2 * KT else GEMV_RING) + 1)
                if g < 2 * KT:
                    q, i = g // GROUP_SLOTS, g % GROUP_SLOTS
                    for b in range(2):
                        pool.dma_start(dst.rearrange("p (k b n) -> p b k n", k=2, b=2)[:, b],
                                       w_ada[:, 2 * i:2 * i + 2, b, CHUNK * q:CHUNK * (q + 1)]
                                       ).then_inc(landed, 16)
                else:
                    b, k = g // KT, g % KT
                    src, col = MOD_SRC[b]
                    pool.dma_start(dst, src[k * P:(k + 1) * P, col:col + D]).then_inc(landed, 16)

            def inverse_root(key):
                if key[0] == "head":
                    _, layer, u = key
                    n = HEAD_ROOTS[key]
                    pool.wait_ge(squared, TT * (n + 1))
                    nc.gpsimd.tensor_scalar(mean_sq[:], square_sums[:], 1.0 / WIDE, EPS if layer == 1 else NORM_EPS,
                                            ALU.mult, ALU.add).then_inc(meaned, 1)
                    pool.wait_ge(meaned, n + 1)
                else:
                    n = NORM_ROOTS[key]
                    pool.wait_ge(var_ready, n + 1)
                    if n == 0:
                        pool.wait_ge(consts_ready, 2)
                nc.gpsimd.tensor_tensor(rstd[:], mean_sq[:], minus_half[:], ALU.pow).then_inc(root_ready, 1)

            def loads_after(pair):
                steps = gemv_steps(pair)
                for h in range(PAIR_STEPS):
                    for at, b, k in steps:
                        if h <= at < h + 1 and KT * b + k + GEMV_RING < MODS * KT:
                            load(KT * b + k + GEMV_RING)
                    if steps_of(pair, h):
                        layer, s = steps_of(pair, h)
                        if root_at(layer, s) is not None:
                            inverse_root(("head", layer, root_at(layer, s)))

            for g in range(START_RING + 2):
                load(g)
            inverse_root(("x",))
            for g in range(START_RING + 2, 2 * KT + GEMV_RING):
                load(g)
            for p in range(PAIRS):
                loads_after(p)
                if p - 1 in OUT_PAIR:
                    inverse_root(("norm", OUT_PAIR.index(p - 1)))

        @block.tensor
        def _(pe):
            def turn_vectors():
                pe.wait_ge(vecs_landed, 16 * VEC_LOADS)
                nc.tensor.transpose(t_bank[:, 0:96], vec_rows[0:96, 0, :], ident[0:96, 0:96])
                nc.tensor.transpose(t_bank[:, 96:VEC_FINAL], vec_rows[:, 1, :], ident[:])
                nc.tensor.transpose(t_bank[:, VEC_FINAL:VECS], vec_rows[0:48, 2, :], ident[0:48, 0:48]
                                    ).then_inc(t_ready, 1)

            def sum_group(q):
                pe.wait_ge(gemv_used, GROUP_SLOTS * (q + 1))
                pe.wait_ge(t_free, T[("start", q)])
                for k in range(2 * GROUP_KT):
                    last = nc.tensor.matmul(t_bank[:, k:k + 1], group_acc(q)[:, k * P:(k + 1) * P], ones[:],
                                            start=True, stop=True)
                last.then_inc(t_ready, 1)

            def start():
                pe.wait_ge(consts_ready, 2)
                for q in range(GROUPS):
                    pe.wait_ge(xhat_ready, TT)
                    for n in range(2):
                        turn_round(0, area[:, Q], 2 * q + n)
                    sum_group(q)
                    for n in range(4 * q, 4 * q + 4):
                        c, j = START_STEPS[n]
                        pe.wait_ge(turned_hi, j + 1)
                        pe.wait_ge(turned_lo, j + 1)
                        pe.wait_ge(lo_ready, n + 1)
                        products(c, j, n % LEAD)

            def sum_mod(b):
                pe.wait_ge(gemv_used, KT * (b + 1))
                pe.wait_ge(t_free, T[("mod", b)])
                for k in range(KT):
                    last = nc.tensor.matmul(t_bank[:, k:k + 1], acc[:, k * P:(k + 1) * P], ones[:],
                                            start=True, stop=True)
                last.then_inc(t_ready, 1)

            def spread_gate(layer, n):
                b = (ADA_GATE, A_GATE, B_GATE)[layer]
                pe.wait_ge(t_free, T[("gate", layer, n)])
                for k in range(4):
                    g = mod[:, b, 4 * n + k:4 * n + k + 1].broadcast_to([P, P])
                    last = nc.tensor.matmul(t_bank[:, k * P:(k + 1) * P], g, ident[:], start=True, stop=True)
                last.then_inc(t_ready, 1)

            def turn_round(m, src, r):
                turns = TURN_BANKS if m else 2
                wait(pe, turned_lo, TURNS * m + r - turns + 1 if r >= turns else TURNS * m)
                bank = turn_bank(m, r)
                for k in range(2):
                    for tt in range(TT):
                        kt = 2 * r + k
                        last = nc.tensor.transpose(bank[:, k * SEQ + tt * P:k * SEQ + (tt + 1) * P],
                                                   src[:, tt, kt * P:(kt + 1) * P], ident[:])
                last.then_inc(turned, 1)

            def half(i, p0, c, j):
                if j == 0:
                    wait(pe, evacuated, i * 4 + (4 * p0 + 2 * c - 2))
                pe.wait_ge(lo_ready, i * 16 + (16 * p0 + STEPS * c + j + 1))
                products(c, j, j % LEAD)

            def products(c, j, b):
                for k in range(STEP_KT):
                    kt = STEP_KT * j + k
                    for tt in range(TT):
                        dst = acc_banks[2 * c + tt][:]
                        hi = act_hi[:, kt, tt * P:(tt + 1) * P]
                        lo = act_lo[:, kt, tt * P:(tt + 1) * P]
                        nc.tensor.matmul(dst, hi, w_hi[:, b, k], start=(kt == 0), stop=False)
                        nc.tensor.matmul(dst, hi, w_lo[:, b, k], start=False, stop=False)
                        last = nc.tensor.matmul(dst, lo, w_hi[:, b, k], start=False, stop=(kt == KT - 1))
                last.then_inc(half_used, 1)

            def pairs(p0, n):
                with pe.Fori(0, n) as i:
                    for c in range(2):
                        for j in range(STEPS):
                            half(i, p0, c, j)

            def turn_and_pair(m, src, t_used):
                p = TURN_PAIR[m]
                pe.wait_ge(t_free, t_used)
                for r in range(TURN_BANKS):
                    turn_round(m, src, r)
                for c in range(2):
                    for j in range(STEPS):
                        if c == 0:
                            pe.wait_ge(turned_hi, TURNS * m + j + 1)
                            pe.wait_ge(turned_lo, TURNS * m + j + 1)
                        half(0, p, c, j)
                        if c == 0 and j < 2:
                            turn_round(m, src, TURN_BANKS + 2 * j)
                            turn_round(m, src, TURN_BANKS + 2 * j + 1)
                        if p in OUT_PAIR and c == 0 and j >= 4:
                            spread_gate(OUT_PAIR.index(p), j - 4)

            def attention_pair(p):
                for h in range(PAIR_STEPS):
                    step = steps_of(p, h)
                    if step:
                        scores_step(*step)
                    half(0, p, h // STEPS, h % STEPS)
                    if step:
                        values_step(*step)

            def scores_step(layer, s):
                units, u0 = UNITS[layer], UNIT0[layer]
                if s < units:
                    u = s
                    pe.wait_ge(evacuated, 4 * (ATTENTION_PAIR[layer] + (layer == 2 and u >= 8)))
                    pe.wait_ge(t_free, T[("qk", layer, u)])
                    c = q_cols(layer, u)
                    for tt in range(TT):
                        nc.tensor.transpose(t_bank[:, tt * P:(tt + 1) * P], area[:, Q, tt, c:c + HEAD], ident[:])
                    for tt in range(TT):
                        last = nc.tensor.transpose(t_bank[:, SEQ + tt * P:SEQ + (tt + 1) * P],
                                                   k_src(layer, u, tt), ident[:])
                    last.then_inc(t_ready, 1)
                if 0 <= s - 1 < units:
                    u = s - 1
                    pe.wait_ge(t_free, T[("qk", layer, u)] + 1)
                    wait(pe, maxed, 2 * (u0 + u - 1) if u >= 2 else 2 * u0)
                    q, k = qk_t[:, u % 2, 0:SEQ], qk_t[:, u % 2, SEQ:2 * SEQ]
                    s_bank = s_banks[u % 2]
                    if is_ret(layer, u):
                        for j in range(TT):
                            last = nc.tensor.matmul(s_bank[:, j * SEQ:(j + 1) * SEQ], k[:, j * P:(j + 1) * P], q,
                                                    start=True, stop=True)
                    else:
                        for tt, (c0, c1) in enumerate(blocks(layer)):
                            last = nc.tensor.matmul(s_bank[:, c0:c1], q[:, tt * P:(tt + 1) * P], k[:, 0:c1 - c0],
                                                    start=True, stop=(layer != 2))
                            if layer == 2:
                                if u == 0 and tt == 0:
                                    pe.wait_ge(forget_ready, 1)
                                for j in range(tt + 1):
                                    f = forget[:, j * FOX_HEADS + u:j * FOX_HEADS + u + 1].broadcast_to([P, P])
                                    last = nc.tensor.matmul(s_bank[:, c0 + j * P:c1], f,
                                                            neg_upto[:, 0:c1 - c0 - j * P],
                                                            start=False, stop=(j == tt))
                    last.then_inc(scored, 1)

            def values_step(layer, s):
                units, u0, o0 = UNITS[layer], UNIT0[layer], OUT0[layer]
                if has_probs(layer, s - 2):
                    u = s - 2
                    pe.wait_ge(t_free, T[("probs", layer, u)])
                    if layer == 1:
                        pe.wait_ge(mixed, u // 2 + 1)
                    else:
                        pe.wait_ge(exped, 2 * (SOFT0[layer] + u + 1))
                    src = prob_slot(layer, u - 1 if layer == 1 else u)
                    for tt, (c0, c1) in enumerate(blocks(layer)):
                        for j in range((c1 - c0) // P):
                            at = j * SEQ + tt * P if layer == 0 else (tt if j == 0 else 2) * P
                            last = nc.tensor.transpose(t_bank[:, at:at + P], src[:, c0 + j * P:c0 + (j + 1) * P],
                                                       ident[:])
                    last.then_inc(t_ready, 1)
                if 0 <= s - 3 < units and out_of(layer, s - 3) is not None:
                    u = s - 3
                    h = out_of(layer, u)
                    c, w = head_cols(layer, u)
                    if layer == 1:
                        pe.wait_ge(evacuated, min(4 * 13 + 2 * (c // CHUNK + 1), 4 * 15))
                    elif is_ret(layer, u):
                        pe.wait_ge(evacuated, 4 * 5)
                    if is_ret(layer, u):
                        pe.wait_ge(maxed, 2 * (u0 + u + 1))
                        pt = prob_slot(layer, u)
                    else:
                        pe.wait_ge(t_free, T[("probs", layer, u)] + 1)
                        pt = probs_t[:, h % 2]
                    wait(pe, finished, o0 + h)
                    for tt in range(TT):
                        keys = TT if layer == 0 else tt + 1
                        for j in range(keys):
                            at = j * SEQ + tt * P if layer == 0 else (tt if j == 0 else 2) * P
                            last = nc.tensor.matmul(o_bank[:, tt * w:(tt + 1) * w], pt[:, at:at + P],
                                                    area[:, V, j, c:c + w], start=(j == 0), stop=(j == keys - 1))
                    last.then_inc(weighed, 1)

            def forget_scores():
                pe.wait_ge(forget_split, 2)
                pe.wait_ge(t_free, T[("forget_rows",)])
                dst = t_bank[0:FOX_HEADS, 0:SEQ]
                for kt in range(KT):
                    nc.tensor.matmul(dst, wf_hi[:, kt], act_hi[:, kt], start=(kt == 0), stop=False)
                    nc.tensor.matmul(dst, wf_lo[:, kt], act_hi[:, kt], start=False, stop=False)
                    last = nc.tensor.matmul(dst, wf_hi[:, kt], act_lo[:, kt], start=False, stop=(kt == KT - 1))
                last.then_inc(t_ready, 1)

            def forget_turn():
                pe.wait_ge(forget_copied, 1)
                pe.wait_ge(t_free, T[("forget",)])
                for tt in range(TT):
                    last = nc.tensor.transpose(t_bank[:, tt * FOX_HEADS:(tt + 1) * FOX_HEADS],
                                               side[0:FOX_HEADS, 0, tt * P:(tt + 1) * P],
                                               ident[0:FOX_HEADS, 0:FOX_HEADS])
                last.then_inc(t_ready, 1)

            def forget_pair():
                forget_scores()
                for h in range(PAIR_STEPS):
                    half(0, FORGET_PAIR, h // STEPS, h % STEPS)
                    if h == FORGET_TURN:
                        forget_turn()

            turn_vectors()
            start()
            pairs(1, 3)
            sum_mod(ADA_GATE)
            attention_pair(4)
            attention_pair(5)
            sum_mod(A_SHIFT)
            attention_pair(6)
            pe.wait_ge(gated, 8)
            turn_and_pair(1, area[:, Q], T[("gate", 0, 0)])
            pairs(8, 1)
            sum_mod(A_SCALE)
            pe.wait_ge(normed, TT)
            turn_and_pair(2, resid, T[("mod", A_SCALE)] + 1)
            pairs(10, 2)
            sum_mod(A_GATE)
            pairs(12, 2)
            attention_pair(14)
            sum_mod(KV_SHIFT)
            attention_pair(15)
            attention_pair(16)
            sum_mod(KV_SCALE)
            pe.wait_ge(gated, 16)
            turn_and_pair(3, area[:, Q], T[("mod", KV_SCALE)] + 1)
            pairs(18, 1)
            pe.wait_ge(normed, 2 * TT)
            turn_and_pair(4, resid, T[("gate", 1, 3)] + 1)
            sum_mod(B_SHIFT)
            pairs(20, 2)
            forget_pair()
            sum_mod(B_SCALE)
            pe.wait_ge(resid_ready, 2 * TT)
            turn_and_pair(5, resid, T[("mod", B_SCALE)] + 1)
            attention_pair(24)
            attention_pair(25)
            attention_pair(26)
            sum_mod(B_GATE)
            pe.wait_ge(gated, 24)
            turn_and_pair(6, area[:, Q], T[("mod", B_GATE)] + 1)
            pairs(28, 1)

        @block.scalar
        def _(act):
            act.dma_start(ident[:], a["t_ident"]).then_inc(vecs_landed, 16)
            for dst, src in ((vec_rows[0:16, 0], a["c"][0]), (vec_rows[16:32, 0], a["c_2"][0]),
                             (vec_rows[32:48, 0], a["norm_gain"][0]), (vec_rows[48:96, 0], a["b_ada"][0]),
                             (vec_rows[0:48, 1], a["b_mod_2"][0]), (vec_rows[48:80, 1], a["kv_b_mod_2"]),
                             (vec_rows[80:128, 1], a["b_mod_2"][1]), (vec_rows[0:16, 2], a["final_gain"]),
                             (vec_rows[16:32, 2], a["ln_g_2"][0]), (vec_rows[32:48, 2], a["ln_b_2"][0])):
                act.dma_start(dst, src.rearrange("(k p) -> k p", p=P)).then_inc(vecs_landed, 16)
            for dst, src in ((probs_t[:, 0], a["t_fwd"]), (probs_t[:, 1], a["t_bwd"]),
                             (neg_upto[:], a["t_neg_upto"]), (subln[:], row_of(a["a_subln_g_2"][0])),
                             (b_forget[:], row_of(a["kv_b_f_2"])),
                             (decay[:, 0:4], row_of(a["ret_decay_logit_f"][0])),
                             (decay[:, 4:8], row_of(a["ret_decay_logit_b"][0])),
                             (probs[:, 0:128], row_of(a["a_lam_q1_2"][0])),
                             (probs[:, 128:256], row_of(a["a_lam_q2_2"][0])),
                             (probs[:, 256:384], row_of(a["a_lam_k1_2"][0])),
                             (probs[:, 384:512], row_of(a["a_lam_k2_2"][0])),
                             (w_forget[:], w_kv[:, :, 2 * D:2 * D + FOX_HEADS]),
                             (bias[:, 0], a["t_dil"][0]), (bias[:, 1], a["t_dil"][1])):
                act.dma_start(dst, src).then_inc(smalls_landed, 16)

            def split_high(half, j, landed):
                b = j % LEAD
                act.wait_ge(raw_landed[j % SLOTS], landed)
                wait(act, half_used, half + (1 - LEAD))
                nc.scalar.copy(w_hi[:, b], raw[:, j % SLOTS]).then_inc(hi_ready, 1)

            def chunk_halves(i, scale, chunk, js):
                for j in js:
                    split_high(i * (STEPS * scale) + (STEPS * chunk + j), j,
                               i * (32 * scale) + 16 * (2 * chunk + j // SLOTS + 1))

            def decay_powers(n):
                act.wait_ge(decay_ready, 1)
                act.wait_ge(turned_lo, TURNS)
                wait(act, decay_used, n)
                nc.scalar.activation(side[:, 0], probs_t[:, 0], ACT.Exp, scale=decay[:, n:n + 1])
                nc.scalar.activation(side[:, 1], probs_t[:, 1], ACT.Exp,
                                     scale=decay[:, 4 + n:5 + n]).then_inc(decay_exped, 1)

            def keep(dst_of, scale):
                def copy_out(i, p0, c):
                    for tt in range(TT):
                        nc.scalar.activation(dst_of(i, p0, c, tt), acc_banks[2 * c + tt][:], ACT.Copy,
                                             scale=scale).then_inc(evacuated, 1)
                return copy_out

            def silu_gate(layer):
                def copy_out(i, p0, c):
                    for tt in range(TT):
                        wait(act, gated, i * 4 + (8 * layer + 4 * (p0 - GATE_PAIR[layer]) + 2 * c + tt - 1))
                        nc.scalar.activation(side[:, tt], acc_banks[2 * c + tt][:], ACT.Silu).then_inc(evacuated, 1)
                return copy_out

            def pair(i, p0, copy_out, last=False):
                for h in range(PAIR_STEPS):
                    c, j = h // STEPS, h % STEPS
                    static = isinstance(i, int)
                    step = steps_of(p0, h) if static else None
                    if step:
                        scores_step(*step)
                    if not (last and h >= PAIR_STEPS - LEAD):
                        chunk_halves(i, 2, 2 * p0 + (h + LEAD) // STEPS, [(h + LEAD) % STEPS])
                    if step:
                        exp_step(*step)
                        values_step(*step)
                    if static and (p0, h) == DECAYS_AT:
                        log_sigmoid(0, 2 * RET_HEADS)
                    if static and (p0, h) == LAMBDA_AT:
                        act.wait_ge(lam_products, 2)
                        nc.scalar.activation(lam[:, 2:4], lam[:, 0:2], ACT.Exp).then_inc(lam_exped, 1)
                    if static and (p0, h) in DECAY_TABLE_AT:
                        decay_powers(DECAY_TABLE_AT[p0, h])
                    if static and (p0, h) == (FORGET_PAIR, FORGET_SIGMOID):
                        log_sigmoid(1, TT * FOX_HEADS)
                    if static and p0 in OUT_PAIR and 4 <= h < 8:
                        gate_row(OUT_PAIR.index(p0), h - 4)
                    if copy_out and j == STEPS - 1:
                        act.wait_ge(half_used, i * 16 + (16 * p0 + h + 1))
                        copy_out(i, p0, c)

            def turn_plain(m):
                for r in range(TURNS):
                    act.wait_ge(turned, TURNS * m + r + 1)
                    nc.scalar.copy(act_hi[:, 2 * r:2 * r + 2], banks[4 + r % TURN_BANKS][:].rearrange(
                        "p (k t) -> p k t", k=2)).then_inc(turned_hi, 1)

            def turn_scaled(m, n, shift):
                act.wait_ge(scales_ready, GROUPS + n)
                for r in range(TURNS):
                    turn_round(m, n, r, shift)

            def turn_round(m, n, r, shift):
                act.wait_ge(turned, TURNS * m + r + 1)
                for k in range(2):
                    kt = 2 * r + k
                    last = nc.scalar.activation(act_hi[:, kt], turn_bank(m, r)[:, k * SEQ:(k + 1) * SEQ],
                                                ACT.Identity, scale=scales[:, n, kt:kt + 1],
                                                bias=shift[:, kt:kt + 1])
                last.then_inc(turned_hi, 1)

            def gate_row(layer, n):
                act.wait_ge(t_ready, T[("gate", layer, n)] + 1)
                nc.scalar.copy(area[:, K, 0, n * CHUNK:(n + 1) * CHUNK], t_bank[:]).then_inc(t_free, 1)

            def norm_rows(layer):
                gain, shift = row_places(layer)
                if layer == 1:
                    act.wait_ge(turned, TURNS * 4)
                else:
                    act.wait_ge(weighed, OUT0[layer] + OUTS[layer])
                act.dma_start(gain, row_of(a["final_gain"] if layer == 0 else a["ln_g_2"][layer - 1])
                              ).then_inc(rows_landed, 16)
                if layer:
                    act.dma_start(shift, row_of(a["ln_b_2"][layer - 1])).then_inc(rows_landed, 16)

            def scores_step(layer, s):
                u0 = UNIT0[layer]
                if s < UNITS[layer]:
                    u = s
                    act.wait_ge(t_ready, T[("qk", layer, u)] + 1)
                    wait(act, scored, u0 + u - 1 if u >= 2 else u0)
                    nc.scalar.copy(qk_t[:, u % 2], t_bank[:]).then_inc(t_free, 1)

            def exp_step(layer, s):
                units, u0, o0 = UNITS[layer], UNIT0[layer], OUT0[layer]
                if 0 <= s - 1 < units and not is_ret(layer, s - 1):
                    u = s - 1
                    p = prob_slot(layer, u)
                    act.wait_ge(maxed, 2 * (u0 + u + 1))
                    if layer == 1:
                        wait(act, mixed, (u - 2) // 2 if u >= 4 else 0)
                    elif u >= 4:
                        act.wait_ge(finished, o0 + u - 3)
                    for tt, (c0, c1) in enumerate(blocks(layer)):
                        nc.scalar.activation(p[:, c0:c1], p[:, c0:c1], ACT.Exp, scale=-1.0,
                                             bias=neg_max[:, u % 4, tt:tt + 1],
                                             accum_out=den[:, u % 4, tt:tt + 1]).then_inc(exped, 1)
                    if layer == 0 and u + 2 < DIL_HEADS:
                        act.dma_start(bias[:, u % 2], a["t_dil"][u + 2]).then_inc(bias_landed[u % 2], 16)
                    if layer == 1 and u % 2 and u // 2 + 2 < DIFF_HEADS:
                        act.dma_start(bias[:, u // 2 % 2, 0:384], a["t_diff"][u // 2 + 2]
                                      ).then_inc(bias_landed[u // 2 % 2], 16)

            def values_step(layer, s):
                if has_probs(layer, s - 2):
                    u = s - 2
                    h, o0 = out_of(layer, u), OUT0[layer]
                    w = 512 if layer == 0 else 384
                    act.wait_ge(t_ready, T[("probs", layer, u)] + 1)
                    wait(act, weighed, o0 + h - 1 if h >= 2 else o0)
                    nc.scalar.copy(probs_t[:, h % 2, 0:w], t_bank[:, 0:w]).then_inc(t_free, 1)
                u = s - 3
                if 0 <= u < UNITS[layer] and is_normed(layer, u):
                    act.wait_ge(weighed, OUT0[layer] + out_of(layer, u) + 1)
                    for tt in range(TT):
                        nc.scalar.activation(squares[:, tt],
                                             o_bank[:, tt * WIDE:(tt + 1) * WIDE], ACT.Square,
                                             accum_out=square_sums[:, tt:tt + 1]).then_inc(squared, 1)

            def first_bias(layer):
                act.wait_ge(maxed, 2 * (UNIT0[layer - 1] + UNITS[layer - 1]))
                if layer == 1:
                    for i in range(2):
                        act.dma_start(bias[:, i, 0:384], a["t_diff"][i]).then_inc(bias_landed[i], 16)
                else:
                    act.dma_start(bias[:, 0, 0:384], a["t_causal"]).then_inc(bias_landed[0], 16)

            def log_sigmoid(n, cols):
                act.wait_ge(sigmoid_to_act, 2 * n + 1)
                nc.scalar.activation(ls[:, 2, 0:cols], ls[:, 1, 0:cols], ACT.Exp).then_inc(sigmoid_to_dve, 1)
                act.wait_ge(sigmoid_to_act, 2 * n + 2)
                nc.scalar.activation(ls[:, 4, 0:cols], ls[:, 3, 0:cols], ACT.Ln).then_inc(sigmoid_to_dve, 1)

            act.wait_ge(t_free, T[("vec",)] + 1)
            nc.scalar.activation(c_act[:], vecs[:, 0:2 * KT], ACT.Silu).then_inc(silu_ready, 1)
            act.wait_ge(root_ready, 1)
            act.wait_ge(x_landed, 16)
            for tt in range(TT):
                nc.scalar.activation(area[:, Q, tt], resid[:, tt], ACT.Copy, scale=rstd[:, tt:tt + 1]
                                     ).then_inc(xhat_ready, 1)
            def keep_at(which, first, scale=1.0, col=0):
                return keep(lambda i, p0, c, tt: area[:, which, tt, bass.ds(
                    i * (2 * CHUNK) + (col + (2 * (p0 - first) + c) * CHUNK), CHUNK)], scale)

            ret_qk = area[:, Q, :, 1024:2048].rearrange("p t (h c e) -> p t c h e", c=2, e=HEAD)

            def keep_ret(i, p0, c):
                for tt in range(TT):
                    nc.scalar.activation(ret_qk[:, tt, c], acc_banks[2 * c + tt][:].rearrange(
                        "p (h e) -> p h e", e=HEAD), ACT.Copy, scale=QK_SCALE if c else 1.0).then_inc(evacuated, 1)

            def two_pairs(p0, copy_out):
                with act.Fori(0, 2) as i:
                    pair(i, p0, copy_out)

            for q in range(GROUPS):
                for n in range(4 * q, 4 * q + 4):
                    split_high(n, n, 16 * (n // SLOTS + 1))
                act.wait_ge(scales_ready, q + 1)
                for r in (2 * q, 2 * q + 1):
                    turn_round(0, 0, r, mod[:, ADA_SHIFT])
            chunk_halves(0, 1, 2, [0])
            act.wait_ge(half_used, PAIR_STEPS - 2)
            keep_at(Q, 0, QK_SCALE)(0, 0, 0)
            chunk_halves(0, 1, 2, range(1, LEAD))
            act.wait_ge(half_used, PAIR_STEPS)
            keep_at(Q, 0, QK_SCALE)(0, 0, 1)
            pair(0, 1, keep_at(K, 1))
            pair(0, 2, keep_at(V, 2))
            pair(0, 3, keep_ret)
            pair(0, 4, keep_at(V, 4, col=1024))
            pair(0, 5, silu_gate(0))
            pair(0, 6, silu_gate(0))
            norm_rows(0)
            first_bias(1)
            turn_plain(1)
            pair(0, 7, None)
            pair(0, 8, None)
            turn_scaled(2, 1, mod[:, A_SHIFT])
            two_pairs(9, keep_at(Q, 9, QK_SCALE))
            two_pairs(11, keep_at(K, 11))
            pair(0, 13, keep_at(V, 13))
            pair(0, 14, keep_at(V, 13))
            pair(0, 15, silu_gate(1))
            pair(0, 16, silu_gate(1))
            first_bias(2)
            turn_plain(3)
            norm_rows(1)
            pair(0, 17, None)
            pair(0, 18, None)
            turn_scaled(4, 2, kv_shift[:])
            two_pairs(19, keep_at(K, 19))
            pair(0, 21, keep_at(V, 21))
            pair(0, 22, keep_at(V, 21))
            turn_scaled(5, 3, mod[:, B_SHIFT])
            pair(0, 23, keep_at(Q, 23, QK_SCALE))
            pair(0, 24, keep_at(Q, 23, QK_SCALE))
            pair(0, 25, silu_gate(2))
            pair(0, 26, silu_gate(2))
            norm_rows(2)
            turn_plain(6)
            pair(0, 27, None)
            pair(0, 28, None, last=True)

        @block.vector
        def _(dve):
            chain = [0]

            def link(ins):
                chain[0] += 1
                ins.then_inc(dve_chain, 1)
                dve.wait_ge(dve_chain, chain[0])

            def chunk_halves(i, scale, chunk, js):
                for j in js:
                    dve.wait_ge(hi_ready, i * (STEPS * scale) + (STEPS * chunk + j + 1))
                    nc.vector.tensor_tensor(w_lo[:, j % LEAD], raw[:, j % SLOTS],
                                            w_hi[:, j % LEAD].bitcast(F32), ALU.subtract).then_inc(lo_ready, 1)

            def split_low(n, j):
                dve.wait_ge(hi_ready, n + 1)
                nc.vector.tensor_tensor(w_lo[:, j % LEAD], raw[:, j % SLOTS], w_hi[:, j % LEAD].bitcast(F32),
                                        ALU.subtract).then_inc(lo_ready, 1)

            def start_slot(q, i):
                g = GROUP_SLOTS * q + i
                slot, landed, count = gemv_slot(g)
                dve.wait_ge(landed, count)
                for n in range(2):
                    w, k = slot[:, n * 2 * CHUNK:(n + 1) * 2 * CHUNK], 2 * i + n
                    if k == 0:
                        link(nc.vector.tensor_scalar(group_acc(q), w, c_act[:, k:k + 1], None, ALU.mult))
                        continue
                    if n == 0:
                        dve.wait_ge(gemv_used, g)
                    step = nc.vector.scalar_tensor_tensor(out=group_acc(q), in0=w, scalar=c_act[:, k:k + 1],
                                                          in1=group_acc(q), op0=ALU.mult, op1=ALU.add)
                    if n == 0:
                        link(step)
                    else:
                        step.then_inc(gemv_used, 1)

            def start_turn(q):
                kts = slice(GROUP_KT * q, GROUP_KT * (q + 1))
                dve.wait_ge(t_ready, T[("start", q)] + 1)
                nc.vector.tensor_tensor(
                    mod[:, ADA_SHIFT:ADA_SCALE + 1, kts],
                    t_bank[:, 0:2 * GROUP_KT].rearrange("p (b k) -> p b k", b=2),
                    vecs[:, VEC_BIAS:VEC_BIAS + 2 * KT].rearrange("p (b k) -> p b k", b=2)[:, :, kts],
                    ALU.add).then_inc(t_free, 1)
                dve.wait_ge(t_free, T[("start", q)] + 1)
                nc.vector.scalar_tensor_tensor(out=scales[:, 0, kts], in0=mod[:, ADA_SCALE, kts], scalar=1.0,
                                               in1=vecs[:, VEC_GAIN:VEC_GAIN + KT][:, kts], op0=ALU.add,
                                               op1=ALU.mult).then_inc(scales_ready, 1)
                dve.wait_ge(scales_ready, q + 1)
                for r in (2 * q, 2 * q + 1):
                    turn_round(0, 0, r, mod[:, ADA_SHIFT])

            def gemv_step(b, k):
                g = KT * b + k
                w, landed, count = gemv_slot(g)
                cc = c_act[:, (0 if b <= ADA_GATE else KT) + k:(0 if b <= ADA_GATE else KT) + k + 1]
                dve.wait_ge(landed, count)
                if k == 0:
                    nc.vector.tensor_scalar(acc[:], w, cc, None, ALU.mult).then_inc(gemv_used, 1)
                else:
                    dve.wait_ge(gemv_used, g)
                    nc.vector.scalar_tensor_tensor(out=acc[:], in0=w, scalar=cc, in1=acc[:],
                                                   op0=ALU.mult, op1=ALU.add).then_inc(gemv_used, 1)

            def finish_mod(b):
                dve.wait_ge(t_ready, T[("mod", b)] + 1)
                nc.vector.tensor_tensor(mod[:, b], t_bank[:, 0:KT], vecs[:, VEC_BIAS + KT * b:VEC_BIAS + KT * (b + 1)],
                                        ALU.add).then_inc(t_free, 1)

            def gate_y(layer):
                heads = ((4, 8, 10, 12), (2, 4, 6, 8), (4, 8, 12, 16))[layer]

                def take(i, p0, c):
                    p1 = p0 - GATE_PAIR[layer]
                    dve.wait_ge(finished, OUT0[layer] + heads[2 * p1 + c])
                    for tt in range(TT):
                        y = area[:, Q, tt, bass.ds(i * (2 * CHUNK) + (2 * p1 + c) * CHUNK, CHUNK)]
                        dve.wait_ge(evacuated, i * 4 + (4 * p0 + 2 * c + tt + 1))
                        nc.vector.tensor_tensor(y, y, side[:, tt], ALU.mult).then_inc(gated, 1)
                return take

            def add_out(layer):
                first = OUT_PAIR[layer]
                alpha = 1.0 if layer == 0 else DN_ALPHA

                def take(i, p0, c):
                    col = i * (2 * CHUNK) + (2 * (p0 - first) + c) * CHUNK
                    dve.wait_ge(half_used, i * 16 + (16 * p0 + STEPS * (c + 1)))
                    dve.wait_ge(t_free, T[("gate", layer, 2 * (p0 - first) + c)] + 1)
                    for tt in range(TT):
                        nc.vector.tensor_tensor(side[:, tt], acc_banks[2 * c + tt][:], area[:, K, 0, bass.ds(col, CHUNK)],
                                                ALU.mult).then_inc(evacuated, 1)
                    for tt in range(TT):
                        x = resid[:, tt, bass.ds(col, CHUNK)]
                        dve.wait_ge(evacuated, i * 4 + (4 * p0 + 2 * c + tt + 1))
                        nc.vector.scalar_tensor_tensor(out=x, in0=x, scalar=alpha, in1=side[:, tt], op0=ALU.mult,
                                                       op1=ALU.add).then_inc(summed, 1)
                    for tt in range(TT):
                        dve.wait_ge(summed, i * 4 + (8 * layer + 4 * (p0 - first) + 2 * c + tt + 1))
                        nc.vector.bn_stats(stats[:, tt, 2 * (p0 - first) + c],
                                           resid[:, tt, bass.ds(col, CHUNK)]).then_inc(measured, 1)
                return take

            def pair(p, take=None, last=False):
                gemv = gemv_steps(p)
                for h in range(PAIR_STEPS):
                    if h == finish_half(p):
                        finish_mod(SUM_AFTER[p - 1])
                    step = steps_of(p, h)
                    if step:
                        scores_step(*step)
                    if not (last and h >= PAIR_STEPS - LEAD):
                        chunk_halves(0, 2, 2 * p + (h + LEAD) // STEPS, [(h + LEAD) % STEPS])
                    for at, b, k in gemv:
                        if h <= at < h + 1:
                            gemv_step(b, k)
                    if step:
                        values_step(*step)
                    if (p, h) == DECAYS_AT:
                        log_decays()
                    if (p, h) == LAMBDA_AT:
                        make_lambda()
                    if (p, h) in DECAY_TABLE_AT:
                        make_decay_table(DECAY_TABLE_AT[p, h])
                    if (p, h) == (FORGET_PAIR, FORGET_COPY):
                        dve.wait_ge(t_ready, T[("forget_rows",)] + 1)
                        for n, used in enumerate((forget_copied, t_free)):
                            cols = slice(n * P, (n + 1) * P)
                            nc.vector.tensor_copy(side[0:FOX_HEADS, 0, cols], t_bank[0:FOX_HEADS, cols]
                                                  ).then_inc(used, 1)
                    if (p, h) == (FORGET_PAIR, FORGET_SIGMOID):
                        forget_gates()
                    if (p, h) in NORM_ROW_AT:
                        norm_row(*NORM_ROW_AT[p, h])
                    if take and h % STEPS == STEPS - 1:
                        take(0, p, h // STEPS)

            def turn_scaled(m, n, shift, scale):
                gain = {0: VEC_GAIN, 1: VEC_FINAL, 2: VEC_LN_G}.get(n)
                dve.wait_ge(t_free, T[("mod", scale)] + 1)
                if n == 2:
                    b = vecs[:, VEC_LN_B:VEC_LN_B + KT]
                    link(nc.vector.scalar_tensor_tensor(out=kv_shift[:], in0=mod[:, scale], scalar=1.0, in1=b,
                                                        op0=ALU.add, op1=ALU.mult))
                    link(nc.vector.tensor_tensor(kv_shift[:], kv_shift[:], shift, ALU.add))
                    shift = kv_shift[:]
                if gain is None:
                    nc.vector.tensor_scalar(scales[:, n], mod[:, scale], 1.0, None, ALU.add).then_inc(scales_ready, 1)
                else:
                    nc.vector.scalar_tensor_tensor(out=scales[:, n], in0=mod[:, scale], scalar=1.0,
                                                   in1=vecs[:, gain:gain + KT], op0=ALU.add, op1=ALU.mult
                                                   ).then_inc(scales_ready, 1)
                dve.wait_ge(scales_ready, GROUPS + n)
                for r in range(TURNS):
                    turn_round(m, n, r, shift)

            def turn_round(m, n, r, shift):
                dve.wait_ge(turned_hi, TURNS * m + r + 1)
                for k in range(2):
                    kt = 2 * r + k
                    nc.vector.tensor_scalar(side[:, r % 2, k * SEQ:(k + 1) * SEQ],
                                            turn_bank(m, r)[:, k * SEQ:(k + 1) * SEQ],
                                            scales[:, n, kt:kt + 1], shift[:, kt:kt + 1], ALU.mult, ALU.add
                                            ).then_inc(shifted, 1)
                dve.wait_ge(shifted, 2 * (TURNS * n + r + 1))
                nc.vector.tensor_tensor(act_lo[:, 2 * r:2 * r + 2], side[:, r % 2].rearrange("p (k t) -> p k t", k=2),
                                        act_hi[:, 2 * r:2 * r + 2].bitcast(F32), ALU.subtract).then_inc(turned_lo, 1)

            def turn_plain(m):
                for r in range(TURNS):
                    dve.wait_ge(turned_hi, TURNS * m + r + 1)
                    nc.vector.tensor_tensor(act_lo[:, 2 * r:2 * r + 2],
                                            banks[4 + r % TURN_BANKS][:].rearrange("p (k t) -> p k t", k=2),
                                            act_hi[:, 2 * r:2 * r + 2].bitcast(F32), ALU.subtract).then_inc(turned_lo, 1)

            def root_mean_square(key, eps):
                link(nc.vector.tensor_tensor(mean_sq[:], moments[:, :, 0], moments[:, :, 0], ALU.mult))
                nc.vector.scalar_tensor_tensor(out=mean_sq[:], in0=mean_sq[:], scalar=eps, in1=moments[:, :, 1],
                                               op0=ALU.add, op1=ALU.add).then_inc(var_ready, 1)

            def measure(layer):
                dve.wait_ge(measured, 4 * TT * (layer + 1))
                nc.vector.bn_aggr(moments[:, 0], stats[:, 0])
                link(nc.vector.bn_aggr(moments[:, 1], stats[:, 1]))
                if layer == 0:
                    root_mean_square(("norm", layer), NORM_EPS)
                else:
                    nc.vector.tensor_scalar(mean_sq[:], moments[:, :, 1], EPS, None, ALU.add).then_inc(var_ready, 1)

            def norm(layer):
                measure(layer)
                dve.wait_ge(root_ready, ROOTS[("norm", layer)] + 1)
                for tt in range(TT):
                    x, r = resid[:, tt], rstd[:, tt:tt + 1]
                    if layer == 0:
                        nc.vector.tensor_scalar(x, x, r, None, ALU.mult).then_inc(normed, 1)
                    else:
                        nc.vector.tensor_scalar(x, x, moments[:, tt, 0:1], r, ALU.subtract, ALU.mult
                                                ).then_inc(normed, 1)

            def norm_row(layer, tt):
                gain, shift = row_places(layer)
                x = resid[:, tt]
                dve.wait_ge(rows_landed, 16 * (1, 3, 5)[layer])
                dve.wait_ge(normed, TT * layer + tt + 1)
                if layer == 0:
                    nc.vector.tensor_tensor(x, x, gain, ALU.mult).then_inc(resid_ready, 1)
                else:
                    link(nc.vector.tensor_tensor(x, x, gain, ALU.mult))
                    nc.vector.tensor_tensor(x, x, shift, ALU.add).then_inc(resid_ready, 1)

            def last_norm():
                gain, shift = row_places(2)
                half_row = [slice(n * D // 2, (n + 1) * D // 2) for n in range(2)]
                measure(2)
                dve.wait_ge(rows_landed, 16 * 5)
                for tt in range(TT):
                    for n, cols in enumerate(half_row):
                        nc.vector.scalar_tensor_tensor(out=resid[:, tt, cols], in0=resid[:, tt, cols],
                                                       scalar=moments[:, tt, 0:1], in1=gain[:, cols],
                                                       op0=ALU.subtract, op1=ALU.mult).then_inc(normed, 1)
                    if tt == 0:
                        dve.wait_ge(root_ready, ROOTS[("norm", 2)] + 1)
                    for n, cols in enumerate(half_row):
                        dve.wait_ge(normed, 2 * TT + 2 * tt + n + 1)
                        nc.vector.scalar_tensor_tensor(out=resid[:, tt, cols], in0=resid[:, tt, cols],
                                                       scalar=rstd[:, tt:tt + 1], in1=shift[:, cols],
                                                       op0=ALU.mult, op1=ALU.add).then_inc(resid_ready, 1)

            def finish_normed(layer, u):
                c, w = head_cols(layer, u)
                dve.wait_ge(root_ready, ROOTS[("head", layer, u)] + 1)
                for tt in range(TT):
                    o, y, r = o_bank[:, tt * w:(tt + 1) * w], area[:, Q, tt, c:c + w], rstd[:, tt:tt + 1]
                    if layer == 1:
                        last = nc.vector.scalar_tensor_tensor(out=y, in0=o, scalar=r, in1=subln[:], op0=ALU.mult,
                                                              op1=ALU.mult)
                    else:
                        last = nc.vector.tensor_scalar(y, o, r, None, ALU.mult)
                last.then_inc(finished, 1)

            def mix(layer, u):
                if 0 <= u < UNITS[layer] and not is_ret(layer, u):
                    dve.wait_ge(exped, 2 * (SOFT0[layer] + u + 1))
                    if layer != 1:
                        link(nc.vector.reciprocal(rden[:, u % 4], den[:, u % 4]))
                    elif u % 2:
                        p0, p1 = prob_slot(layer, u - 1), prob_slot(layer, u)
                        link(nc.vector.reciprocal(rden[:, u % 4 - 1:u % 4 + 1], den[:, u % 4 - 1:u % 4 + 1]))
                        nc.vector.tensor_scalar(p0[:, 0:P], p0[:, 0:P], rden[:, u % 4 - 1, 0:1], None, ALU.mult)
                        nc.vector.tensor_scalar(p0[:, P:384], p0[:, P:384], rden[:, u % 4 - 1, 1:2], None, ALU.mult)
                        link(nc.vector.tensor_scalar(rden[:, u % 4], rden[:, u % 4], lam[:, 4:5], None, ALU.mult))
                        for tt, (c0, c1) in enumerate(blocks(layer)):
                            last = nc.vector.scalar_tensor_tensor(
                                out=p0[:, c0:c1], in0=p1[:, c0:c1], scalar=rden[:, u % 4, tt:tt + 1],
                                in1=p0[:, c0:c1], op0=ALU.mult, op1=ALU.add)
                        last.then_inc(mixed, 1)

            def values_step(layer, s):
                finish_values(layer, s - 3)
                mix(layer, s - 1)

            def finish_values(layer, u):
                if not 0 <= u < UNITS[layer] or out_of(layer, u) is None or is_normed(layer, u):
                    return
                c, w = head_cols(layer, u)
                dve.wait_ge(weighed, OUT0[layer] + out_of(layer, u) + 1)
                for tt in range(TT):
                    last = nc.vector.tensor_scalar(area[:, Q, tt, c:c + w], o_bank[:, tt * w:(tt + 1) * w],
                                                   rden[:, u % 4, tt:tt + 1], None, ALU.mult)
                last.then_inc(finished, 1)

            def scores_step(layer, s):
                units, u0 = UNITS[layer], UNIT0[layer]
                if 0 <= s - 4 < units and is_normed(layer, s - 4):
                    finish_normed(layer, s - 4)
                if 0 <= s - 1 < units:
                    u = s - 1
                    dve.wait_ge(scored, u0 + u + 1)
                    s_bank, p = s_banks[u % 2], prob_slot(layer, u)
                    if layer == 0 and u >= 3:
                        if is_ret(layer, u - 3):
                            dve.wait_ge(weighed, OUT0[layer] + u - 2)
                        else:
                            dve.wait_ge(t_ready, T[("probs", layer, u - 3)] + 1)
                    if layer == 1 and u >= 4:
                        dve.wait_ge(t_ready, T[("probs", layer, (u - 4) | 1)] + 1)
                    if layer == 2 and u >= 4:
                        dve.wait_ge(t_ready, T[("probs", layer, u - 4)] + 1)
                    if is_ret(layer, u):
                        nc.vector.tensor_tensor(p, s_bank[:], decay_table(u - DIL_HEADS), ALU.mult).then_inc(maxed, 2)
                    else:
                        if layer == 0:
                            if u >= 2:
                                dve.wait_ge(bias_landed[u % 2], 16 * (u // 2))
                            b = bias[:, u % 2]
                        elif layer == 1:
                            h = u // 2
                            dve.wait_ge(bias_landed[h % 2], 16 * (DIL_HEADS // 2 - 1 + h // 2 + 1))
                            b = bias[:, h % 2]
                        else:
                            dve.wait_ge(bias_landed[0], 16 * (DIL_HEADS // 2 - 1 + DIFF_HEADS // 2 + 1))
                            b = bias[:, 0]
                        for tt, (c0, c1) in enumerate(blocks(layer)):
                            nc.vector.tensor_tensor_reduce(
                                out=p[:, c0:c1], in0=s_bank[:, c0:c1], in1=b[:, c0:c1], scale=-1.0, scalar=FLT_MAX,
                                op0=ALU.add, op1=ALU.min, accum_out=neg_max[:, u % 4, tt:tt + 1]).then_inc(maxed, 1)

            def log_sigmoid(n, cols, dst):
                z, nz, e, w, l, d, one = (ls[:, k, 0:cols] for k in range(7))
                nc.vector.scalar_tensor_tensor(out=nz, in0=z, scalar=-1.0, in1=z, op0=ALU.mult,
                                               op1=ALU.min).then_inc(sigmoid_to_act, 1)
                dve.wait_ge(sigmoid_to_dve, 2 * n + 1)
                nc.vector.tensor_scalar(w, e, 1.0, None, ALU.add).then_inc(sigmoid_to_act, 1)
                dve.wait_ge(sigmoid_to_act, 2 * n + 2)
                link(nc.vector.tensor_scalar(d, w, -1.0, None, ALU.add))
                link(nc.vector.tensor_scalar(one, d, 0.0, None, ALU.is_equal))
                link(nc.vector.tensor_tensor(d, d, one, ALU.add))
                link(nc.vector.reciprocal(d, d))
                link(nc.vector.tensor_tensor(d, d, e, ALU.mult))
                dve.wait_ge(sigmoid_to_dve, 2 * n + 2)
                link(nc.vector.tensor_tensor(l, l, one, ALU.add))
                link(nc.vector.tensor_tensor(d, d, l, ALU.mult))
                return nc.vector.scalar_tensor_tensor(out=dst, in0=z, scalar=0.0, in1=d, op0=ALU.min, op1=ALU.subtract)

            def forget_gates():
                dve.wait_ge(t_ready, T[("forget",)] + 1)
                for tt in range(TT):
                    last = nc.vector.tensor_tensor(ls[:, 0, tt * FOX_HEADS:(tt + 1) * FOX_HEADS],
                                                   t_bank[:, tt * FOX_HEADS:(tt + 1) * FOX_HEADS], b_forget[:],
                                                   ALU.add)
                last.then_inc(t_free, 1)
                dve.wait_ge(t_free, T[("forget",)] + 1)
                log_sigmoid(1, TT * FOX_HEADS, forget[:]).then_inc(forget_ready, 1)

            def log_decays():
                dve.wait_ge(smalls_landed, 16 * 14)
                link(nc.vector.tensor_copy(ls[:, 0, 0:2 * RET_HEADS], decay[:]))
                link(log_sigmoid(0, 2 * RET_HEADS, decay[:]))
                nc.vector.tensor_scalar(decay[:], decay[:], -1e-20, None, ALU.min).then_inc(decay_ready, 1)

            def make_lambda():
                for n in range(2):
                    nc.vector.tensor_tensor_reduce(
                        out=ls[:].rearrange("p a b -> p (a b)")[:, 0:HEAD], in0=probs[:, n * HEAD:(n + 1) * HEAD],
                        in1=probs[:, (2 + n) * HEAD:(3 + n) * HEAD], scale=1.0, scalar=0.0, op0=ALU.mult,
                        op1=ALU.add, accum_out=lam[:, n:n + 1]).then_inc(lam_products, 1)
                    dve.wait_ge(lam_products, n + 1)
                dve.wait_ge(lam_exped, 1)
                link(nc.vector.scalar_tensor_tensor(out=lam[:, 4:5], in0=lam[:, 3:4], scalar=LAM_INIT,
                                                    in1=lam[:, 2:3], op0=ALU.subtract, op1=ALU.subtract))
                link(nc.vector.tensor_scalar(subln[:], subln[:], 1.0 - LAM_INIT, None, ALU.mult))

            def make_decay_table(h):
                dve.wait_ge(decay_exped, h + 1)
                nc.vector.tensor_tensor(decay_table(h), side[:, 0], side[:, 1], ALU.add).then_inc(decay_used, 1)

            nc.vector.memset(ones[:], 1.0).then_inc(consts_ready, 1)
            dve.wait_ge(t_ready, T[("vec",)] + 1)
            nc.vector.tensor_copy(vecs[:], t_bank[:, 0:VECS]).then_inc(t_free, 1)
            dve.wait_ge(silu_ready, 1)
            for q in range(GROUPS):
                for i in range(GROUP_SLOTS):
                    start_slot(q, i)
                    if q == 0 and i == 1:
                        dve.wait_ge(x_landed, 16)
                        for tt in range(TT):
                            for n in range(D // CHUNK):
                                link(nc.vector.bn_stats(stats[:, tt, n], resid[:, tt, n * CHUNK:(n + 1) * CHUNK]))
                            link(nc.vector.bn_aggr(moments[:, tt], stats[:, tt]))
                        root_mean_square(("x",), NORM_EPS)
                    if q and i == 1:
                        start_turn(q - 1)
                    if i >= 4:
                        split_low(4 * q + i - 4, i - 4)
            start_turn(GROUPS - 1)
            for n in range(LEAD):
                split_low(PAIR_STEPS + n, n)
            dve.wait_ge(smalls_landed, 16 * 14)
            nc.vector.tensor_copy(wf_hi[:], w_forget[:]).then_inc(forget_split, 1)
            dve.wait_ge(forget_split, 1)
            nc.vector.tensor_tensor(wf_lo[:], w_forget[:], wf_hi[:].bitcast(F32), ALU.subtract
                                    ).then_inc(forget_split, 1)
            for p in range(1, 5):
                pair(p)
            pair(5, gate_y(0))
            pair(6, gate_y(0))
            turn_plain(1)
            pair(7, add_out(0))
            pair(8, add_out(0))
            finish_mod(A_SCALE)
            norm(0)
            turn_scaled(2, 1, mod[:, A_SHIFT], A_SCALE)
            for p in range(9, 15):
                pair(p)
            pair(15, gate_y(1))
            pair(16, gate_y(1))
            finish_mod(KV_SCALE)
            turn_plain(3)
            pair(17, add_out(1))
            pair(18, add_out(1))
            norm(1)
            turn_scaled(4, 2, mod[:, KV_SHIFT], KV_SCALE)
            for p in range(19, 23):
                pair(p)
            finish_mod(B_SCALE)
            turn_scaled(5, 3, mod[:, B_SHIFT], B_SCALE)
            pair(23)
            pair(24)
            pair(25, gate_y(2))
            pair(26, gate_y(2))
            finish_mod(B_GATE)
            turn_plain(6)
            pair(27, add_out(2))
            pair(28, add_out(2), last=True)
            last_norm()


INPUTS = ["x", "c", "norm_gain", "w_ada", "b_ada", "w_in", "w_out", "ret_decay_logit_f", "ret_decay_logit_b",
          "final_gain", "c_2", "w_mod_2", "b_mod_2", "ln_g_2", "ln_b_2", "a_w_in_2", "a_w_out_2", "a_lam_q1_2",
          "a_lam_k1_2", "a_lam_q2_2", "a_lam_k2_2", "a_subln_g_2", "kv_w_mod_2", "kv_b_mod_2", "kv_w_2", "kv_b_f_2",
          "b_w_in_2", "b_w_out_2"]


def kernel(**inputs):
    import concourse.bacc as bacc
    from concourse.bass_utils import run_bass_kernel_spmd as run

    nc = bacc.Bacc("TRN2", target_bir_lowering=False, num_devices=1)
    arrays = {name: np.ascontiguousarray(inputs[name]) for name in INPUTS}
    arrays.update(shape_tables())
    aps = {name: nc.dram_tensor(f"in_{name}", v.shape, mybir.dt.from_np(v.dtype), kind="ExternalInput").ap()
           for name, v in arrays.items()}
    out = nc.dram_tensor("out_0", (1, SEQ, D), F32, kind="ExternalOutput").ap()
    two_blocks(nc, aps, out)
    r = run(nc, [{f"in_{k}": v for k, v in arrays.items()}], core_ids=[0])
    return r.results[0]["out_0"]
```
